# Optimizing a Trainium2 kernel written in Bass

```python
import jax, jax.numpy as jnp
from jax import lax
import numpy as np
import math

D_MODEL = 1024
BATCH = 1
SEQ = 256
DEPTH = 2

HEAD_DIM = 64
N_MIXERS = 2
MOBA_HEADS = 16
MOBA_BLOCK = 256
MOBA_TOPK = 3
MOBA_Q_CHUNK = 32
DIL_GROUPS = ((128, 1), (512, 4), (2048, 16))
DIL_HEADS_PER_GROUP = 4
DIL_HEADS = DIL_HEADS_PER_GROUP * len(DIL_GROUPS)
DIL_BLOCK = 128
D_FF = 4 * D_MODEL
ROPE_THETA = 10000.0
LN_EPS = 1e-5
DEEPNORM_ALPHA = (2.0 * DEPTH) ** 0.25
DEEPNORM_BETA = (8.0 * DEPTH) ** -0.25
N_LAYERS_A = (DEPTH + N_MIXERS - 1) // N_MIXERS
N_LAYERS_B = DEPTH // N_MIXERS


def layer_norm(x, g, b):
    xf = x.astype(jnp.float32)
    mu = jnp.mean(xf, axis=-1, keepdims=True)
    var = jnp.mean(jnp.square(xf - mu), axis=-1, keepdims=True)
    y = (xf - mu) * lax.rsqrt(var + LN_EPS)
    return (y * g.astype(jnp.float32) + b.astype(jnp.float32)).astype(x.dtype)

def rotary_tables(seq, dtype):
    inv = 1.0 / (ROPE_THETA ** (jnp.arange(0, HEAD_DIM, 2, dtype=jnp.float32) / HEAD_DIM))
    ang = jnp.arange(seq, dtype=jnp.float32)[:, None] * inv[None, :]
    return jnp.cos(ang).astype(dtype), jnp.sin(ang).astype(dtype)

def apply_rotary(t, cos, sin):
    t1, t2 = jnp.split(t, 2, axis=-1)
    c = cos[None, :, None, :]
    s = sin[None, :, None, :]
    return jnp.concatenate([t1 * c - t2 * s, t2 * c + t1 * s], axis=-1)

def moba_attention(x, w_qkv, w_o, cos, sin):
    B, S, _ = x.shape
    H, dh, BLK, QC = MOBA_HEADS, HEAD_DIM, MOBA_BLOCK, MOBA_Q_CHUNK
    qkv = (x @ w_qkv).reshape(B, S, 3, H, dh)
    q = apply_rotary(qkv[:, :, 0], cos, sin) * (dh ** -0.5)
    k = apply_rotary(qkv[:, :, 1], cos, sin)
    v = qkv[:, :, 2]
    pad = (-S) % BLK
    Sp = S + pad
    nb = Sp // BLK
    padw = ((0, 0), (0, pad), (0, 0), (0, 0))
    q = jnp.pad(q, padw).transpose(0, 2, 1, 3)
    k = jnp.pad(k, padw).transpose(0, 2, 1, 3)
    v = jnp.pad(v, padw).transpose(0, 2, 1, 3)
    k_blk = k.reshape(B, H, nb, BLK, dh)
    v_blk = v.reshape(B, H, nb, BLK, dh)
    k_mean = jnp.mean(k_blk.astype(jnp.float32), axis=3).astype(k.dtype)

    gate = jnp.einsum('bhsd,bhnd->bhsn', q, k_mean).astype(jnp.float32)
    q_block = jnp.arange(Sp) // BLK
    past = jnp.arange(nb)[None, :] < q_block[:, None]
    gate = jnp.where(past[None, None], gate, -jnp.inf)
    kk = min(MOBA_TOPK, nb)
    sel_score, sel_idx = lax.top_k(gate, kk)
    sel_valid = jnp.isfinite(sel_score)

    nc = Sp // QC
    q_c = q.reshape(B, H, nc, QC, dh).transpose(2, 0, 1, 3, 4)
    idx_c = sel_idx.reshape(B, H, nc, QC, kk).transpose(2, 0, 1, 3, 4)
    val_c = sel_valid.reshape(B, H, nc, QC, kk).transpose(2, 0, 1, 3, 4)
    b_ix = jnp.arange(B)[:, None, None, None]
    h_ix = jnp.arange(H)[None, :, None, None]
    key_off = jnp.arange(BLK)

    def one_chunk(args):
        c, qc, idx, valid = args
        kg = k_blk[b_ix, h_ix, idx]
        vg = v_blk[b_ix, h_ix, idx]
        s_past = jnp.einsum('bhqd,bhqnkd->bhqnk', qc, kg).astype(jnp.float32)
        s_past = jnp.where(valid[..., None], s_past, -jnp.inf).reshape(B, H, QC, kk * BLK)
        start = c * QC
        blk = start // BLK
        k_own = lax.dynamic_index_in_dim(k_blk, blk, axis=2, keepdims=False)
        v_own = lax.dynamic_index_in_dim(v_blk, blk, axis=2, keepdims=False)
        s_own = jnp.einsum('bhqd,bhkd->bhqk', qc, k_own).astype(jnp.float32)
        q_off = start % BLK + jnp.arange(QC)
        causal = key_off[None, :] <= q_off[:, None]
        s_own = jnp.where(causal[None, None], s_own, -jnp.inf)
        p = jax.nn.softmax(jnp.concatenate([s_past, s_own], axis=-1), axis=-1).astype(v.dtype)
        p_past = p[..., :kk * BLK].reshape(B, H, QC, kk, BLK)
        p_own = p[..., kk * BLK:]
        return (jnp.einsum('bhqnk,bhqnkd->bhqd', p_past, vg)
                + jnp.einsum('bhqk,bhkd->bhqd', p_own, v_own))

    out = lax.map(one_chunk, (jnp.arange(nc, dtype=jnp.int32), q_c, idx_c, val_c))
    out = out.transpose(1, 0, 3, 2, 4).reshape(B, Sp, H * dh)[:, :S]
    return out @ w_o

def dilated_group(q, k, v, window, dilation):
    B, S, Hg, dh = q.shape
    span = window // dilation
    WB = DIL_BLOCK
    assert span <= WB
    L = S // dilation
    Lp = -(-L // WB) * WB
    nblk = Lp // WB

    def to_blocks(t):
        t = t.reshape(B, L, dilation, Hg, dh).transpose(0, 2, 1, 3, 4)
        t = jnp.pad(t, ((0, 0), (0, 0), (0, Lp - L), (0, 0), (0, 0)))
        return t.reshape(B, dilation, nblk, WB, Hg, dh)

    def with_prev(t):
        prev = jnp.pad(t, ((0, 0), (0, 0), (1, 0), (0, 0), (0, 0), (0, 0)))[:, :, :-1]
        return jnp.concatenate([prev, t], axis=3)

    qb = to_blocks(q)
    kw = with_prev(to_blocks(k))
    vw = with_prev(to_blocks(v))
    s = jnp.einsum('brnqhd,brnkhd->brnhqk', qb, kw).astype(jnp.float32)
    qi = jnp.arange(nblk)[:, None, None] * WB + jnp.arange(WB)[None, :, None]
    ki = jnp.arange(nblk)[:, None, None] * WB - WB + jnp.arange(2 * WB)[None, None, :]
    dist = qi - ki
    mask = (dist >= 0) & (dist <= span) & (ki >= 0)
    s = jnp.where(mask[None, None, :, None], s, -jnp.inf)
    lse = jax.nn.logsumexp(s, axis=-1)
    p = jnp.exp(s - lse[..., None]).astype(v.dtype)
    o = jnp.einsum('brnhqk,brnkhd->brnqhd', p, vw)
    o = o.reshape(B, dilation, Lp, Hg, dh)[:, :, :L].transpose(0, 2, 1, 3, 4).reshape(B, S, Hg, dh)
    lse = lse.transpose(0, 1, 2, 4, 3).reshape(B, dilation, Lp, Hg)[:, :, :L]
    lse = lse.transpose(0, 2, 1, 3).reshape(B, S, Hg)
    return o, lse

def dilated_attention(x, w_qkv, w_o, cos, sin):
    B, S, _ = x.shape
    G, Hg, dh = len(DIL_GROUPS), DIL_HEADS_PER_GROUP, HEAD_DIM
    qkv = (x @ w_qkv).reshape(B, S, 3, DIL_HEADS, dh)
    q = apply_rotary(qkv[:, :, 0], cos, sin) * (dh ** -0.5)
    k = apply_rotary(qkv[:, :, 1], cos, sin)
    v = qkv[:, :, 2]
    outs, lses = [], []
    for g, (window, dilation) in enumerate(DIL_GROUPS):
        hs = slice(g * Hg, (g + 1) * Hg)
        o_g, lse_g = dilated_group(q[:, :, hs], k[:, :, hs], v[:, :, hs], window, dilation)
        outs.append(o_g)
        lses.append(lse_g)
    alpha = jax.nn.softmax(jnp.stack(lses, axis=0), axis=0).astype(x.dtype)
    o = jnp.stack(outs, axis=0) * alpha[..., None]
    o = o.transpose(1, 2, 0, 3, 4).reshape(B, S, G * Hg * dh)
    return o @ w_o

def sq_relu_mlp(x, w_in, w_out):
    return jnp.square(jax.nn.relu(x @ w_in)) @ w_out

def first_inputs(seed: int = 0) -> dict:
    key = jax.random.key(seed)
    ks = jax.random.split(key, 12)
    f32 = jnp.float32
    moba_w = MOBA_HEADS * HEAD_DIM
    dil_w = DIL_HEADS * HEAD_DIM
    x = jax.random.normal(ks[0], (BATCH, SEQ, D_MODEL), f32)
    moba_w_qkv = jax.random.normal(ks[1], (N_LAYERS_A, D_MODEL, 3 * moba_w), f32) * D_MODEL ** -0.5
    moba_w_o = jax.random.normal(ks[2], (N_LAYERS_A, moba_w, D_MODEL), f32) * (moba_w ** -0.5 * DEEPNORM_BETA)
    dil_w_qkv = jax.random.normal(ks[3], (N_LAYERS_B, D_MODEL, 3 * dil_w), f32) * D_MODEL ** -0.5
    dil_w_o = jax.random.normal(ks[4], (N_LAYERS_B, dil_w, D_MODEL), f32) * (dil_w ** -0.5 * DEEPNORM_BETA)
    mlp_w_in = jax.random.normal(ks[5], (DEPTH, D_MODEL, D_FF), f32) * D_MODEL ** -0.5
    mlp_w_out = jax.random.normal(ks[6], (DEPTH, D_FF, D_MODEL), f32) * (D_FF ** -0.5 * DEEPNORM_BETA)
    ln_mix_g = 1.0 + 0.02 * jax.random.normal(ks[7], (DEPTH, D_MODEL), f32)
    ln_mix_b = 0.02 * jax.random.normal(ks[8], (DEPTH, D_MODEL), f32)
    ln_mlp_g = 1.0 + 0.02 * jax.random.normal(ks[9], (DEPTH, D_MODEL), f32)
    ln_mlp_b = 0.02 * jax.random.normal(ks[10], (DEPTH, D_MODEL), f32)
    return {"x": x, "moba_w_qkv": moba_w_qkv, "moba_w_o": moba_w_o,
            "dil_w_qkv": dil_w_qkv, "dil_w_o": dil_w_o,
            "mlp_w_in": mlp_w_in, "mlp_w_out": mlp_w_out,
            "ln_mix_g": ln_mix_g, "ln_mix_b": ln_mix_b,
            "ln_mlp_g": ln_mlp_g, "ln_mlp_b": ln_mlp_b}

def first_block(x, moba_w_qkv, moba_w_o, dil_w_qkv, dil_w_o, mlp_w_in, mlp_w_out,
              ln_mix_g, ln_mix_b, ln_mlp_g, ln_mlp_b):
    S = x.shape[1]
    cos, sin = rotary_tables(S, x.dtype)
    h = x
    for i in range(DEPTH):
        j = i // N_MIXERS
        if i % N_MIXERS == 0:
            mix = moba_attention(h, moba_w_qkv[j], moba_w_o[j], cos, sin)
        else:
            mix = dilated_attention(h, dil_w_qkv[j], dil_w_o[j], cos, sin)
        h = layer_norm(DEEPNORM_ALPHA * h + mix, ln_mix_g[i], ln_mix_b[i])
        h = layer_norm(DEEPNORM_ALPHA * h + sq_relu_mlp(h, mlp_w_in[i], mlp_w_out[i]),
                       ln_mlp_g[i], ln_mlp_b[i])
    return h


CONV_DIM = D_MODEL
CONV_KERNEL = 31
RET_QK_DIM = 256
RET_V_DIM = 512
RET_HEADS = D_MODEL // RET_QK_DIM
RET_QK_WIDTH = RET_HEADS * RET_QK_DIM
RET_V_WIDTH = RET_HEADS * RET_V_DIM
RET_CHUNK = 128
ROPE_BASE = 10000.0
N_BRANCHES = 2
IN_SIZES = (CONV_DIM, CONV_DIM, RET_QK_WIDTH, RET_QK_WIDTH, RET_V_WIDTH, RET_V_WIDTH, D_MODEL, D_MODEL)
IN_WIDTH = sum(IN_SIZES)
IN_SPLITS = tuple(int(s) for s in np.cumsum(IN_SIZES)[:-1])
D_FF_2 = 2816
N_EXPERTS = 8
TOP_K = 2
N_DENSE = (DEPTH + 1) // 2
N_MOE = DEPTH // 2
DEEPNORM_ALPHA_2 = (2 * DEPTH) ** 0.25
DEEPNORM_BETA_2 = (8 * DEPTH) ** -0.25
N_ADA = 6


def layer_norm_2(x, g, b):
    xf = x.astype(jnp.float32)
    mu = jnp.mean(xf, axis=-1, keepdims=True)
    var = jnp.mean(jnp.square(xf - mu), axis=-1, keepdims=True)
    y = (xf - mu) * lax.rsqrt(var + LN_EPS)
    return (y * g.astype(jnp.float32) + b.astype(jnp.float32)).astype(x.dtype)

def head_norm(x):
    mu = jnp.mean(x, axis=-1, keepdims=True)
    var = jnp.mean(jnp.square(x - mu), axis=-1, keepdims=True)
    return (x - mu) * lax.rsqrt(var + LN_EPS)

def rotary(x, positions):
    half = x.shape[-1] // 2
    inv_freq = ROPE_BASE ** (-jnp.arange(half, dtype=jnp.float32) / half)
    ang = positions.astype(jnp.float32)[:, :, None] * inv_freq
    cos = jnp.cos(ang)[:, :, None, :]
    sin = jnp.sin(ang)[:, :, None, :]
    xf = x.astype(jnp.float32)
    x1, x2 = xf[..., :half], xf[..., half:]
    return jnp.concatenate([x1 * cos - x2 * sin, x2 * cos + x1 * sin], axis=-1)

def chunkwise_retention(q, k, v):
    b, t, h, dk = q.shape
    dv = v.shape[-1]
    n_chunks = t // RET_CHUNK
    log_g = jnp.log1p(-jnp.exp2(-5.0 - jnp.arange(h, dtype=jnp.float32)))
    j = jnp.arange(RET_CHUNK, dtype=jnp.float32)
    diff = j[:, None] - j[None, :]
    intra = jnp.where(diff >= 0, jnp.exp(log_g[:, None, None] * jnp.maximum(diff, 0.0)), 0.0)
    q_decay = jnp.exp(log_g[:, None] * (j + 1.0))[None, :, :, None]
    k_decay = jnp.exp(log_g[:, None] * (RET_CHUNK - 1.0 - j))[None, :, :, None]
    chunk_decay = jnp.exp(log_g * RET_CHUNK)[None, :, None, None]

    def to_chunks(a):
        return a.reshape(b, n_chunks, RET_CHUNK, h, a.shape[-1]).transpose(1, 0, 3, 2, 4)

    qc, kc, vc = to_chunks(q), to_chunks(k * (dk ** -0.5)), to_chunks(v)

    def step(state, inp):
        qi, ki, vi = inp
        scores = jnp.einsum('bhid,bhjd->bhij', qi, ki) * intra
        inner = jnp.einsum('bhij,bhjv->bhiv', scores, vi)
        cross = jnp.einsum('bhid,bhdv->bhiv', qi * q_decay, state)
        new_state = state * chunk_decay + jnp.einsum('bhjd,bhjv->bhdv', ki * k_decay, vi)
        return new_state, inner + cross

    state0 = jnp.zeros((b, h, dk, dv), jnp.float32)
    _, out = lax.scan(step, state0, (qc, kc, vc))
    return out.transpose(1, 0, 3, 2, 4).reshape(b, t, h, dv)

def causal_depthwise_conv(u, w, bias):
    y = lax.conv_general_dilated(
        u, w[:, None, :].astype(u.dtype), window_strides=(1,), padding=[(CONV_KERNEL - 1, 0)],
        dimension_numbers=('NWC', 'WIO', 'NWC'), feature_group_count=u.shape[-1])
    return y + bias

def token_mixer(h, positions, w_in, w_dw, b_dw, ln_conv_g, ln_conv_b, w_conv_o, w_ret_o, w_out):
    b, t, _ = h.shape
    proj = h @ w_in
    conv_a, conv_b, q, k, v, ret_gate, gate_conv, gate_ret = jnp.split(proj, IN_SPLITS, axis=-1)
    u = conv_a * jax.nn.sigmoid(conv_b)
    u = causal_depthwise_conv(u, w_dw, b_dw)
    u = jax.nn.silu(layer_norm_2(u, ln_conv_g, ln_conv_b))
    y_conv = u @ w_conv_o
    q = rotary(q.reshape(b, t, RET_HEADS, RET_QK_DIM), positions)
    k = rotary(k.reshape(b, t, RET_HEADS, RET_QK_DIM), positions)
    v = v.reshape(b, t, RET_HEADS, RET_V_DIM).astype(jnp.float32)
    o = head_norm(chunkwise_retention(q, k, v)).reshape(b, t, RET_V_WIDTH).astype(h.dtype)
    y_ret = (jax.nn.silu(ret_gate) * o) @ w_ret_o
    merged = jax.nn.sigmoid(gate_conv) * y_conv + jax.nn.sigmoid(gate_ret) * y_ret
    return merged @ w_out

def swiglu(h, w_gate, w_up, w_down):
    return (jax.nn.silu(h @ w_gate) * (h @ w_up)) @ w_down

def moe_swiglu(h, w_router, w_gate, w_up, w_down):
    b, t, d = h.shape
    tokens = h.reshape(b * t, d)
    logits = (tokens @ w_router).astype(jnp.float32)
    top_vals, top_idx = lax.top_k(logits, TOP_K)
    top_w = jax.nn.softmax(top_vals, axis=-1)
    combine = jnp.sum(jax.nn.one_hot(top_idx, N_EXPERTS, dtype=jnp.float32) * top_w[..., None], axis=1)
    combine = combine.astype(tokens.dtype)
    out = jnp.zeros_like(tokens)
    for e in range(N_EXPERTS):
        out = out + combine[:, e:e + 1] * swiglu(tokens, w_gate[e], w_up[e], w_down[e])
    return out.reshape(b, t, d)

def second_inputs(seed: int = 0) -> dict:
    key = jax.random.key(seed)
    ks = jax.random.split(key, 32)
    f32 = jnp.float32
    D = D_MODEL

    def nrm(k, shape, scale):
        return jax.random.normal(k, shape, f32) * scale

    x = jax.random.normal(ks[0], (BATCH, SEQ, D), f32)
    c = jax.random.normal(ks[1], (BATCH, D), f32)
    positions = (jnp.arange(SEQ, dtype=jnp.int32)[None, :]
                 + jax.random.randint(ks[2], (BATCH, 1), 0, 1024, dtype=jnp.int32))
    return {
        "x": x,
        "c": c,
        "positions": positions,
        "w_ada": nrm(ks[3], (DEPTH, D, N_ADA * D), D ** -0.5),
        "b_ada": nrm(ks[4], (DEPTH, N_ADA * D), 0.02),
        "w_in": nrm(ks[5], (DEPTH, D, IN_WIDTH), D ** -0.5),
        "w_dw": nrm(ks[6], (DEPTH, CONV_KERNEL, CONV_DIM), CONV_KERNEL ** -0.5),
        "b_dw": nrm(ks[7], (DEPTH, CONV_DIM), 0.02),
        "ln_conv_g": 1.0 + nrm(ks[8], (DEPTH, CONV_DIM), 0.02),
        "ln_conv_b": nrm(ks[9], (DEPTH, CONV_DIM), 0.02),
        "w_conv_o": nrm(ks[10], (DEPTH, CONV_DIM, D), CONV_DIM ** -0.5),
        "w_ret_o": nrm(ks[11], (DEPTH, RET_V_WIDTH, D), RET_V_WIDTH ** -0.5),
        "w_out": nrm(ks[12], (DEPTH, D, D), DEEPNORM_BETA_2 * D ** -0.5),
        "ln1_g": 1.0 + nrm(ks[13], (DEPTH, D), 0.02),
        "ln1_b": nrm(ks[14], (DEPTH, D), 0.02),
        "ffn_w_gate": nrm(ks[15], (N_DENSE, D, D_FF_2), D ** -0.5),
        "ffn_w_up": nrm(ks[16], (N_DENSE, D, D_FF_2), D ** -0.5),
        "ffn_w_down": nrm(ks[17], (N_DENSE, D_FF_2, D), DEEPNORM_BETA_2 * D_FF_2 ** -0.5),
        "moe_w_router": nrm(ks[18], (N_MOE, D, N_EXPERTS), D ** -0.5),
        "moe_w_gate": nrm(ks[19], (N_MOE, N_EXPERTS, D, D_FF_2), D ** -0.5),
        "moe_w_up": nrm(ks[20], (N_MOE, N_EXPERTS, D, D_FF_2), D ** -0.5),
        "moe_w_down": nrm(ks[21], (N_MOE, N_EXPERTS, D_FF_2, D), DEEPNORM_BETA_2 * D_FF_2 ** -0.5),
        "ln2_g": 1.0 + nrm(ks[22], (DEPTH, D), 0.02),
        "ln2_b": nrm(ks[23], (DEPTH, D), 0.02),
    }

def second_block(x, c, positions, w_ada, b_ada, w_in, w_dw, b_dw, ln_conv_g, ln_conv_b,
              w_conv_o, w_ret_o, w_out, ln1_g, ln1_b, ffn_w_gate, ffn_w_up, ffn_w_down,
              moe_w_router, moe_w_gate, moe_w_up, moe_w_down, ln2_g, ln2_b):
    c_act = jax.nn.silu(c)
    for l in range(DEPTH):
        ada = c_act @ w_ada[l] + b_ada[l]
        shift1, scale1, gate1, shift2, scale2, gate2 = [a[:, None, :] for a in jnp.split(ada, N_ADA, axis=-1)]
        h = x * (1.0 + scale1) + shift1
        mix = token_mixer(h, positions, w_in[l], w_dw[l], b_dw[l], ln_conv_g[l], ln_conv_b[l],
                          w_conv_o[l], w_ret_o[l], w_out[l])
        x = layer_norm_2(DEEPNORM_ALPHA_2 * x + gate1 * mix, ln1_g[l], ln1_b[l])
        h = x * (1.0 + scale2) + shift2
        if l % 2 == 0:
            i = l // 2
            ff = swiglu(h, ffn_w_gate[i], ffn_w_up[i], ffn_w_down[i])
        else:
            i = l // 2
            ff = moe_swiglu(h, moe_w_router[i], moe_w_gate[i], moe_w_up[i], moe_w_down[i])
        x = layer_norm_2(DEEPNORM_ALPHA_2 * x + gate2 * ff, ln2_g[l], ln2_b[l])
    return x


def setup_inputs(seed=0):
    out = dict(first_inputs(seed))
    for name, value in second_inputs(seed + 1).items():
        if name != "x":
            out[name + "_2"] = value
    return out


def reference(
    x, moba_w_qkv, moba_w_o, dil_w_qkv, dil_w_o, mlp_w_in, mlp_w_out, ln_mix_g, ln_mix_b,
    ln_mlp_g, ln_mlp_b, c_2, positions_2, w_ada_2, b_ada_2, w_in_2, w_dw_2, b_dw_2, ln_conv_g_2,
    ln_conv_b_2, w_conv_o_2, w_ret_o_2, w_out_2, ln1_g_2, ln1_b_2, ffn_w_gate_2, ffn_w_up_2,
    ffn_w_down_2, moe_w_router_2, moe_w_gate_2, moe_w_up_2, moe_w_down_2, ln2_g_2, ln2_b_2,
):
    x = first_block(
        x, moba_w_qkv, moba_w_o, dil_w_qkv, dil_w_o, mlp_w_in, mlp_w_out, ln_mix_g, ln_mix_b,
        ln_mlp_g, ln_mlp_b,
    )
    return second_block(
        x, c_2, positions_2, w_ada_2, b_ada_2, w_in_2, w_dw_2, b_dw_2, ln_conv_g_2, ln_conv_b_2,
        w_conv_o_2, w_ret_o_2, w_out_2, ln1_g_2, ln1_b_2, ffn_w_gate_2, ffn_w_up_2,
        ffn_w_down_2, moe_w_router_2, moe_w_gate_2, moe_w_up_2, moe_w_down_2, ln2_g_2, ln2_b_2,
    )


_drawn_inputs = setup_inputs


def setup_inputs(seed=0):
    import zlib

    import numpy as np

    out = dict(_drawn_inputs(seed))
    spreads = {}
    factors = {'b_dw_2': 8.0, 'ln_conv_g_2': 22.118, 'ln_conv_b_2': 23.815}
    for name, (base, spread) in spreads.items():
        noise = np.random.default_rng([zlib.crc32(name.encode()), seed]).standard_normal(out[name].shape)
        drawn = base * np.exp(spread * noise) if base else spread * noise
        out[name] = __import__('jax').numpy.asarray(drawn.astype(out[name].dtype))
    for name, factor in factors.items():
        out[name] = (out[name] * factor).astype(out[name].dtype)
    return out
```

```python
from contextlib import ExitStack

import numpy as np

import concourse.bass as bass
from concourse import mybir

P = 128
S = 256
D = 1024
KT = D // P
TT = S // P
UNIT = 2048
RAWS = 4
HEAD = 64
HALF_HIDDEN = 2048
FF = 2816
FT = FF // P
EXPERTS = 8
RET_HEADS = 4
RET_DK = 256
RET_DV = 512
TAPS = 31
ALPHA = float(4.0 ** 0.25)
EPS = 1e-5
NEG = -1e30
QSCALE = HEAD ** -0.5
TRI = 384

F32 = mybir.dt.float32
F32R = mybir.dt.float32r
I32 = mybir.dt.int32
U32 = mybir.dt.uint32
ALU = mybir.AluOpType
ACT = mybir.ActivationFunctionType
AX = mybir.AxisListType

PCOL = {}
_n = 0
for _name, _w in ([(f"lnA{i}{c}", KT) for i in range(4) for c in "gb"]
                  + [(f"ln{k}_{l}{c}", KT) for l in range(2) for k in ("c", "1", "2") for c in "gb"]
                  + [(f"bdw_{l}", KT) for l in range(2)] + [(f"bada_{l}", 48) for l in range(2)]
                  + [("c", KT), ("invf", 1), ("iota8", 8), ("eps", 1), ("wr", 8 * EXPERTS)]
                  + [(f"wdw_{l}", KT * TAPS) for l in range(2)]):
    PCOL[_name] = _n
    _n += _w
NPAR = _n

ORDER = [("ada0", 24, "ada"), ("ada1", 24, "ada"),
         ("aqk", 8, "T"), ("av", 4, "N"), ("ao", 4, "T"),
         ("ain0", 8, "relu"), ("aout0", 8, "R"), ("ain1", 8, "relu"), ("aout1", 8, "R"),
         ("bqk", 6, "T"), ("bv", 3, "N"), ("bo", 3, "R"),
         ("bin0", 8, "relu"), ("bout0", 8, "R"), ("bin1", 8, "relu"), ("bout1", 8, "R")]
for _l in range(2):
    ORDER += [(f"pb{_l}", 4, "T"), (f"pa{_l}", 4, "T"), (f"pqk{_l}", 8, "T"), (f"pv{_l}", 8, "N"),
              (f"prg{_l}", 8, "T"), (f"pgc{_l}", 4, "T"), (f"pgr{_l}", 4, "T"),
              (f"co{_l}", 4, "T"), (f"ro{_l}", 8, "R"), (f"wo{_l}", 4, "T"),
              (f"gu{_l}", 22, "T"), (f"dn{_l}", 11, "R")]


class Phase:
    pass


def slot_uses(n):
    return [len(range(s, n, RAWS)) for s in range(RAWS)]


def plan():
    phases = {}
    g, uses, da, dd = 0, [0] * RAWS, 4, 4
    prev_n = None
    eu = [a + b for a, b in zip(slot_uses(22), slot_uses(11))]
    for name, n, kind in ORDER:
        p = Phase()
        p.name, p.n, p.kind, p.g0, p.uses0 = name, n, kind, g, list(uses)
        p.moe = name in ("gu1", "dn1")
        p.g_e, p.uses_e = (33, eu) if p.moe else (0, [0] * RAWS)
        p.raw_back = None if prev_n is None else [
            min(prev_n - i for i in range(prev_n) if i % RAWS == s) if prev_n > s else RAWS for s in range(RAWS)]
        p.pair_back = None if prev_n is None else [
            min([prev_n - i for i in range(prev_n) if i % 2 == s]) for s in range(2)]
        if name == "gu1":
            p.raw_back, p.pair_back = [1] * RAWS, [1, 1]
        if prev_n == 3:
            p.raw_back = [3, 2, 1, 1]
        p.da0, p.dd0 = da, dd
        ga = {"gu": n // 2, "pb": n, "pq": n, "pv": n, "pr": n, "pg": n}.get(name[:2], 0)
        ga = n if name in ("aqk", "av", "bqk", "bv") else ga
        p.act_drains = ga
        p.dve_drains = {"R": 8, "relu": 0}.get(kind, n - ga)
        p.da_e, p.dd_e = (11, 19) if p.moe else (0, 0)
        da, dd = da + p.act_drains, dd + p.dve_drains
        g += n
        uses = [a + b for a, b in zip(uses, slot_uses(n))]
        prev_n = n
        phases[name] = p
    names = [n for n, _, _ in ORDER]
    for a, b in zip(names, names[1:]):
        phases[a].next = phases[b]
    phases["dn1"].next = phases["gu1"]
    return phases, g


PH, STREAM = plan()
TOTAL = PH["gu1"].g0 + 33 * EXPERTS
LOOKAHEAD = 2


def lin(const, *terms):
    for reg, k in terms:
        if k and not (isinstance(reg, int) and reg == 0):
            const = reg * k + const
    return const


def build(nc, wstream, xT, par, posb, consts, blockA, decay, outT):
    with ExitStack() as ctx:
        def sb(name, shape, dt=F32):
            return ctx.enter_context(nc.sbuf_tensor(name, shape, dt))

        def sem(name):
            return ctx.enter_context(nc.semaphore(name))

        raw = sb("raw", [P, RAWS, UNIT])
        wh = sb("wh", [P, 2, UNIT], F32R)
        wl = sb("wl", [P, 2, UNIT], F32R)
        x = sb("x", [P, KT, S])
        xh = sb("xh", [P, KT, S], F32R)
        xl = sb("xl", [P, KT, S], F32R)
        cs = sb("cs", [P, 3, P])
        pr = sb("pr", [P, NPAR])
        cosr = sb("cosr", [P, S])
        sinr = sb("sinr", [P, S])
        std = sb("std", [P, S])
        rstd = sb("rstd", [P, S])
        ada = sb("ada", [P, 2, 48])
        ch = sb("ch", [P, KT, 2], F32R)
        cl = sb("cl", [P, KT, 2], F32R)
        cf = sb("cf", [P, KT, 2])
        st = sb("st", [P, 128])
        ix = sb("ix", [P, 16], U32)
        pos = sb("pos", [P, S], I32)
        work = sb("work", [P, 14592])
        with ExitStack() as hidden:
            mh = hidden.enter_context(nc.sbuf_tensor("mh", [P, FT, S], F32R))
            ml = hidden.enter_context(nc.sbuf_tensor("ml", [P, FT, S], F32R))
        ret = sb("ret", [P, 11264])

        def view(buf, off, width, pat, **kw):
            return buf[:, off:off + width].rearrange(pat, **kw)

        ident, ones, swap = cs[:, 0, :], cs[:, 1, :], cs[:, 2, :]
        RG = view(work, 0, 4096, "p (j t) -> p j t", t=S)
        GC = view(work, 4096, 2048, "p (j t) -> p j t", t=S)
        GR = view(work, 6144, 2048, "p (j t) -> p j t", t=S)
        PADW = TAPS - 1 + S
        U = view(work, 8192, KT * PADW, "p (j t) -> p j t", t=PADW)
        CV = view(work, 10480, 2048, "p (j t) -> p j t", t=S)
        SRC = view(work, 12528, 2048, "p (j t) -> p j t", t=S)
        ON = view(work, 8192, 4096, "p (h n d) -> p h n d", h=RET_HEADS, n=TT)
        RQ = view(ret, 0, 2048, "p (j t) -> p j t", t=S)
        RK = view(ret, 2048, 2048, "p (j t) -> p j t", t=S)
        RV = view(ret, 4096, 4096, "p (t c) -> p t c", t=TT)
        DEC = view(ret, 8192, RET_HEADS * TRI, "p (h c) -> p h c", h=RET_HEADS)
        RST = view(ret, 8192 + 1536, 2 * TRI, "p (h c) -> p h c", h=2)
        QK = view(work, 0, 4096, "p (j t) -> p j t", t=S)
        VN = view(work, 4096, 2048, "p (t c) -> p t c", t=TT)
        RC = view(work, 6144, 1024, "p (b c) -> p b c", b=2)
        SS = view(work, 7168, 3 * TRI, "p (g c) -> p g c", g=3)
        PT = view(work, 8320, 3 * TRI, "p (g c) -> p g c", g=3)
        MASK = view(work, 9472, 4 * TRI, "p (g c) -> p g c", g=4)
        COSA = work[:, 11008:11264]
        SINA = work[:, 11264:11520]
        RT = work[:, 11520:12032]
        SG = work[:, 0:512]
        HF = work[:, 512:1024]
        TMP = view(work, 1024, 512, "p (b c) -> p b c", b=2)
        LG = view(work, 1536, 16, "p (t e) -> p t e", t=TT)
        CMB = view(work, 1552, 16, "p (t e) -> p t e", t=TT)
        CMB2 = view(work, 1568, 16, "p (t e) -> p t e", t=TT)
        ACC = view(work, 4096, 2048, "p (j t) -> p j t", t=S)
        CB = view(work, 6144, 2048, "p (e t) -> p e t", t=S)
        BC = view(work, 8192, 2048, "p (c m) -> p c m", m=P)

        ps = ctx.enter_context(nc.psum_tensor("ps", [P, 8, 512], F32))

        def col(name, j=0, w=1):
            return pr[:, PCOL[name] + j:PCOL[name] + j + w]

        landed = [sem(f"raw_landed{s}") for s in range(RAWS)]
        hi_split = sem("hi_split")
        lo_split = sem("lo_split")
        consumed = sem("consumed")
        drained_act = sem("drained_act")
        drained_dve = sem("drained_dve")
        consts_in = sem("consts_in")
        x_in = sem("x_in")
        par_in = sem("par_in")
        pos_in = sem("pos_in")
        blocka_in = sem("blocka_in")
        decay_in = sem("decay_in")
        out_done = sem("out_done")
        src_ready = sem("src_ready")
        xh_ready = sem("xh_ready")
        moving = sem("moving")
        nonlin = sem("nonlin")
        hf_ready = sem("hf_ready")
        mh_ready = sem("mh_ready")
        hidden_ready = sem("hidden_ready")
        ln_mean = sem("ln_mean")
        ln_cen = sem("ln_cen")
        ln_sq = sem("ln_sq")
        ln_var = sem("ln_var")
        ln_std = sem("ln_std")
        swapped = sem("swapped")
        cos_done = sem("cos_done")
        roped = sem("roped")
        qk_done = sem("qk_done")
        masked = sem("masked")
        mx_ready = sem("mx_ready")
        exp_done = sem("exp_done")
        p_ready = sem("p_ready")
        pt_done = sem("pt_done")
        pt_copied = sem("pt_copied")
        pv_done = sem("pv_done")
        ao_copied = sem("ao_copied")
        vstep = sem("vstep")
        pstep = sem("pstep")
        tap_done = sem("tap_done")
        trig_arg = sem("trig_arg")
        trig_done = sem("trig_done")
        ret_roped = sem("ret_roped")
        st_done = sem("st_done")
        st_decayed = sem("st_decayed")
        o_done = sem("o_done")
        o_copied = sem("o_copied")
        ovar = sem("ovar")
        ostd = sem("ostd")
        o_normed = sem("o_normed")
        g_turned = sem("g_turned")
        logits = sem("logits")
        gap_ready = sem("gap_ready")
        gap_exp = sem("gap_exp")
        comb_ready = sem("comb_ready")
        comb_spread = sem("comb_spread")
        cb_ready = sem("cb_ready")
        down_scaled = sem("down_scaled")
        ln_in = sem("ln_in")
        final = sem("final")
        u_ready = sem("u_ready")
        c_act = sem("c_act")

        block = ctx.enter_context(nc.Block())

        def run_units(eng, ph, emit, ahead=LOOKAHEAD):
            nb = max((ph.n - ahead) // RAWS, 0)
            if nb > 1:
                with eng.Fori(0, nb) as b:
                    for s in range(RAWS):
                        emit(b, s)
            else:
                nb = 0
            for i in range(nb * RAWS, ph.n):
                emit(i // RAWS, i % RAWS)

        def ahead_of(ph, b, s, e):
            s2 = s + LOOKAHEAD
            if isinstance(b, int) and RAWS * b + s2 >= ph.n:
                i = RAWS * b + s2 - ph.n
                return ph.next, i // RAWS, i % RAWS, (e + 1 if ph.name == "dn1" else e)
            return ph, b + s2 // RAWS, s2 % RAWS, e

        def unit_no(ph, b, s, e, k=1, add=0):
            return lin(k * (ph.g0 + s) + add, (b, k * RAWS), (e, k * ph.g_e))

        @block.sync
        def _(sp):
            sp.dma_start(cs[:], consts).then_inc(consts_in, 16)
            sp.dma_start(pr[:], par).then_inc(par_in, 16)

            def stream(ph, e=0):
                def load(b, s, peeled):
                    if peeled and ph.raw_back is not None:
                        sp.wait_ge(lo_split, lin(2 * (ph.g0 - ph.raw_back[s] + 1), (e, 2 * ph.g_e)))
                    elif not peeled:
                        sp.wait_ge(lo_split, unit_no(ph, b, s, e, 2, -2 * RAWS + 2))
                    sp.dma_start(raw[:, s, :], wstream[unit_no(ph, b, s, e)]).then_inc(landed[s], 16)
                for s in range(min(RAWS, ph.n)):
                    load(0, s, True)
                nb = ph.n // RAWS
                if nb > 1:
                    with sp.Fori(1, nb) as b:
                        for s in range(RAWS):
                            load(b, s, False)
                for i in range(max(nb, 1) * RAWS, ph.n):
                    load(i // RAWS, i % RAWS, False)

            for name, _, _ in ORDER:
                ph = PH[name]
                if name == "dn1":
                    continue
                if name == "gu1":
                    with sp.Fori(0, EXPERTS) as e:
                        stream(PH["gu1"], e)
                        stream(PH["dn1"], e)
                    for i in range(LOOKAHEAD):
                        sp.wait_ge(lo_split, 2 * TOTAL)
                        sp.dma_start(raw[:, i, :], wstream[TOTAL + i]).then_inc(landed[i], 16)
                    continue
                stream(ph)
                if name == "ada0":
                    sp.dma_start(x[:], xT).then_inc(x_in, 16)
                    sp.dma_start(pos[:], posb).then_inc(pos_in, 16)
                    sp.dma_start(work[:, 9472:11520], blockA).then_inc(blocka_in, 16)
                if name[:2] == "pb":
                    sp.wait_ge(consumed, 2 * ph.g0)
                    sp.dma_start(ret[:, 8192:8192 + 1536], decay).then_inc(decay_in, 16)
            sp.wait_ge(final, 1)
            sp.dma_start(outT, x[:]).then_inc(out_done, 16)
            sp.wait_ge(out_done, 16)

        @block.scalar
        def _(act):
            A = nc.scalar.activation

            def split(ph, b, s, e=0):
                r = raw[:, s, :].rearrange("p (h c) -> p h c", h=2)
                o = wh[:, s % 2, :].rearrange("p (h c) -> p h c", h=2)
                act.wait_ge(landed[s], lin(16 * (ph.uses0[s] + 1), (b, 16), (e, 16 * ph.uses_e[s])))
                for half in range(2):
                    if isinstance(b, int) and b == 0 and s < 2:
                        if ph.pair_back is not None:
                            act.wait_ge(consumed, lin(2 * (ph.g0 - ph.pair_back[s]) + half + 1, (e, 2 * ph.g_e)))
                    else:
                        act.wait_ge(consumed, unit_no(ph, b, s, e, 2, half + 1 - 4))
                    A(o[:, half], r[:, half], ACT.Copy).then_inc(hi_split, 1)

            def split_ahead(ph, b, s, e=0):
                split(*ahead_of(ph, b, s, e))

            def filled(ph, b, s, e=0):
                act.wait_ge(consumed, unit_no(ph, b, s, e, 2, 2))

            def columns(name, drain=None):
                ph = PH[name]
                if drain is not None and ph.dd0 > 4:
                    act.wait_ge(drained_dve, ph.dd0)

                def one(b, s):
                    split_ahead(ph, b, s)
                    if drain is not None:
                        filled(ph, b, s)
                        drain(lin(s, (b, RAWS)), ps[:, s, :]).then_inc(drained_act, 1)
                run_units(act, ph, one)

            copies = [0, 0, 0]

            def xh_from(src):
                copies[0] += 1
                act.wait_ge(src_ready, copies[0])
                A(xh[:], src, ACT.Copy).then_inc(xh_ready, 1)

            lns = [0]

            def layer_norm(src):
                n = lns[0]
                lns[0] += 1
                act.wait_ge(ln_cen, n + 1)
                A(SRC, src, ACT.Square).then_inc(ln_sq, 1)
                act.wait_ge(ln_var, n + 1)
                A(std[:], ps[:, 5, 0:S], ACT.Sqrt, bias=col("eps")).then_inc(ln_std, 1)

            nl = [0]

            def relu_phase(name):
                ph, n0 = PH[name], nl[0]
                nl[0] += ph.n

                def one(b, s):
                    split_ahead(ph, b, s)
                    filled(ph, b, s)
                    A(SG, ps[:, s, :], ACT.Relu).then_inc(nonlin, 1)
                    act.wait_ge(hf_ready, lin(n0 + s + 1, (b, RAWS)))
                    A(mh[:, :, :].rearrange("p (i a) t -> p i (a t)", a=2)[:, lin(s, (b, RAWS))], HF,
                      ACT.Copy).then_inc(mh_ready, 1)
                run_units(act, ph, one)

            def gate_phase(ph, n0, e=0):
                def one(b, s):
                    split_ahead(ph, b, s, e)
                    if s % 2 == 0:
                        filled(ph, b, s, e)
                        A(SG, ps[:, s, :], ACT.Silu).then_inc(drained_act, 1)
                    else:
                        act.wait_ge(hf_ready, lin(n0 + s // 2 + 1, (b, 2), (e, 11)))
                        A(mh[:, :, :].rearrange("p (i a) t -> p i (a t)", a=2)[:, lin(s // 2, (b, 2))], HF,
                          ACT.Copy).then_inc(mh_ready, 1)
                run_units(act, ph, one)

            act.sem_inc(drained_act, 4)
            act.sem_inc(drained_dve, 4)
            act.sem_inc(nonlin, 4)
            act.wait_ge(par_in, 16)
            A(cf[:], col("c", 0, KT).unsqueeze(2).broadcast_to([P, KT, 2]), ACT.Silu).then_inc(c_act, 1)
            act.wait_ge(c_act, 1)
            A(ch[:], cf[:], ACT.Copy).then_inc(c_act, 1)
            split(PH["ada0"], 0, 0)
            split(PH["ada0"], 0, 1)
            columns("ada0")
            columns("ada1")
            act.wait_ge(trig_arg, 1)
            A(cosr[:], std[:], ACT.Sin)
            A(sinr[:], rstd[:], ACT.Sin).then_inc(trig_done, 1)

            def attention(groups, heads_of, g0, h0):
                G = len(heads_of(0))
                for i in range(groups):
                    act.wait_ge(mx_ready, g0 + i + 1)
                    A(SS[:, 0:G, 0:128], SS[:, 0:G, 0:128], ACT.Exp, bias=st[:, 0:1], scale=QSCALE,
                      accum_out=st[:, 4:5])
                    A(SS[:, 0:G, 128:384], SS[:, 0:G, 128:384], ACT.Exp, bias=st[:, 1:2], scale=QSCALE,
                      accum_out=st[:, 5:6]).then_inc(exp_done, 1)
                    act.wait_ge(pt_done, g0 + i + 1)
                    A(PT[:, 0:G, :], ps[:, 3:3 + G, 0:TRI], ACT.Copy).then_inc(pt_copied, 1)
                    for k, h in enumerate(heads_of(i)):
                        n = h0 + i * G + k
                        r = slice(64 * (h % 2), 64 * (h % 2) + 64)
                        act.wait_ge(pv_done, n + 1)
                        A(SRC[r, h // 2, :], ps[r, 6 + n % 2, 0:S], ACT.Copy).then_inc(ao_copied, 1)

            def pairs_out(dst):
                v = dst.rearrange("p (i a) t -> p i (a t)", a=2)
                return lambda i, bank: A(v[:, i], bank, ACT.Copy)

            def tokens_out(dst):
                v = dst.rearrange("p t (i c) -> p i t c", c=256)
                return lambda i, bank: A(v[:, i], bank.rearrange("p (t c) -> p t c", t=2), ACT.Copy)

            def pairs_act(dst, func):
                v = dst.rearrange("p (i a) t -> p i (a t)", a=2)
                return lambda i, bank: A(v[:, i], bank, func)

            xh_from(x[:])
            columns("aqk", pairs_out(QK[:, 0:16, :]))
            columns("av", tokens_out(VN))
            attention(16, lambda i: [i], 0, 0)
            act.wait_ge(ao_copied, 16)
            A(xh[:], SRC, ACT.Copy).then_inc(xh_ready, 1)
            columns("ao")
            layer_norm(x[:])
            xh_from(x[:])
            relu_phase("ain0")
            columns("aout0")
            relu_phase("ain1")
            columns("aout1")
            layer_norm(x[:])
            xh_from(x[:])
            columns("bqk", pairs_out(QK[:, 0:12, :]))
            columns("bv", tokens_out(VN[:, :, 0:768]))
            attention(4, lambda j: [j, 4 + j, 8 + j], 16, 16)
            act.wait_ge(ao_copied, 28)
            A(xh[:, 0:6, :], SRC[:, 0:6, :], ACT.Copy).then_inc(xh_ready, 1)
            columns("bo")
            layer_norm(x[:])
            xh_from(x[:])
            relu_phase("bin0")
            columns("bout0")
            relu_phase("bin1")
            columns("bout1")
            layer_norm(x[:])

            for l in range(2):
                xh_from(SRC)
                columns(f"pb{l}", pairs_act(CV, ACT.Sigmoid))
                columns(f"pa{l}")
                columns(f"pqk{l}", pairs_out(ret[:, 0:4096].rearrange("p (j t) -> p j t", t=S)))
                columns(f"pv{l}", tokens_out(RV))
                columns(f"prg{l}", pairs_act(RG, ACT.Silu))
                columns(f"pgc{l}", pairs_act(GC, ACT.Sigmoid))
                columns(f"pgr{l}", pairs_act(GR, ACT.Sigmoid))
                act.wait_ge(ret_roped, l + 1)
                layer_norm(CV)
                act.wait_ge(u_ready, l + 1)
                for j in range(KT):
                    last = A(SRC[:, j, :], CV[:, j, :], ACT.Silu, bias=col(f"lnc_{l}b", j), scale=col(f"lnc_{l}g", j))
                last.then_inc(src_ready, 1)
                xh_from(SRC)
                for i in range(8):
                    act.wait_ge(o_done, 8 * l + i + 1)
                    A(ON[:, i // 2, i % 2, :], ps[:, 2 + i % 4, :], ACT.Copy).then_inc(o_copied, 1)
                act.wait_ge(ovar, l + 1)
                A(st[:, 80:88], st[:, 64:80].rearrange("p (i c) -> p i c", c=2)[:, :, 1], ACT.Sqrt,
                  bias=col("eps")).then_inc(ostd, 1)
                for i in range(8):
                    act.wait_ge(hf_ready, nl[0] + i + 1)
                    A(mh[:, 2 * i:2 * i + 2, :], RG[:, 2 * i:2 * i + 2, :], ACT.Copy).then_inc(mh_ready, 1)
                nl[0] += 8
                columns(f"co{l}")
                columns(f"ro{l}")
                xh_from(SRC)
                columns(f"wo{l}")
                layer_norm(x[:])
                xh_from(SRC)
                if l == 0:
                    gate_phase(PH["gu0"], nl[0])
                    nl[0] += 11
                    columns("dn0")
                    layer_norm(x[:])
                else:
                    act.wait_ge(gap_ready, 1)
                    A(st[:, 34:36], st[:, 32:34], ACT.Exp).then_inc(gap_exp, 1)
                    for i in range(4):
                        act.wait_ge(comb_spread, i + 1)
                        A(CB[:, 2 * i:2 * i + 2, :], ps[:, i, :], ACT.Copy).then_inc(cb_ready, 1)
                    with act.Fori(0, EXPERTS) as e:
                        gate_phase(PH["gu1"], nl[0], e)
                        ph = PH["dn1"]
                        run_units(act, ph, lambda b, s: split_ahead(ph, b, s, e))
                    layer_norm(x[:])

        @block.gpsimd
        def _(pool):
            steps = [0]

            def link(ins):
                steps[0] += 1
                ins.then_inc(pstep, 1)
                pool.wait_ge(pstep, steps[0])

            T2 = nc.gpsimd.tensor_tensor

            def rope_cos(ntiles, k0, act_total):
                pool.wait_ge(drained_act, act_total)
                for i in range(ntiles // 2):
                    if i >= 2:
                        pool.wait_ge(roped, k0 + i - 1)
                    T2(RC[:, i % 2, :].rearrange("p (a t) -> p a t", a=2), QK[:, 2 * i:2 * i + 2, :],
                       COSA.unsqueeze(1).broadcast_to([P, 2, S]), ALU.mult).then_inc(cos_done, 1)

            pool.wait_ge(blocka_in, 16)
            rope_cos(16, 0, PH["av"].da0)
            rope_cos(12, 8, PH["bv"].da0)
            pool.wait_ge(trig_done, 1)
            for l in range(2):
                pool.wait_ge(drained_act, PH[f"pv{l}"].da0)
                pool.wait_ge(moving, 1 + 6 + 4 * l + 1)
                cosb = cosr[:].unsqueeze(1).broadcast_to([P, 4, S])
                sinb = sinr[:].unsqueeze(1).broadcast_to([P, 4, S])
                t1, t2 = SRC[:, 0:4, :], SRC[:, 4:8, :]
                for q in (RQ, RK):
                    v = q.rearrange("p (h a) t -> p a h t", a=2)
                    x1, x2 = v[:, 0], v[:, 1]
                    T2(t1, x1, sinb, ALU.mult)
                    link(T2(t2, x2, sinb, ALU.mult))
                    T2(x1, x1, cosb, ALU.mult)
                    link(T2(x2, x2, cosb, ALU.mult))
                    T2(x1, x1, t2, ALU.subtract)
                    ins = T2(x2, x2, t1, ALU.add)
                    if q is RQ:
                        link(ins)
                    else:
                        ins.then_inc(ret_roped, 1)

        @block.vector
        def _(dve):
            V = nc.vector
            steps = [0]

            def link(ins):
                steps[0] += 1
                ins.then_inc(vstep, 1)
                dve.wait_ge(vstep, steps[0])

            def split(ph, b, s, e=0):
                r = raw[:, s, :].rearrange("p (h c) -> p h c", h=2)
                hi = wh[:, s % 2, :].rearrange("p (h c) -> p h c", h=2)
                o = wl[:, s % 2, :].rearrange("p (h c) -> p h c", h=2)
                for half in range(2):
                    dve.wait_ge(hi_split, unit_no(ph, b, s, e, 2, half + 1))
                    V.tensor_tensor(o[:, half], r[:, half], hi[:, half].bitcast(F32),
                                    ALU.subtract).then_inc(lo_split, 1)

            def split_ahead(ph, b, s, e=0):
                split(*ahead_of(ph, b, s, e))

            def filled(ph, b, s, e=0):
                dve.wait_ge(consumed, unit_no(ph, b, s, e, 2, 2))

            def columns(name, drain=None, extra=None):
                ph = PH[name]
                if drain is not None and ph.da0 > 4:
                    dve.wait_ge(drained_act, ph.da0)

                def one(b, s):
                    split_ahead(ph, b, s)
                    if drain is not None:
                        filled(ph, b, s)
                        drain(b, s, ps[:, s, :]).then_inc(drained_dve, 1)
                    if extra is not None:
                        extra(lin(s, (b, RAWS)))
                run_units(dve, ph, one)

            def rows(name, drain):
                ph = PH[name]
                run_units(dve, ph, lambda b, s: split_ahead(ph, b, s))
                dve.wait_ge(consumed, 2 * (ph.g0 + ph.n))
                for m in range(KT):
                    drain(m, ps[:, m, 0:S]).then_inc(drained_dve, 1)

            splits = [0]

            def rest_of(src, n=KT):
                splits[0] += 1
                dve.wait_ge(xh_ready, splits[0])
                V.tensor_tensor(xl[:, 0:n, :], src[:, 0:n, :], xh[:, 0:n, :].bitcast(F32),
                                ALU.subtract).then_inc(moving, 1)

            lns = [0]

            def layer_norm(src, g=None, b=None):
                n = lns[0]
                lns[0] += 1
                dve.wait_ge(ln_mean, n + 1)
                V.tensor_tensor(src, src, ps[:, 4, 0:S].unsqueeze(1).broadcast_to([P, KT, S]),
                                ALU.subtract).then_inc(ln_cen, 1)
                dve.wait_ge(ln_std, n + 1)
                link(V.reciprocal(rstd[:], std[:]))
                last = V.tensor_tensor(src, src, rstd[:].unsqueeze(1).broadcast_to([P, KT, S]), ALU.mult)
                if g is None:
                    return last
                link(last)
                for j in range(KT):
                    last = V.tensor_scalar(src[:, j, :], src[:, j, :], col(g, j), col(b, j), ALU.mult, ALU.add)
                return last

            def modulate(l, which):
                o = 24 * which
                for j in range(KT):
                    last = V.tensor_scalar(SRC[:, j, :], x[:, j, :], ada[:, l, o + 8 + j:o + 9 + j],
                                           ada[:, l, o + j:o + j + 1], ALU.mult, ALU.add)
                return last

            nl = [0, 4]

            def relu_phase(name):
                ph, n0, h0 = PH[name], nl[0], nl[1]
                nl[0] += ph.n
                nl[1] += ph.n

                def one(b, s):
                    split_ahead(ph, b, s)
                    i = lin(s, (b, RAWS))
                    dve.wait_ge(nonlin, lin(h0 + s + 1, (b, RAWS)))
                    if n0 or s or b:
                        dve.wait_ge(hidden_ready, lin(n0 + s, (b, RAWS)))
                    V.tensor_tensor(HF, SG, SG, ALU.mult).then_inc(hf_ready, 1)
                    dve.wait_ge(mh_ready, lin(n0 + s + 1, (b, RAWS)))
                    V.tensor_tensor(pair(ml, i), HF, pair(mh, i).bitcast(F32), ALU.subtract).then_inc(hidden_ready, 1)
                run_units(dve, ph, one)

            def pair(t, i):
                return t[:, :, :].rearrange("p (i a) t -> p i (a t)", a=2)[:, i]

            def gate_phase(ph, n0, e=0):
                def one(b, s):
                    split_ahead(ph, b, s, e)
                    if s % 2 == 1:
                        filled(ph, b, s, e)
                        dve.wait_ge(drained_act, lin(ph.da0 + s // 2 + 1, (b, 2), (e, ph.da_e)))
                        dve.wait_ge(hidden_ready, lin(n0 + s // 2, (b, 2), (e, 11)))
                        V.tensor_tensor(HF, SG, ps[:, s, :], ALU.mult).then_inc(hf_ready, 1)
                        dve.wait_ge(mh_ready, lin(n0 + s // 2 + 1, (b, 2), (e, 11)))
                        i = lin(s // 2, (b, 2))
                        V.tensor_tensor(pair(ml, i), HF, pair(mh, i).bitcast(F32),
                                        ALU.subtract).then_inc(hidden_ready, 1)
                        V.sem_inc(drained_dve, 1)
                run_units(dve, ph, one)

            dve.wait_ge(c_act, 2)
            V.tensor_tensor(cl[:], cf[:], ch[:].bitcast(F32), ALU.subtract).then_inc(moving, 1)
            split(PH["ada0"], 0, 0)
            split(PH["ada0"], 0, 1)
            for l in range(2):
                ph = PH[f"ada{l}"]
                av = ada[:, l, :].rearrange("p (i c) -> p i c", c=2)
                bv = pr[:, PCOL[f"bada_{l}"]:PCOL[f"bada_{l}"] + 48].rearrange("p (i c) -> p i c", c=2)

                def ada_out(b, s, bank, av=av, bv=bv):
                    i = lin(s, (b, RAWS))
                    return V.tensor_tensor(av[:, i], bank[:, 0:4].rearrange("p (m c) -> p m c", c=2)[:, :, 0],
                                           bv[:, i], ALU.add)
                columns(f"ada{l}", ada_out)
            dve.wait_ge(drained_dve, PH["aqk"].dd0)
            for l in range(2):
                for o in (8, 32):
                    link(V.tensor_scalar(ada[:, l, o:o + 8], ada[:, l, o:o + 8], 1.0, None, ALU.add))
            dve.wait_ge(pos_in, 16)
            link(V.tensor_copy(cosr[:], pos[:]))
            link(V.tensor_scalar(cosr[:], cosr[:], col("invf"), None, ALU.mult))
            two_pi = 2 * np.pi
            parts, left = [], two_pi
            for bits in (2 ** 5, 2 ** 13, 2 ** 21):
                v = float(np.floor(left * bits) / bits)
                parts.append(v)
                left -= v
            parts.append(float(left))
            magic = float(1.5 * 2 ** 23)
            for dst, shift in ((std, 0.25), (rstd, 0.0)):
                link(V.tensor_scalar(sinr[:], cosr[:], float(1 / two_pi), shift, ALU.mult, ALU.add))
                link(V.tensor_scalar(sinr[:], sinr[:], magic, None, ALU.add))
                link(V.tensor_scalar(sinr[:], sinr[:], -magic, None, ALU.add))
                link(V.scalar_tensor_tensor(dst[:], sinr[:], -parts[0], cosr[:], ALU.mult, ALU.add))
                for v in parts[1:]:
                    link(V.scalar_tensor_tensor(dst[:], sinr[:], -v, dst[:], ALU.mult, ALU.add))
                if shift:
                    link(V.tensor_scalar(dst[:], dst[:], float(np.pi / 2), None, ALU.add))
                link(V.tensor_scalar(dst[:], dst[:], 3.1415925, -3.1415925, ALU.min, ALU.max))
            V.sem_inc(trig_arg, 1)

            def rope(ntiles, k0):
                for i in range(ntiles // 2):
                    dve.wait_ge(swapped, k0 + i + 1)
                    if k0 + i:
                        dve.wait_ge(roped, k0 + i)
                    link(V.tensor_tensor(RT.rearrange("p (a t) -> p a t", a=2),
                                         ps[:, i % 8, :].rearrange("p (a t) -> p a t", a=2),
                                         SINA.unsqueeze(1).broadcast_to([P, 2, S]), ALU.mult))
                    dve.wait_ge(cos_done, k0 + i + 1)
                    V.tensor_tensor(QK[:, 2 * i:2 * i + 2, :].rearrange("p a t -> p (a t)"), RC[:, i % 2, :], RT,
                                    ALU.add).then_inc(roped, 1)

            def attention(groups, heads_of, masks, g0):
                G = len(masks)
                for i in range(groups):
                    dve.wait_ge(qk_done, g0 + i + 1)
                    if g0 + i:
                        dve.wait_ge(pt_done, g0 + i)
                    link(V.tensor_tensor(SS[:, 0:G, :], ps[:, 0:G, 0:TRI], MASK[:, masks[0]:masks[0] + G, :], ALU.add))
                    V.sem_inc(masked, 1)
                    V.tensor_reduce(st[:, 2:3], SS[:, 0:G, 0:128], AX.XY, ALU.max)
                    link(V.tensor_reduce(st[:, 3:4], SS[:, 0:G, 128:384], AX.XY, ALU.max))
                    V.tensor_scalar(st[:, 0:2], st[:, 2:4], -QSCALE, None, ALU.mult).then_inc(mx_ready, 1)
                    dve.wait_ge(exp_done, g0 + i + 1)
                    link(V.reciprocal(st[:, 6:8], st[:, 4:6]))
                    V.tensor_scalar(SS[:, 0:G, 0:128], SS[:, 0:G, 0:128], st[:, 6:7], None, ALU.mult)
                    V.tensor_scalar(SS[:, 0:G, 128:384], SS[:, 0:G, 128:384], st[:, 7:8], None,
                                    ALU.mult).then_inc(p_ready, 1)

            def add_residual(b, s, bank):
                xv = x[:].rearrange("p (i a) t -> p i (a t)", a=2)[:, lin(s, (b, RAWS))]
                return V.scalar_tensor_tensor(xv, xv, ALPHA, bank, ALU.mult, ALU.add)

            def first_half(m, bank):
                return V.scalar_tensor_tensor(x[:, m, :], x[:, m, :], ALPHA, bank, ALU.mult, ALU.add)

            def second_half(m, bank):
                return V.tensor_tensor(x[:, m, :], x[:, m, :], bank, ALU.add)

            dve.wait_ge(x_in, 16)
            V.sem_inc(src_ready, 1)
            rest_of(x[:])
            columns("aqk")
            columns("av")
            rope(16, 0)
            attention(16, lambda i: [i], [0], 0)
            rest_of(SRC)
            columns("ao", add_residual)
            layer_norm(x[:], "lnA0g", "lnA0b").then_inc(src_ready, 1)
            rest_of(x[:])
            relu_phase("ain0")
            rows("aout0", first_half)
            relu_phase("ain1")
            dve.wait_ge(drained_dve, PH["ain1"].dd0)
            rows("aout1", second_half)
            layer_norm(x[:], "lnA1g", "lnA1b").then_inc(src_ready, 1)
            rest_of(x[:])
            columns("bqk")
            columns("bv")
            rope(12, 8)
            attention(4, None, [1, 2, 3], 16)
            rest_of(SRC, 6)
            rows("bo", first_half)
            layer_norm(x[:], "lnA2g", "lnA2b").then_inc(src_ready, 1)
            rest_of(x[:])
            relu_phase("bin0")
            rows("bout0", first_half)
            relu_phase("bin1")
            rows("bout1", second_half)
            link(layer_norm(x[:], "lnA3g", "lnA3b"))
            modulate(0, 0).then_inc(src_ready, 1)

            taps = [0]
            for l in range(2):
                rest_of(SRC)
                V.memset(U[:, :, 0:TAPS - 1], 0.0)
                columns(f"pb{l}")

                def gated(b, s, bank):
                    i = lin(s, (b, RAWS))
                    cv = CV.rearrange("p (i a) t -> p i a t", a=2)[:, i]
                    uv = U.rearrange("p (i a) t -> p i a t", a=2)[:, i]
                    return V.tensor_tensor(uv[:, :, TAPS - 1:PADW], cv, bank.rearrange("p (a t) -> p a t", a=2),
                                           ALU.mult)
                columns(f"pa{l}", gated)
                wv = pr[:, PCOL[f"wdw_{l}"]:PCOL[f"wdw_{l}"] + KT * TAPS].rearrange("p (j k) -> p k j", k=TAPS)
                base = taps[0]

                def tap(i, wv=wv, base=base, l=l):
                    for j in range(KT):
                        if isinstance(i, int) and i == 0:
                            ins = V.tensor_scalar(CV[:, j, :], U[:, j, 0:S], wv[:, 0, j:j + 1], col(f"bdw_{l}", j),
                                                  ALU.mult, ALU.add)
                        else:
                            dve.wait_ge(tap_done, lin(base + j + 1 - KT, (i, KT)))
                            ins = V.scalar_tensor_tensor(CV[:, j, :], U[:, j, bass.ds(i, S)],
                                                         wv[:, i, j:j + 1], CV[:, j, :], ALU.mult, ALU.add)
                        ins.then_inc(tap_done, 1)
                dve.wait_ge(drained_dve, PH[f"pqk{l}"].dd0)
                tap(0)
                off = 1
                for nm in (f"pqk{l}", f"pv{l}", f"prg{l}", f"pgc{l}"):
                    columns(nm, extra=lambda i, off=off: tap(lin(off, (i, 1))))
                    off += PH[nm].n
                columns(f"pgr{l}")
                tap(29)
                tap(30)
                taps[0] += KT * TAPS
                layer_norm(CV).then_inc(u_ready, 1)
                rest_of(SRC)
                dve.wait_ge(decay_in, 16 * (l + 1))
                for h in range(RET_HEADS):
                    dve.wait_ge(st_done, 4 * l + h + 1)
                    if h >= 2:
                        dve.wait_ge(o_done, 8 * l + 2 * (h - 1))
                    V.tensor_tensor(RST[:, h % 2, :], ps[:, h % 2, 0:TRI], DEC[:, h, :], ALU.mult).then_inc(st_decayed, 1)
                sv = st[:, 16:64].rearrange("p (i c) -> p i c", c=6)
                mv = st[:, 64:80].rearrange("p (i c) -> p i c", c=2)
                for i in range(8):
                    dve.wait_ge(o_copied, 8 * l + i + 1)
                    link(V.bn_stats(sv[:, i], ON[:, i // 2, i % 2, :]))
                for i in range(8):
                    last = V.bn_aggr(mv[:, i], sv[:, i])
                last.then_inc(ovar, 1)
                dve.wait_ge(ostd, l + 1)
                link(V.reciprocal(st[:, 88:96], st[:, 80:88]))
                for i in range(8):
                    V.tensor_scalar(ON[:, i // 2, i % 2, :], ON[:, i // 2, i % 2, :], mv[:, i, 0:1],
                                    st[:, 88 + i:89 + i], ALU.subtract, ALU.mult).then_inc(o_normed, 1)
                for i in range(8):
                    dve.wait_ge(g_turned, 8 * l + i + 1)
                    rg = RG[:, 2 * i:2 * i + 2, :].rearrange("p a t -> p (a t)")
                    V.tensor_tensor(rg, rg, ps[:, i, :], ALU.mult).then_inc(hf_ready, 1)
                for i in range(8):
                    dve.wait_ge(mh_ready, nl[0] + i + 1)
                    V.tensor_tensor(ml[:, 2 * i:2 * i + 2, :], RG[:, 2 * i:2 * i + 2, :],
                                    mh[:, 2 * i:2 * i + 2, :].bitcast(F32), ALU.subtract).then_inc(hidden_ready, 1)
                nl[0] += 8

                def conv_gate(b, s, bank):
                    v = GC.rearrange("p (i a) t -> p i (a t)", a=2)[:, lin(s, (b, RAWS))]
                    return V.tensor_tensor(v, v, bank, ALU.mult)
                columns(f"co{l}", conv_gate)
                rows(f"ro{l}", lambda m, bank: V.tensor_tensor(GR[:, m, :], GR[:, m, :], bank, ALU.mult))
                dve.wait_ge(drained_dve, PH[f"wo{l}"].dd0)
                V.tensor_tensor(SRC, GR, GC, ALU.add).then_inc(src_ready, 1)
                rest_of(SRC)
                link(V.tensor_scalar(x[:], x[:], ALPHA, None, ALU.mult))

                def gated_add(which):
                    def go(m, bank):
                        g = ada[:, l, 24 * which + 16 + m:24 * which + 17 + m]
                        return V.scalar_tensor_tensor(x[:, m, :], bank, g, x[:, m, :], ALU.mult, ALU.add)
                    return go

                def mix_out(b, s, bank, l=l):
                    i = lin(s, (b, RAWS))
                    for a in range(2):
                        last = gated_add(0)(2 * i + a, bank[:, a * S:a * S + S])
                    return last
                columns(f"wo{l}", mix_out)
                link(layer_norm(x[:], f"ln1_{l}g", f"ln1_{l}b"))
                modulate(l, 1).then_inc(src_ready, 1)
                rest_of(SRC)
                if l == 0:
                    gate_phase(PH["gu0"], nl[0])
                    nl[0] += 11
                    link(V.tensor_scalar(x[:], x[:], ALPHA, None, ALU.mult))
                    rows("dn0", gated_add(1))
                    link(layer_norm(x[:], "ln2_0g", "ln2_0b"))
                    modulate(1, 0).then_inc(src_ready, 1)
                    continue
                dve.wait_ge(logits, 1)
                link(V.tensor_copy(LG, ps[:, 6, 0:16].rearrange("p (t e) -> p t e", t=2)))
                mx = st[:, 0:16].rearrange("p (t c) -> p t c", t=2)
                ixf = st[:, 16:32].rearrange("p (t c) -> p t c", t=2)
                for t in range(TT):
                    link(V.max(mx[:, t], LG[:, t]))
                    link(V.max_index(ix[:, 8 * t:8 * t + 8], mx[:, t], LG[:, t]))
                link(V.tensor_copy(st[:, 16:32], ix[:]))
                V.tensor_tensor(st[:, 32:34], mx[:, :, 1], mx[:, :, 0], ALU.subtract).then_inc(gap_ready, 1)
                dve.wait_ge(gap_exp, 1)
                link(V.tensor_scalar(st[:, 36:38], st[:, 34:36], 1.0, None, ALU.add))
                link(V.reciprocal(st[:, 38:40], st[:, 36:38]))
                link(V.tensor_tensor(st[:, 40:42], st[:, 38:40], st[:, 34:36], ALU.mult))
                for t in range(TT):
                    V.tensor_scalar(CMB[:, t], col("iota8", 0, 8), ixf[:, t, 0:1], st[:, 38 + t:39 + t],
                                    ALU.is_equal, ALU.mult)
                    link(V.tensor_scalar(CMB2[:, t], col("iota8", 0, 8), ixf[:, t, 1:2], st[:, 40 + t:41 + t],
                                         ALU.is_equal, ALU.mult))
                link(V.tensor_tensor(CMB, CMB, CMB2, ALU.add))
                V.tensor_copy(BC, CMB.rearrange("p t e -> p (t e)").unsqueeze(2).broadcast_to([P, 16, P])).then_inc(
                    comb_ready, 1)
                link(V.memset(ACC, 0.0))
                dve.wait_ge(cb_ready, 4)
                n0 = nl[0]
                with dve.Fori(0, EXPERTS) as e:
                    gate_phase(PH["gu1"], n0, e)
                    ph = PH["dn1"]
                    run_units(dve, ph, lambda b, s: split_ahead(ph, b, s, e))
                    dve.wait_ge(consumed, lin(2 * (ph.g0 + ph.n), (e, 2 * ph.g_e)))
                    for m in range(KT):
                        V.tensor_tensor(TMP[:, m % 2, :], ps[:, m, 0:S], CB[:, e, :], ALU.mult).then_inc(down_scaled, 1)
                        dve.wait_ge(down_scaled, lin(m + 1, (e, KT)))
                        V.tensor_tensor(ACC[:, m, :], ACC[:, m, :], TMP[:, m % 2, :], ALU.add).then_inc(drained_dve, 1)
                dve.wait_ge(drained_dve, PH["gu1"].dd0 + 19 * EXPERTS)
                link(V.tensor_scalar(x[:], x[:], ALPHA, None, ALU.mult))
                for m in range(KT):
                    last = gated_add(1)(m, ACC[:, m, :])
                last.then_inc(ln_in, 1)
                layer_norm(x[:], "ln2_1g", "ln2_1b").then_inc(final, 1)

        @block.tensor
        def _(pe):
            mm = nc.tensor.matmul

            def three(out, w, m, start, stop):
                (w_h, w_l), (m_h, m_l) = w, m
                mm(out, w_l, m_h, start=start, stop=False)
                mm(out, w_h, m_l, start=False, stop=False)
                return mm(out, w_h, m_h, start=False, stop=stop)

            def split_ready(ph, b, s, half, e):
                pe.wait_ge(lo_split, unit_no(ph, b, s, e, 2, half + 1))

            def columns(ph, kind, bank_free, e=0, moving_op=None):
                mhh, mll = moving_op or (xh, xl)

                def one(b, s):
                    w_h = wh[:, s % 2, :].rearrange("p (m k c) -> p m k c", m=2, k=KT)
                    w_l = wl[:, s % 2, :].rearrange("p (m k c) -> p m k c", m=2, k=KT)
                    bank_free(b, s)
                    split_ready(ph, b, s, 0, e)
                    if kind == "N":
                        split_ready(ph, b, s, 1, e)
                        for t in range(TT):
                            for k in range(KT):
                                tok = slice(t * P, t * P + P)
                                o = ps[:, s, t * 256:t * 256 + 256].rearrange("p (a c) -> p a c", a=2)
                                mm(o, mll[:, k, tok], w_h[:, :, k, :], start=k == 0, stop=False)
                                mm(o, mhh[:, k, tok], w_l[:, :, k, :], start=False, stop=False)
                                last = mm(o, mhh[:, k, tok], w_h[:, :, k, :], start=False, stop=k == KT - 1)
                        last.then_inc(consumed, 2)
                        return
                    n = mhh.shape[2]
                    for m in range(2):
                        if m:
                            split_ready(ph, b, s, 1, e)
                        for k in range(KT):
                            last = three(ps[:, s, m * n:m * n + n], (w_h[:, m, k, :], w_l[:, m, k, :]),
                                         (mhh[:, k, :], mll[:, k, :]), k == 0, k == KT - 1)
                        last.then_inc(consumed, 1)
                run_units(pe, ph, one, 0)

            def rows(ph, need, first_k=0, e=0, hidden=True):
                mhh, mll = (mh, ml) if hidden else (xh, xl)
                last_unit = ph.n - 1

                def one(b, s):
                    w_h = wh[:, s % 2, :].rearrange("p (k m c) -> p k m c", k=2, m=KT)
                    w_l = wl[:, s % 2, :].rearrange("p (k m c) -> p k m c", k=2, m=KT)
                    need(b, s)
                    for kk in range(2):
                        split_ready(ph, b, s, kk, e)
                        kt = lin(2 * s + kk, (b, 2 * RAWS))
                        st0 = isinstance(b, int) and b == 0 and s == 0 and kk == 0
                        sp0 = isinstance(b, int) and RAWS * b + s == last_unit and kk == 1
                        for m in range(KT):
                            last = three(ps[:, m, 0:S], (w_h[:, kk, m, :], w_l[:, kk, m, :]),
                                         (mhh[:, kt, :], mll[:, kt, :]), st0, sp0)
                        last.then_inc(consumed, 1)
                for i in range(ph.n):
                    one(i // RAWS, i % RAWS)

            def by_act(ph, e=0):
                def go(b, s):
                    pe.wait_ge(drained_act, lin(ph.da0 + s - 3, (b, RAWS)))
                return go

            def by_dve(ph, e=0):
                def go(b, s):
                    pe.wait_ge(drained_dve, lin(ph.dd0 + s - 3, (b, RAWS)))
                return go

            def all_free(ph, e=0):
                pe.wait_ge(drained_act, lin(ph.da0, (e, ph.da_e)))
                pe.wait_ge(drained_dve, lin(ph.dd0, (e, ph.dd_e)))

            def proj(name, by, kind="T"):
                ph = PH[name]
                all_free(ph)
                columns(ph, kind, by(ph))

            hid = [0]

            def relu_phase(name):
                ph = PH[name]
                all_free(ph)
                h0 = hid[0]
                hid[0] += ph.n

                def bank(b, s):
                    if not isinstance(b, int) or b > 0:
                        pe.wait_ge(nonlin, lin(nls[0] + s - 3, (b, RAWS)))
                columns(ph, "T", bank)
                nls[0] += ph.n
                return h0

            nls = [4]

            def out_phase(name, h0):
                ph = PH[name]
                all_free(ph)
                pe.wait_ge(nonlin, nls[0])
                rows(ph, lambda b, s: pe.wait_ge(hidden_ready, lin(h0 + s + 1, (b, RAWS))))

            lns = [0]

            def layer_norm(src, semaphore, value):
                n = lns[0]
                lns[0] += 1
                pe.wait_ge(semaphore, value)
                for k in range(KT):
                    last = mm(ps[:, 4, 0:S], ones, src[:, k, :], start=k == 0, stop=k == KT - 1)
                last.then_inc(ln_mean, 1)
                pe.wait_ge(ln_sq, n + 1)
                for k in range(KT):
                    last = mm(ps[:, 5, 0:S], ones, SRC[:, k, :], start=k == 0, stop=k == KT - 1)
                last.then_inc(ln_var, 1)

            def dve_after(name):
                return PH[name].dd0 + PH[name].dve_drains

            mv = [1]

            def moving_ready():
                mv[0] += 1
                pe.wait_ge(moving, mv[0])

            def rope(ntiles, k0):
                pe.wait_ge(drained_act, PH["ao"].da0 if k0 == 0 else PH["bo"].da0)
                for i in range(ntiles // 2):
                    mm(ps[:, i % 8, :], swap, QK[:, 2 * i:2 * i + 2, :].rearrange("p a t -> p (a t)"),
                       start=True, stop=True).then_inc(swapped, 1)

            def attention(groups, heads_of, g0, h0, ktile0):
                G = len(heads_of(0))
                for i in range(groups):
                    if i:
                        pe.wait_ge(masked, g0 + i)
                    for k, h in enumerate(heads_of(i)):
                        r = slice(64 * (h % 2), 64 * (h % 2) + 64)
                        q, kk = QK[r, h // 2, :], QK[r, ktile0 + h // 2, :]
                        mm(ps[:, k, 0:128], q[:, 0:128], kk[:, 0:128], start=True, stop=True)
                        last = mm(ps[:, k, 128:384], q[:, 128:256], kk[:, 0:256], start=True, stop=True)
                    last.then_inc(qk_done, 1)
                    pe.wait_ge(p_ready, g0 + i + 1)
                    for k in range(G):
                        for c in range(3):
                            last = nc.tensor.transpose(ps[:, 3 + k, c * P:c * P + P], SS[:, k, c * P:c * P + P], ident)
                    last.then_inc(pt_done, 1)
                    pe.wait_ge(pt_copied, g0 + i + 1)
                    for k, h in enumerate(heads_of(i)):
                        n = h0 + i * G + k
                        if n >= 2:
                            pe.wait_ge(ao_copied, n - 1)
                        r = slice(64 * (h % 2), 64 * (h % 2) + 64)
                        v0, v1 = VN[:, 0, h * 64:h * 64 + 64], VN[:, 1, h * 64:h * 64 + 64]
                        mm(ps[r, 6 + n % 2, 0:128], v0, PT[:, k, 0:128], start=True, stop=True)
                        mm(ps[r, 6 + n % 2, 128:256], v0, PT[:, k, 128:256], start=True, stop=False)
                        mm(ps[r, 6 + n % 2, 128:256], v1, PT[:, k, 256:384], start=False,
                           stop=True).then_inc(pv_done, 1)

            pe.wait_ge(consts_in, 16)
            pe.wait_ge(moving, 1)
            for l in range(2):
                ph = PH[f"ada{l}"]
                all_free(ph)
                columns(ph, "T", by_dve(ph), moving_op=(ch, cl))

            moving_ready()
            proj("aqk", by_act)
            proj("av", by_act, "N")
            rope(16, 0)
            pe.wait_ge(roped, 8)
            attention(16, lambda i: [i], 0, 0, 8)
            moving_ready()
            proj("ao", by_dve)
            layer_norm(x, drained_dve, dve_after("ao"))
            moving_ready()
            h0 = relu_phase("ain0")
            out_phase("aout0", h0)
            h0 = relu_phase("ain1")
            out_phase("aout1", h0)
            layer_norm(x, drained_dve, dve_after("aout1"))
            moving_ready()
            proj("bqk", by_act)
            proj("bv", by_act, "N")
            rope(12, 8)
            pe.wait_ge(roped, 14)
            attention(4, lambda j: [j, 4 + j, 8 + j], 16, 16, 6)
            moving_ready()
            ph = PH["bo"]
            all_free(ph)
            rows(ph, lambda b, s: None, hidden=False)
            layer_norm(x, drained_dve, dve_after("bo"))
            moving_ready()
            h0 = relu_phase("bin0")
            out_phase("bout0", h0)
            h0 = relu_phase("bin1")
            out_phase("bout1", h0)
            layer_norm(x, drained_dve, dve_after("bout1"))

            for l in range(2):
                moving_ready()
                proj(f"pb{l}", by_act)
                proj(f"pa{l}", by_dve)
                proj(f"pqk{l}", by_act)
                proj(f"pv{l}", by_act, "N")
                proj(f"prg{l}", by_act)
                proj(f"pgc{l}", by_act)
                proj(f"pgr{l}", by_act)
                pe.wait_ge(drained_act, PH[f"co{l}"].da0)
                layer_norm(CV, tap_done, KT * TAPS * (l + 1))
                pe.wait_ge(ret_roped, l + 1)
                for h in range(RET_HEADS + 1):
                    if h < RET_HEADS:
                        if h >= 2:
                            pe.wait_ge(st_decayed, 4 * l + h - 1)
                        for a in range(2):
                            mm(ps[:, h % 2, 0:256], RK[:, 2 * h + a, 0:128], RQ[:, 2 * h + a, :], start=a == 0, stop=a == 1)
                        for a in range(2):
                            last = mm(ps[:, h % 2, 256:384], RK[:, 2 * h + a, 128:256], RQ[:, 2 * h + a, 128:256],
                                      start=a == 0, stop=a == 1)
                        last.then_inc(st_done, 1)
                    if h >= 1:
                        g = h - 1
                        pe.wait_ge(st_decayed, 4 * l + g + 1)
                        va, vb = (RV[:, t, g * RET_DV:(g + 1) * RET_DV] for t in range(TT))
                        s_ = RST[:, g % 2, :]
                        i = 2 * g
                        if i >= 4:
                            pe.wait_ge(o_copied, 8 * l + i - 3)
                        elif g == 1:
                            pe.wait_ge(ln_std, lns[0])
                        mm(ps[:, 2 + i % 4, :], s_[:, 0:128], va, start=True, stop=True).then_inc(o_done, 1)
                        i += 1
                        if i >= 4:
                            pe.wait_ge(o_copied, 8 * l + i - 3)
                        mm(ps[:, 2 + i % 4, :], s_[:, 128:256], va, start=True, stop=False)
                        mm(ps[:, 2 + i % 4, :], s_[:, 256:384], vb, start=False, stop=True).then_inc(o_done, 1)
                pe.wait_ge(o_copied, 8 * l + 8)
                for i in range(8):
                    h, dd = i // 2, i % 2
                    pe.wait_ge(o_normed, 8 * l + 2 * h + 2)
                    for a in range(2):
                        for t in range(TT):
                            last = nc.tensor.transpose(
                                ps[:, i, a * S + t * P:a * S + t * P + P],
                                ON[:, h, t, (2 * dd + a) * P:(2 * dd + a) * P + P], ident)
                    last.then_inc(g_turned, 1)
                pe.wait_ge(hidden_ready, hid[0] + 8)
                moving_ready()
                proj(f"co{l}", by_dve)
                all_free(PH[f"ro{l}"])
                h0 = hid[0]
                hid[0] += 8
                rows(PH[f"ro{l}"], lambda b, s: None)
                moving_ready()
                proj(f"wo{l}", by_dve)
                layer_norm(x, drained_dve, dve_after(f"wo{l}"))
                moving_ready()

                def gate_up(ph, e=0):
                    if not ph.moe:
                        all_free(ph)

                    def bank(b, s):
                        if ph.moe and s == 0:
                            pe.wait_ge(drained_dve, lin(ph.dd0, (b, 1), (e, ph.dd_e)))
                        if isinstance(b, int) and b == 0:
                            return
                        if s % 2 == 0:
                            pe.wait_ge(drained_act, lin(ph.da0 + s // 2 - 1, (b, 2), (e, ph.da_e)))
                        else:
                            pe.wait_ge(drained_dve, lin(ph.dd0 + s // 2 - 1, (b, 2), (e, ph.dd_e)))
                    columns(ph, "T", bank, e)

                def down(ph, h0, e=0):
                    all_free(ph, e)
                    rows(ph, lambda b, s: pe.wait_ge(hidden_ready, lin(h0 + RAWS * b + s + 1, (e, 11))), e=e)

                if l == 0:
                    gate_up(PH["gu0"])
                    down(PH["dn0"], hid[0])
                    hid[0] += 11
                    layer_norm(x, drained_dve, dve_after("dn0"))
                else:
                    for t in range(TT):
                        for k in range(KT):
                            last = mm(ps[:, 6, 8 * t:8 * t + 8], SRC[:, k, t * P:t * P + P],
                                      pr[:, PCOL["wr"] + 8 * k:PCOL["wr"] + 8 * k + 8], start=k == 0, stop=k == KT - 1)
                    last.then_inc(logits, 1)
                    pe.wait_ge(comb_ready, 1)
                    for q in range(4):
                        for a in range(2):
                            for t in range(TT):
                                last = mm(ps[:, q, a * S + t * P:a * S + t * P + P], BC[:, 8 * t + 2 * q + a, :], ident,
                                          start=True, stop=True)
                        last.then_inc(comb_spread, 1)
                    pe.wait_ge(cb_ready, 4)
                    with pe.Fori(0, EXPERTS) as e:
                        gate_up(PH["gu1"], e)
                        down(PH["dn1"], hid[0], e)
                    layer_norm(x, ln_in, 1)


def col_units(w):
    n = w.shape[1] // 256
    return w.reshape(KT, P, n, 2, P).transpose(2, 1, 3, 0, 4).reshape(n, P, UNIT)


def row_units(w):
    n = w.shape[0] // 256
    return w.reshape(n, 2, P, D).transpose(0, 2, 1, 3).reshape(n, P, UNIT)


def feat(v):
    return v.reshape(-1, P).T


def shape_constants():
    cs = np.zeros((P, 3, P), np.float32)
    cs[:, 0] = np.eye(P)
    cs[:, 1] = 1.0 / D
    for h in range(2):
        for i in range(32):
            cs[64 * h + 32 + i, 2, 64 * h + i] = -1.0
            cs[64 * h + i, 2, 64 * h + 32 + i] = 1.0
    inv = (1.0 / (np.float32(10000.0) ** (np.arange(0, HEAD, 2, dtype=np.float32) / np.float32(HEAD)))).astype(np.float32)
    ang = (np.arange(S, dtype=np.float32)[:, None] * inv[None]).astype(np.float32)
    rows = np.arange(P) % 32
    cosa, sina = np.cos(ang).T[rows], np.sin(ang).T[rows]
    q, k = np.arange(S)[:, None], np.arange(S)[None]
    causal = k <= q
    seen = [causal, causal & (q - k <= 128), causal & ((q - k) % 4 == 0), causal & ((q - k) % 16 == 0)]
    masks = []
    for m in seen:
        a = np.where(m, 0.0, NEG).astype(np.float32)
        masks.append(np.concatenate([a[:P, :P], a[P:, :]], axis=1))
    block_a = np.concatenate(masks + [cosa, sina], axis=1).astype(np.float32)
    log_g = np.log1p(-np.exp2(-5.0 - np.arange(RET_HEADS)))
    dec = []
    for h in range(RET_HEADS):
        n, m = np.arange(S)[None], np.arange(S)[:, None]
        a = np.where(n >= m, np.exp(log_g[h] * np.maximum(n - m, 0)), 0.0) * RET_DK ** -0.5
        dec.append(np.concatenate([a[:P, :], a[P:, P:]], axis=1))
    decay = np.concatenate(dec, axis=1).astype(np.float32)
    invf = (np.float32(10000.0) ** (-np.arange(P, dtype=np.float32) / np.float32(P))).astype(np.float32)
    return cs, block_a, decay, invf


def kernel(**inputs):
    import concourse.bacc as _bacc
    from concourse.bass_utils import run_bass_kernel_spmd as _run

    a = {k: np.asarray(v) for k, v in inputs.items()}
    cs, block_a, decay, invf = shape_constants()

    ws = np.empty((TOTAL + LOOKAHEAD, P, UNIT), np.float32)

    def put(name, units, off=0):
        g = PH[name].g0 + off
        ws[g:g + len(units)] = units

    for l in range(2):
        put(f"ada{l}", col_units(a["w_ada_2"][l]))
    qkv, wo = a["moba_w_qkv"][0], a["moba_w_o"][0]
    put("aqk", col_units(qkv[:, :2 * D]))
    put("av", col_units(qkv[:, 2 * D:]))
    put("ao", col_units(wo))
    dq = a["dil_w_qkv"][0]
    put("bqk", col_units(dq[:, :1536]))
    put("bv", col_units(dq[:, 1536:]))
    put("bo", row_units(a["dil_w_o"][0]))
    for l, c in enumerate("ab"):
        for h in range(2):
            hs = slice(h * HALF_HIDDEN, (h + 1) * HALF_HIDDEN)
            put(f"{c}in{h}", col_units(a["mlp_w_in"][l][:, hs]))
            put(f"{c}out{h}", row_units(a["mlp_w_out"][l][hs]))
    for l in range(2):
        w = a["w_in_2"][l]
        put(f"pa{l}", col_units(w[:, 0:D]))
        put(f"pb{l}", col_units(w[:, D:2 * D]))
        put(f"pqk{l}", col_units(w[:, 2 * D:4 * D]))
        put(f"pv{l}", col_units(w[:, 4 * D:6 * D]))
        put(f"prg{l}", col_units(w[:, 6 * D:8 * D]))
        put(f"pgc{l}", col_units(w[:, 8 * D:9 * D]))
        put(f"pgr{l}", col_units(w[:, 9 * D:10 * D]))
        put(f"co{l}", col_units(a["w_conv_o_2"][l]))
        put(f"ro{l}", row_units(a["w_ret_o_2"][l]))
        put(f"wo{l}", col_units(a["w_out_2"][l]))

    def gated(g, u):
        return np.stack([col_units(g), col_units(u)], axis=1).reshape(-1, P, UNIT)

    put("gu0", gated(a["ffn_w_gate_2"][0], a["ffn_w_up_2"][0]))
    put("dn0", row_units(a["ffn_w_down_2"][0]))
    for e in range(EXPERTS):
        put("gu1", gated(a["moe_w_gate_2"][0, e], a["moe_w_up_2"][0, e]), 33 * e)
        put("dn1", row_units(a["moe_w_down_2"][0, e]), 33 * e)
    ws[TOTAL:] = ws[:LOOKAHEAD]

    par = np.zeros((P, NPAR), np.float32)

    def pcol(name, v):
        par[:, PCOL[name]:PCOL[name] + v.shape[1]] = v

    for i, (g, b) in enumerate([("ln_mix", 0), ("ln_mlp", 0), ("ln_mix", 1), ("ln_mlp", 1)]):
        pcol(f"lnA{i}g", feat(a[f"{g}_g"][b]))
        pcol(f"lnA{i}b", feat(a[f"{g}_b"][b]))
    for l in range(2):
        for k, nm in (("c", "ln_conv"), ("1", "ln1"), ("2", "ln2")):
            pcol(f"ln{k}_{l}g", feat(a[f"{nm}_g_2"][l]))
            pcol(f"ln{k}_{l}b", feat(a[f"{nm}_b_2"][l]))
        pcol(f"bdw_{l}", feat(a["b_dw_2"][l]))
        pcol(f"bada_{l}", feat(a["b_ada_2"][l]))
        pcol(f"wdw_{l}", a["w_dw_2"][l].reshape(TAPS, KT, P).transpose(2, 1, 0).reshape(P, KT * TAPS))
    pcol("c", feat(a["c_2"][0]))
    pcol("invf", invf[:, None])
    pcol("iota8", np.tile(np.arange(8, dtype=np.float32), (P, 1)))
    pcol("eps", np.full((P, 1), EPS, np.float32))
    pcol("wr", a["moe_w_router_2"][0].reshape(KT, P, EXPERTS).transpose(1, 0, 2).reshape(P, KT * EXPERTS))

    arrays = {
        "wstream": ws,
        "xT": np.ascontiguousarray(a["x"][0].reshape(S, KT, P).transpose(2, 1, 0)),
        "par": par,
        "posb": np.ascontiguousarray(np.broadcast_to(a["positions_2"].astype(np.int32).reshape(1, S), (P, S))),
        "consts": cs, "blocka": block_a, "decay": decay,
    }
    nc = _bacc.Bacc("TRN2", target_bir_lowering=False, num_devices=1)
    args = [nc.dram_tensor(n, v.shape, mybir.dt.from_np(v.dtype), kind="ExternalInput").ap() for n, v in arrays.items()]
    out = nc.dram_tensor("outT", (P, KT, S), F32, kind="ExternalOutput").ap()
    build(nc, *args, out)
    r = _run(nc, [arrays], core_ids=[0])
    got = r.results[0]["outT"]
    return np.ascontiguousarray(got.transpose(2, 1, 0).reshape(1, S, D))
```

```python
from contextlib import ExitStack

import numpy as np

import concourse.bass as bass
from concourse import mybir

P = 128
S = 256
D = 1024
KT = D // P
TT = S // P
UNIT = 2048
RAWS = 4
HEAD = 64
HALF_HIDDEN = 2048
FF = 2816
FT = FF // P
EXPERTS = 8
BLK = 128
JOBS = 16
RET_HEADS = 4
RET_DK = 256
RET_DV = 512
TAPS = 31
ALPHA = float(4.0 ** 0.25)
EPS = 1e-5
NEG = -1e30
QSCALE = HEAD ** -0.5
TRI = 384

F32 = mybir.dt.float32
F32R = mybir.dt.float32r
I32 = mybir.dt.int32
U32 = mybir.dt.uint32
ALU = mybir.AluOpType
ACT = mybir.ActivationFunctionType
AX = mybir.AxisListType

PCOL = {}
_n = 0
for _name, _w in ([(f"lnA{i}{c}", KT) for i in range(4) for c in "gb"]
                  + [(f"ln{k}_{l}{c}", KT) for l in range(2) for k in ("c", "1", "2") for c in "gb"]
                  + [(f"bdw_{l}", KT) for l in range(2)] + [(f"bada_{l}", 48) for l in range(2)]
                  + [("c", KT), ("invf", 1), ("iota", P), ("eps", 1), ("wr", 8 * EXPERTS)]
                  + [(f"wdw_{l}", KT * TAPS) for l in range(2)]):
    PCOL[_name] = _n
    _n += _w
NPAR = _n

ORDER = [("ada0", 24, "ada"), ("ada1", 24, "ada"),
         ("aqk", 8, "T"), ("av", 4, "N"), ("ao", 4, "T"),
         ("ain0", 8, "relu"), ("aout0", 8, "R"), ("ain1", 8, "relu"), ("aout1", 8, "R"),
         ("bqk", 6, "T"), ("bv", 3, "N"), ("bo", 3, "R"),
         ("bin0", 8, "relu"), ("bout0", 8, "R"), ("bin1", 8, "relu"), ("bout1", 8, "R")]
for _l in range(2):
    ORDER += [(f"pb{_l}", 4, "T"), (f"pa{_l}", 4, "T"), (f"pqk{_l}", 8, "T"), (f"pv{_l}", 8, "N"),
              (f"prg{_l}", 8, "T"), (f"pgc{_l}", 4, "T"), (f"pgr{_l}", 4, "T"),
              (f"co{_l}", 4, "T"), (f"ro{_l}", 8, "R"), (f"wo{_l}", 4, "T"),
              (f"gu{_l}", 22, "T"), (f"dn{_l}", 11, "R")]


class Phase:
    pass


def slot_uses(n):
    return [len(range(s, n, RAWS)) for s in range(RAWS)]


def plan():
    phases = {}
    g, uses, da, dd = 0, [0] * RAWS, 4, 4
    prev_n = None
    eu = [a + b for a, b in zip(slot_uses(22), slot_uses(11))]
    for name, n, kind in ORDER:
        p = Phase()
        p.name, p.n, p.kind, p.g0, p.uses0 = name, n, kind, g, list(uses)
        p.moe = name in ("gu1", "dn1")
        p.g_e, p.uses_e = (33, eu) if p.moe else (0, [0] * RAWS)
        p.raw_back = None if prev_n is None else [
            min(prev_n - i for i in range(prev_n) if i % RAWS == s) if prev_n > s else RAWS for s in range(RAWS)]
        p.pair_back = None if prev_n is None else [
            min([prev_n - i for i in range(prev_n) if i % 2 == s]) for s in range(2)]
        if name == "gu1":
            p.raw_back, p.pair_back = [3, 2, 1, 1], [1, 1]
        if prev_n == 3:
            p.raw_back = [3, 2, 1, 1]
        p.da0, p.dd0 = da, dd
        ga = {"gu": n // 2, "pb": n, "pq": n, "pv": n, "pr": n, "pg": n}.get(name[:2], 0)
        ga = n if name in ("aqk", "av", "bqk", "bv") else ga
        p.act_drains = ga
        p.dve_drains = {"R": 8, "relu": 0}.get(kind, n - ga)
        p.da_e, p.dd_e = (11, 11) if p.moe else (0, 0)
        da, dd = da + p.act_drains, dd + p.dve_drains
        g += n
        uses = [a + b for a, b in zip(uses, slot_uses(n))]
        prev_n = n
        phases[name] = p
    names = [n for n, _, _ in ORDER]
    for a, b in zip(names, names[1:]):
        phases[a].next = phases[b]
    phases["dn1"].next = phases["gu1"]
    return phases, g


PH, STREAM = plan()
TOTAL = PH["gu1"].g0 + 33 * EXPERTS
LOOKAHEAD = 2


ROW_M = [4, 5, 6, 7, 0, 1, 2, 3]


def lin(const, *terms):
    for reg, k in terms:
        if k and not (isinstance(reg, int) and reg == 0):
            const = reg * k + const
    return const


def build(nc, wstream, xT, par, posb, consts, blockA, decay, outT):
    with ExitStack() as ctx:
        def sb(name, shape, dt=F32):
            return ctx.enter_context(nc.sbuf_tensor(name, shape, dt))

        def sem(name):
            return ctx.enter_context(nc.semaphore(name))

        raw = sb("raw", [P, RAWS, UNIT])
        wh = sb("wh", [P, 2, UNIT], F32R)
        wl = sb("wl", [P, 2, UNIT], F32R)
        x = sb("x", [P, KT, S])
        xh = sb("xh", [P, KT, S], F32R)
        xl = sb("xl", [P, KT, S], F32R)
        cs = sb("cs", [P, 4, P])
        ji = sb("ji", [P, JOBS + 1], I32)
        pr = sb("pr", [P, NPAR])
        cosr = sb("cosr", [P, S])
        sinr = sb("sinr", [P, S])
        std = sb("std", [P, S])
        rstd = sb("rstd", [P, S])
        ada = sb("ada", [P, 2, 48])
        cf = sb("cf", [P, KT])
        bs = sb("bs", [P, KT])
        st = sb("st", [P, 128])
        ix = sb("ix", [P, 16], U32)
        pos = sb("pos", [P, S], I32)
        work = sb("work", [P, 14592])
        with ExitStack() as hidden:
            mh = hidden.enter_context(nc.sbuf_tensor("mh", [P, FT, S], F32R))
            ml = hidden.enter_context(nc.sbuf_tensor("ml", [P, FT, S], F32R))
        CH = mh[:, 0:4, :].rearrange("p a (b c) -> p (a b) c", c=P)
        CL = ml[:, 0:4, :].rearrange("p a (b c) -> p (a b) c", c=P)
        with ExitStack() as mixer:
            ret = mixer.enter_context(nc.sbuf_tensor("ret", [P, 11264], F32))
        hn = sb("hn", [P, TT, D])
        jmh = sb("jmh", [P, FT, BLK], F32R)
        jml = sb("jml", [P, FT, BLK], F32R)
        gx = sb("gx", [P, TT, BLK])
        gt = sb("gt", [P, S], F32R)

        def view(buf, off, width, pat, **kw):
            return buf[:, off:off + width].rearrange(pat, **kw)

        ident, ones, swap = cs[:, 0, :], cs[:, 1, :], cs[:, 2, :]
        RG = view(work, 0, 4096, "p (j t) -> p j t", t=S)
        GC = view(work, 4096, 2048, "p (j t) -> p j t", t=S)
        GR = view(work, 6144, 2048, "p (j t) -> p j t", t=S)
        PADW = TAPS - 1 + S
        U = view(work, 8192, KT * PADW, "p (j t) -> p j t", t=PADW)
        CV = view(work, 10480, 2048, "p (j t) -> p j t", t=S)
        SRC = view(work, 12528, 2048, "p (j t) -> p j t", t=S)
        ON = view(work, 8192, 4096, "p (h n d) -> p h n d", h=RET_HEADS, n=TT)
        RQ = view(ret, 0, 2048, "p (j t) -> p j t", t=S)
        RK = view(ret, 2048, 2048, "p (j t) -> p j t", t=S)
        RV = view(ret, 4096, 4096, "p (t c) -> p t c", t=TT)
        DEC = view(ret, 8192, RET_HEADS * TRI, "p (h c) -> p h c", h=RET_HEADS)
        RST = view(ret, 8192 + 1536, 2 * TRI, "p (h c) -> p h c", h=2)
        QK = view(work, 0, 4096, "p (j t) -> p j t", t=S)
        VN = view(work, 4096, 2048, "p (t c) -> p t c", t=TT)
        RC = view(work, 6144, 1024, "p (b c) -> p b c", b=2)
        SS = view(work, 7168, 3 * TRI, "p (g c) -> p g c", g=3)
        PT = view(work, 8320, 3 * TRI, "p (g c) -> p g c", g=3)
        MASK = view(work, 9472, 4 * TRI, "p (g c) -> p g c", g=4)
        COSA = work[:, 11008:11264]
        SINA = work[:, 11264:11520]
        RT = work[:, 11520:12032]
        SG = work[:, 0:512]
        HF = work[:, 512:1024]
        HF2 = view(work, 512, 512, "p (b c) -> p b c", b=2)
        YF = work[:, 1024:2048]
        DG = view(work, 0, 48 * P, "p (i m c) -> p i m c", i=24, m=2)
        LG = view(work, 2048, 16, "p (t e) -> p t e", t=TT)
        CMB = view(work, 2064, 16, "p (t e) -> p t e", t=TT)
        CMB2 = view(work, 2080, 16, "p (t e) -> p t e", t=TT)
        SEL = view(work, 2096, 16, "p (t e) -> p t e", t=TT)
        SEL2 = view(work, 2112, 16, "p (t e) -> p t e", t=TT)
        POS = view(work, 2128, 16, "p (t e) -> p t e", t=TT)
        CNT = work[:, 2144:2152]
        CUM = view(work, 2152, 4 * 12, "p (i c) -> p i c", i=4)
        EXPJ = work[:, 2200:2216]
        STARTJ = work[:, 2216:2232]
        PJ = view(work, 2232, 2 * JOBS, "p (t j) -> p t j", t=TT)
        CJ = view(work, 2264, 2 * JOBS, "p (t j) -> p t j", t=TT)
        WS = work[:, 2296:2297]
        MJ = view(work, 2304, 4 * 8 * JOBS, "p (t e j) -> p t e j", t=4, e=EXPERTS)
        ACC = view(work, 4096, 2048, "p (j t) -> p j t", t=S)

        ps = ctx.enter_context(nc.psum_tensor("ps", [P, 8, 512], F32))

        def col(name, j=0, w=1):
            return pr[:, PCOL[name] + j:PCOL[name] + j + w]

        landed = [sem(f"raw_landed{s}") for s in range(RAWS)]
        hi_split = sem("hi_split")
        lo_split = sem("lo_split")
        consumed = sem("consumed")
        drained_act = sem("drained_act")
        drained_dve = sem("drained_dve")
        consts_in = sem("consts_in")
        x_in = sem("x_in")
        par_in = sem("par_in")
        pos_in = sem("pos_in")
        blocka_in = sem("blocka_in")
        decay_in = sem("decay_in")
        out_done = sem("out_done")
        src_ready = sem("src_ready")
        xh_ready = sem("xh_ready")
        moving = sem("moving")
        nonlin = sem("nonlin")
        hf_ready = sem("hf_ready")
        mh_ready = sem("mh_ready")
        hidden_ready = sem("hidden_ready")
        ln_mean = sem("ln_mean")
        ln_cen = sem("ln_cen")
        ln_sq = sem("ln_sq")
        ln_var = sem("ln_var")
        ln_std = sem("ln_std")
        swapped = sem("swapped")
        cos_done = sem("cos_done")
        roped = sem("roped")
        qk_done = sem("qk_done")
        masked = sem("masked")
        mx_ready = sem("mx_ready")
        exp_done = sem("exp_done")
        p_ready = sem("p_ready")
        pt_done = sem("pt_done")
        pt_copied = sem("pt_copied")
        pv_done = sem("pv_done")
        ao_copied = sem("ao_copied")
        vstep = sem("vstep")
        pstep = sem("pstep")
        tap_done = sem("tap_done")
        trig_arg = sem("trig_arg")
        trig_done = sem("trig_done")
        ret_roped = sem("ret_roped")
        st_done = sem("st_done")
        st_decayed = sem("st_decayed")
        o_done = sem("o_done")
        o_copied = sem("o_copied")
        ovar = sem("ovar")
        ostd = sem("ostd")
        o_normed = sem("o_normed")
        g_turned = sem("g_turned")
        logits = sem("logits")
        gap_ready = sem("gap_ready")
        gap_exp = sem("gap_exp")
        sel_ready = sem("sel_ready")
        ranked = sem("ranked")
        jobs_ready = sem("jobs_ready")
        h_turned = sem("h_turned")
        h_copied = sem("h_copied")
        turned = sem("turned")
        g_ready = sem("g_ready")
        xg_filled = sem("xg_filled")
        xg_hi = sem("xg_hi")
        xg_lo = sem("xg_lo")
        gt_filled = sem("gt_filled")
        gt_copied = sem("gt_copied")
        yf_done = sem("yf_done")
        y_hi = sem("y_hi")
        y_split = sem("y_split")
        sc_filled = sem("sc_filled")
        sc_added = sem("sc_added")
        ln_in = sem("ln_in")
        final = sem("final")
        u_ready = sem("u_ready")
        c_act = sem("c_act")

        block = ctx.enter_context(nc.Block())

        def run_units(eng, ph, emit, ahead=LOOKAHEAD):
            nb = max((ph.n - ahead) // RAWS, 0)
            if nb > 1:
                with eng.Fori(0, nb) as b:
                    for s in range(RAWS):
                        emit(b, s)
            else:
                nb = 0
            for i in range(nb * RAWS, ph.n):
                emit(i // RAWS, i % RAWS)

        def job_units(eng, ph, emit, middle):
            for s in range(RAWS):
                emit(0, s)
            middle()
            with eng.Fori(1, (ph.n - LOOKAHEAD) // RAWS) as b:
                for s in range(RAWS):
                    emit(b, s)
            for i in range((ph.n - LOOKAHEAD) // RAWS * RAWS, ph.n):
                emit(i // RAWS, i % RAWS)

        def ahead_of(ph, b, s, e):
            s2 = s + LOOKAHEAD
            if isinstance(b, int) and RAWS * b + s2 >= ph.n:
                i = RAWS * b + s2 - ph.n
                return ph.next, i // RAWS, i % RAWS, (e + 1 if ph.name == "dn1" else e)
            return ph, b + s2 // RAWS, s2 % RAWS, e

        def unit_no(ph, b, s, e, k=1, add=0):
            return lin(k * (ph.g0 + s) + add, (b, k * RAWS), (e, k * ph.g_e))

        @block.sync
        def _(sp):
            sp.dma_start(cs[:], consts).then_inc(consts_in, 16)
            sp.dma_start(pr[:], par).then_inc(par_in, 16)

            def stream(ph, e=0):
                def load(b, s, peeled):
                    if peeled and ph.raw_back is not None:
                        sp.wait_ge(lo_split, lin(2 * (ph.g0 - ph.raw_back[s] + 1), (e, 2 * ph.g_e)))
                    elif not peeled:
                        sp.wait_ge(lo_split, unit_no(ph, b, s, e, 2, -2 * RAWS + 2))
                    sp.dma_start(raw[:, s, :], wstream[unit_no(ph, b, s, e)]).then_inc(landed[s], 16)
                for s in range(min(RAWS, ph.n)):
                    load(0, s, True)
                nb = ph.n // RAWS
                if nb > 1:
                    with sp.Fori(1, nb) as b:
                        for s in range(RAWS):
                            load(b, s, False)
                for i in range(max(nb, 1) * RAWS, ph.n):
                    load(i // RAWS, i % RAWS, False)

            def jobs(sp):
                gu, dn = PH["gu1"], PH["dn1"]

                def load(ph, b, s, j, expert):
                    if isinstance(b, int) and b == 0:
                        sp.wait_ge(lo_split, lin(2 * (ph.g0 - ph.raw_back[s] + 1), (j, 2 * ph.g_e)))
                    else:
                        sp.wait_ge(lo_split, unit_no(ph, b, s, j, 2, -2 * RAWS + 2))
                    sp.dma_start(raw[:, s, :], wstream[unit_no(ph, b, s, expert)]).then_inc(landed[s], 16)
                for s in range(LOOKAHEAD):
                    load(gu, 0, s, 0, 0)
                sp.wait_ge(jobs_ready, 1)
                n_jobs = sp.value_load(ji[0:1, JOBS:JOBS + 1], min_val=EXPERTS, max_val=JOBS - 1)
                with sp.Fori(0, n_jobs) as j:
                    expert = sp.value_load(ji[0:1, bass.ds(j, 1)], min_val=0, max_val=EXPERTS - 1)
                    for s in range(LOOKAHEAD, RAWS):
                        load(gu, 0, s, j, expert)
                    with sp.Fori(1, gu.n // RAWS) as b:
                        for s in range(RAWS):
                            load(gu, b, s, j, expert)
                    for i in range(gu.n // RAWS * RAWS, gu.n):
                        load(gu, i // RAWS, i % RAWS, j, expert)
                    for i in range(dn.n):
                        load(dn, i // RAWS, i % RAWS, j, expert)
                    after = sp.value_load(ji[0:1, bass.ds(j + 1, 1)], min_val=0, max_val=EXPERTS)
                    for s in range(LOOKAHEAD):
                        load(gu, 0, s, j + 1, after)

            for name, _, _ in ORDER:
                ph = PH[name]
                if name == "dn1":
                    continue
                if name == "gu1":
                    jobs(sp)
                    continue
                stream(ph)
                if name == "ada0":
                    sp.dma_start(x[:], xT).then_inc(x_in, 16)
                    sp.dma_start(pos[:], posb).then_inc(pos_in, 16)
                    sp.dma_start(work[:, 9472:11520], blockA).then_inc(blocka_in, 16)
                if name[:2] == "pb":
                    sp.wait_ge(consumed, 2 * ph.g0)
                    sp.dma_start(ret[:, 8192:8192 + 1536], decay).then_inc(decay_in, 16)
            sp.wait_ge(final, 1)
            sp.dma_start(outT, x[:]).then_inc(out_done, 16)
            sp.wait_ge(out_done, 16)

        @block.scalar
        def _(act):
            A = nc.scalar.activation

            def split(ph, b, s, e=0):
                r = raw[:, s, :].rearrange("p (h c) -> p h c", h=2)
                o = wh[:, s % 2, :].rearrange("p (h c) -> p h c", h=2)
                act.wait_ge(landed[s], lin(16 * (ph.uses0[s] + 1), (b, 16), (e, 16 * ph.uses_e[s])))
                for half in range(2):
                    if isinstance(b, int) and b == 0 and s < 2:
                        if ph.pair_back is not None:
                            act.wait_ge(consumed, lin(2 * (ph.g0 - ph.pair_back[s]) + half + 1, (e, 2 * ph.g_e)))
                    else:
                        act.wait_ge(consumed, unit_no(ph, b, s, e, 2, half + 1 - 4))
                    A(o[:, half], r[:, half], ACT.Copy).then_inc(hi_split, 1)

            def split_ahead(ph, b, s, e=0):
                split(*ahead_of(ph, b, s, e))

            def filled(ph, b, s, e=0):
                act.wait_ge(consumed, unit_no(ph, b, s, e, 2, 2))

            def columns(name, drain=None):
                ph = PH[name]
                if drain is not None and ph.dd0 > 4:
                    act.wait_ge(drained_dve, ph.dd0)

                def one(b, s):
                    split_ahead(ph, b, s)
                    if drain is not None:
                        filled(ph, b, s)
                        drain(lin(s, (b, RAWS)), ps[:, s, :]).then_inc(drained_act, 1)
                run_units(act, ph, one)

            copies = [0, 0, 0]

            def xh_from(src, tiles=KT):
                for c in range(tiles // 2):
                    copies[0] += 1
                    act.wait_ge(src_ready, copies[0])
                    A(xh[:, 2 * c:2 * c + 2, :], src[:, 2 * c:2 * c + 2, :], ACT.Copy).then_inc(xh_ready, 1)

            lns = [0]

            def layer_norm(src):
                n = lns[0]
                lns[0] += 1
                for c in range(4):
                    act.wait_ge(ln_cen, 4 * n + c + 1)
                    A(SRC[:, 2 * c:2 * c + 2, :], src[:, 2 * c:2 * c + 2, :], ACT.Square).then_inc(ln_sq, 1)
                act.wait_ge(ln_var, n + 1)
                A(std[:], ps[:, 5, 0:S], ACT.Sqrt, bias=col("eps")).then_inc(ln_std, 1)

            nl = [0]

            def relu_phase(name):
                ph, n0 = PH[name], nl[0]
                nl[0] += ph.n

                def one(b, s):
                    split_ahead(ph, b, s)
                    filled(ph, b, s)
                    A(SG, ps[:, s, :], ACT.Relu).then_inc(nonlin, 1)
                    act.wait_ge(hf_ready, lin(n0 + s + 1, (b, RAWS)))
                    A(mh[:, :, :].rearrange("p (i a) t -> p i (a t)", a=2)[:, lin(s, (b, RAWS))], HF,
                      ACT.Copy).then_inc(mh_ready, 1)
                run_units(act, ph, one)

            def gate_unit(ph, n0):
                def one(b, s):
                    split_ahead(ph, b, s)
                    if s % 2 == 0:
                        filled(ph, b, s)
                        A(SG, ps[:, s, :], ACT.Silu).then_inc(drained_act, 1)
                    else:
                        act.wait_ge(hf_ready, lin(n0 + s // 2 + 1, (b, 2)))
                        A(mh[:, :, :].rearrange("p (i a) t -> p i (a t)", a=2)[:, lin(s // 2, (b, 2))], HF,
                          ACT.Copy).then_inc(mh_ready, 1)
                return one

            def job_unit(ph, n0, j):
                def one(b, s):
                    split_ahead(ph, b, s, j)
                    if s % 2 == 0:
                        act.wait_ge(hf_ready, lin(n0 + s // 2, (b, 2), (j, 11)))
                        filled(ph, b, s, j)
                        A(SG[:, 0:256], ps[:, s, 0:256], ACT.Silu).then_inc(drained_act, 1)
                    elif not (isinstance(b, int) and b == 0 and s == 1):
                        upper(lin(s // 2 - 1, (b, 2)), (s // 2 + 1) % 2, j)
                return one

            def upper(i, parity, j):
                act.wait_ge(turned, lin(i + 2, (j, 11)))
                A(jmh[:].rearrange("p (i a) t -> p i (a t)", a=2)[:, i], ps[:, 4 + parity, 0:256],
                  ACT.Copy).then_inc(mh_ready, 1)

            act.sem_inc(drained_act, 4)
            act.sem_inc(drained_dve, 4)
            act.sem_inc(nonlin, 4)
            act.wait_ge(par_in, 16)
            A(cf[:], col("c", 0, KT), ACT.Silu).then_inc(c_act, 1)
            act.wait_ge(c_act, 1)
            A(CH, cf[:].unsqueeze(2).broadcast_to([P, KT, P]), ACT.Copy).then_inc(c_act, 1)
            split(PH["ada0"], 0, 0)
            split(PH["ada0"], 0, 1)
            columns("ada0")
            columns("ada1")
            act.wait_ge(trig_arg, 1)
            A(cosr[:], std[:], ACT.Sin)
            A(sinr[:], rstd[:], ACT.Sin).then_inc(trig_done, 1)

            def attention(groups, heads_of, g0, h0):
                G = len(heads_of(0))
                for i in range(groups):
                    act.wait_ge(mx_ready, g0 + i + 1)
                    A(SS[:, 0:G, 0:128], SS[:, 0:G, 0:128], ACT.Exp, bias=st[:, 0:1], scale=QSCALE,
                      accum_out=st[:, 4:5])
                    A(SS[:, 0:G, 128:384], SS[:, 0:G, 128:384], ACT.Exp, bias=st[:, 1:2], scale=QSCALE,
                      accum_out=st[:, 5:6]).then_inc(exp_done, 1)
                    act.wait_ge(pt_done, g0 + i + 1)
                    A(PT[:, 0:G, :], ps[:, 3:3 + G, 0:TRI], ACT.Copy).then_inc(pt_copied, 1)
                    for k, h in enumerate(heads_of(i)):
                        n = h0 + i * G + k
                        r = slice(64 * (h % 2), 64 * (h % 2) + 64)
                        act.wait_ge(pv_done, n + 1)
                        A(SRC[r, h // 2, :], ps[r, 6 + n % 2, 0:S], ACT.Copy).then_inc(ao_copied, 1)

            def pairs_out(dst):
                v = dst.rearrange("p (i a) t -> p i (a t)", a=2)
                return lambda i, bank: A(v[:, i], bank, ACT.Copy)

            def tokens_out(dst):
                v = dst.rearrange("p t (i c) -> p i t c", c=256)
                return lambda i, bank: A(v[:, i], bank.rearrange("p (t c) -> p t c", t=2), ACT.Copy)

            def pairs_act(dst, func):
                v = dst.rearrange("p (i a) t -> p i (a t)", a=2)
                return lambda i, bank: A(v[:, i], bank, func)

            xh_from(x[:])
            columns("aqk", pairs_out(QK[:, 0:16, :]))
            columns("av", tokens_out(VN))
            attention(16, lambda i: [i], 0, 0)
            act.wait_ge(ao_copied, 16)
            act.sem_inc(src_ready, 4)
            xh_from(SRC)
            columns("ao")
            layer_norm(x[:])
            xh_from(x[:])
            relu_phase("ain0")
            columns("aout0")
            relu_phase("ain1")
            columns("aout1")
            layer_norm(x[:])
            xh_from(x[:])
            columns("bqk", pairs_out(QK[:, 0:12, :]))
            columns("bv", tokens_out(VN[:, :, 0:768]))
            attention(4, lambda j: [j, 4 + j, 8 + j], 16, 16)
            act.wait_ge(ao_copied, 28)
            act.sem_inc(src_ready, 3)
            xh_from(SRC, 6)
            columns("bo")
            layer_norm(x[:])
            xh_from(x[:])
            relu_phase("bin0")
            columns("bout0")
            relu_phase("bin1")
            columns("bout1")
            layer_norm(x[:])

            for l in range(2):
                xh_from(SRC)
                columns(f"pb{l}", pairs_act(CV, ACT.Sigmoid))
                columns(f"pa{l}")
                columns(f"pqk{l}", pairs_out(ret[:, 0:4096].rearrange("p (j t) -> p j t", t=S)))
                columns(f"pv{l}", tokens_out(RV))
                columns(f"prg{l}", pairs_act(RG, ACT.Silu))
                columns(f"pgc{l}", pairs_act(GC, ACT.Sigmoid))
                columns(f"pgr{l}", pairs_act(GR, ACT.Sigmoid))
                act.wait_ge(ret_roped, l + 1)
                layer_norm(CV)
                for j in range(KT):
                    act.wait_ge(u_ready, 4 * l + j // 2 + 1)
                    last = A(SRC[:, j, :], CV[:, j, :], ACT.Silu, bias=col(f"lnc_{l}b", j), scale=col(f"lnc_{l}g", j))
                    if j % 2:
                        last.then_inc(src_ready, 1)
                xh_from(SRC)
                for i in range(8):
                    act.wait_ge(o_done, 8 * l + i + 1)
                    A(ON[:, i // 2, i % 2, :], ps[:, 2 + i % 4, :], ACT.Copy).then_inc(o_copied, 1)
                act.wait_ge(ovar, l + 1)
                A(st[:, 80:88], st[:, 64:80].rearrange("p (i c) -> p i c", c=2)[:, :, 1], ACT.Sqrt,
                  bias=col("eps")).then_inc(ostd, 1)
                for i in range(8):
                    act.wait_ge(hf_ready, nl[0] + i + 1)
                    A(mh[:, 2 * i:2 * i + 2, :], RG[:, 2 * i:2 * i + 2, :], ACT.Copy).then_inc(mh_ready, 1)
                nl[0] += 8
                columns(f"co{l}")
                columns(f"ro{l}")
                xh_from(SRC)
                columns(f"wo{l}")
                layer_norm(x[:])
                xh_from(SRC)
                if l == 0:
                    run_units(act, PH["gu0"], gate_unit(PH["gu0"], nl[0]))
                    nl[0] += 11
                    columns("dn0")
                    layer_norm(x[:])
                else:
                    act.wait_ge(gap_ready, 1)
                    A(st[:, 34:36], st[:, 32:34], ACT.Exp).then_inc(gap_exp, 1)
                    for i in range(4):
                        act.wait_ge(h_turned, i + 1)
                        A(hn[:, i // 2, i % 2 * 512:i % 2 * 512 + 512], ps[:, i, :], ACT.Copy).then_inc(h_copied, 1)
                    act.sem_inc(yf_done, 1)
                    act.sem_inc(turned, 1)

                    def gathered(j):
                        for q in range(2):
                            act.wait_ge(xg_filled, lin(q + 1, (j, 2)))
                            A(xh[:, 4 * q:4 * q + 4, 0:BLK], ps[:, 6 + q, :].rearrange("p (k t) -> p k t", k=4),
                              ACT.Copy).then_inc(xg_hi, 1)
                    gathered(0)
                    act.wait_ge(jobs_ready, 1)
                    n_jobs = act.value_load(ji[0:1, JOBS:JOBS + 1], min_val=EXPERTS, max_val=JOBS - 1)
                    gu, dn = PH["gu1"], PH["dn1"]
                    with act.Fori(0, n_jobs) as j:
                        one = job_unit(gu, nl[0], j)

                        def middle():
                            act.wait_ge(gt_filled, j + 1)
                            A(gt[:], ps[:, 6, 0:S], ACT.Copy)
                            A(WS, ps[:, 6, S:S + 1], ACT.Copy).then_inc(gt_copied, 1)
                        job_units(act, gu, one, middle)
                        gathered(j + 1)
                        upper(FT // 2 - 1, 0, j)
                        run_units(act, dn, lambda b, s: split_ahead(dn, b, s, j))
                        act.wait_ge(consumed, unit_no(dn, 0, dn.n, j, 2))
                        act.wait_ge(gt_copied, j + 1)
                        A(YF.rearrange("p (h c) -> p h c", h=2), ps[:, 4:6, :], ACT.Copy, scale=WS).then_inc(yf_done, 1)
                        act.wait_ge(yf_done, j + 2)
                        A(xh[:, :, BLK:2 * BLK], YF.rearrange("p (m c) -> p m c", m=KT), ACT.Copy).then_inc(y_hi, 1)
                    layer_norm(x[:])

        @block.gpsimd
        def _(pool):
            steps = [0]

            def link(ins):
                steps[0] += 1
                ins.then_inc(pstep, 1)
                pool.wait_ge(pstep, steps[0])

            T2 = nc.gpsimd.tensor_tensor

            def rope_cos(ntiles, k0, act_total):
                pool.wait_ge(drained_act, act_total)
                for i in range(ntiles // 2):
                    if i >= 2:
                        pool.wait_ge(roped, k0 + i - 1)
                    T2(RC[:, i % 2, :].rearrange("p (a t) -> p a t", a=2), QK[:, 2 * i:2 * i + 2, :],
                       COSA.unsqueeze(1).broadcast_to([P, 2, S]), ALU.mult).then_inc(cos_done, 1)

            pool.wait_ge(blocka_in, 16)
            rope_cos(16, 0, PH["av"].da0)
            rope_cos(12, 8, PH["bv"].da0)
            pool.wait_ge(trig_done, 1)
            for l in range(2):
                pool.wait_ge(drained_act, PH[f"pv{l}"].da0)
                pool.wait_ge(moving, 1 + 4 * (7 + 4 * l) - 1)
                cosb = cosr[:].unsqueeze(1).broadcast_to([P, 4, S])
                sinb = sinr[:].unsqueeze(1).broadcast_to([P, 4, S])
                t1, t2 = SRC[:, 0:4, :], SRC[:, 4:8, :]
                for q in (RQ, RK):
                    v = q.rearrange("p (h a) t -> p a h t", a=2)
                    x1, x2 = v[:, 0], v[:, 1]
                    T2(t1, x1, sinb, ALU.mult)
                    link(T2(t2, x2, sinb, ALU.mult))
                    T2(x1, x1, cosb, ALU.mult)
                    link(T2(x2, x2, cosb, ALU.mult))
                    T2(x1, x1, t2, ALU.subtract)
                    ins = T2(x2, x2, t1, ALU.add)
                    if q is RQ:
                        link(ins)
                    else:
                        ins.then_inc(ret_roped, 1)

        @block.vector
        def _(dve):
            V = nc.vector
            steps = [0]

            def link(ins):
                steps[0] += 1
                ins.then_inc(vstep, 1)
                dve.wait_ge(vstep, steps[0])

            def split(ph, b, s, e=0):
                r = raw[:, s, :].rearrange("p (h c) -> p h c", h=2)
                hi = wh[:, s % 2, :].rearrange("p (h c) -> p h c", h=2)
                o = wl[:, s % 2, :].rearrange("p (h c) -> p h c", h=2)
                for half in range(2):
                    dve.wait_ge(hi_split, unit_no(ph, b, s, e, 2, half + 1))
                    V.tensor_tensor(o[:, half], r[:, half], hi[:, half].bitcast(F32),
                                    ALU.subtract).then_inc(lo_split, 1)

            def split_ahead(ph, b, s, e=0):
                split(*ahead_of(ph, b, s, e))

            def filled(ph, b, s, e=0):
                dve.wait_ge(consumed, unit_no(ph, b, s, e, 2, 2))

            def columns(name, drain=None, extra=None):
                ph = PH[name]
                if drain is not None and ph.da0 > 4:
                    dve.wait_ge(drained_act, ph.da0)

                def one(b, s):
                    split_ahead(ph, b, s)
                    if drain is not None:
                        filled(ph, b, s)
                        drain(b, s, ps[:, s, :]).then_inc(drained_dve, 1)
                    if extra is not None:
                        extra(lin(s, (b, RAWS)))
                run_units(dve, ph, one)

            def rows(name, drain):
                ph = PH[name]
                run_units(dve, ph, lambda b, s: split_ahead(ph, b, s))
                dve.wait_ge(consumed, 2 * (ph.g0 + ph.n))
                for bank in range(8):
                    drain(ROW_M[bank], ps[:, bank, 0:S]).then_inc(drained_dve, 1)

            splits = [0]

            def rest_chunk(src, c):
                splits[0] += 1
                dve.wait_ge(xh_ready, splits[0])
                v = slice(2 * c, 2 * c + 2)
                V.tensor_tensor(xl[:, v, :], src[:, v, :], xh[:, v, :].bitcast(F32), ALU.subtract).then_inc(moving, 1)

            def rest_of(src, tiles=KT):
                for c in range(tiles // 2):
                    rest_chunk(src, c)

            lns = [0]

            def normed(src):
                n = lns[0]
                lns[0] += 1
                dve.wait_ge(ln_mean, n + 1)
                for c in range(4):
                    v = src[:, 2 * c:2 * c + 2, :]
                    V.tensor_tensor(v, v, ps[:, 4, 0:S].unsqueeze(1).broadcast_to([P, 2, S]),
                                    ALU.subtract).then_inc(ln_cen, 1)
                dve.wait_ge(ln_std, n + 1)
                link(V.reciprocal(rstd[:], std[:]))

            def layer_norm(g, b):
                normed(x[:])
                for c in range(5):
                    if c < 4:
                        for j in (2 * c, 2 * c + 1):
                            last = V.scalar_tensor_tensor(x[:, j, :], x[:, j, :], col(g, j), rstd[:], ALU.mult, ALU.mult)
                        link(last)
                        for j in (2 * c, 2 * c + 1):
                            last = V.tensor_scalar(x[:, j, :], x[:, j, :], col(b, j), None, ALU.add)
                        last.then_inc(src_ready, 1)
                    if c > 0:
                        rest_chunk(x, c - 1)

            def layer_norm_modulated(g, b, l, which):
                o = 24 * which
                link(V.tensor_tensor(bs[:], col(b, 0, KT), ada[:, l, o + 8:o + 16], ALU.mult))
                link(V.tensor_tensor(bs[:], bs[:], ada[:, l, o:o + 8], ALU.add))
                normed(x[:])
                for c in range(5):
                    if c < 4:
                        for j in (2 * c, 2 * c + 1):
                            last = V.scalar_tensor_tensor(x[:, j, :], x[:, j, :], col(g, j), rstd[:], ALU.mult, ALU.mult)
                        link(last)
                        for j in (2 * c, 2 * c + 1):
                            last = V.tensor_scalar(SRC[:, j, :], x[:, j, :], ada[:, l, o + 8 + j:o + 9 + j],
                                                   bs[:, j:j + 1], ALU.mult, ALU.add)
                        last.then_inc(src_ready, 1)
                    if c > 0:
                        rest_chunk(SRC, c - 1)
                for j in range(KT):
                    last = V.tensor_scalar(x[:, j, :], x[:, j, :], col(b, j), None, ALU.add)
                return last

            nl = [0, 4]

            def relu_phase(name):
                ph, n0, h0 = PH[name], nl[0], nl[1]
                nl[0] += ph.n
                nl[1] += ph.n

                def one(b, s):
                    split_ahead(ph, b, s)
                    i = lin(s, (b, RAWS))
                    dve.wait_ge(nonlin, lin(h0 + s + 1, (b, RAWS)))
                    if n0 or s or b:
                        dve.wait_ge(hidden_ready, lin(n0 + s, (b, RAWS)))
                    V.tensor_tensor(HF, SG, SG, ALU.mult).then_inc(hf_ready, 1)
                    dve.wait_ge(mh_ready, lin(n0 + s + 1, (b, RAWS)))
                    V.tensor_tensor(pair(ml, i), HF, pair(mh, i).bitcast(F32), ALU.subtract).then_inc(hidden_ready, 1)
                run_units(dve, ph, one)

            def pair(t, i):
                return t[:, :, :].rearrange("p (i a) t -> p i (a t)", a=2)[:, i]

            def gate_unit(ph, n0):
                def one(b, s):
                    split_ahead(ph, b, s)
                    if s % 2 == 1:
                        filled(ph, b, s)
                        dve.wait_ge(drained_act, lin(ph.da0 + s // 2 + 1, (b, 2)))
                        dve.wait_ge(hidden_ready, lin(n0 + s // 2, (b, 2)))
                        V.tensor_tensor(HF, SG, ps[:, s, :], ALU.mult).then_inc(hf_ready, 1)
                        dve.wait_ge(mh_ready, lin(n0 + s // 2 + 1, (b, 2)))
                        i = lin(s // 2, (b, 2))
                        V.tensor_tensor(pair(ml, i), HF, pair(mh, i).bitcast(F32),
                                        ALU.subtract).then_inc(hidden_ready, 1)
                        V.sem_inc(drained_dve, 1)
                return one

            def job_unit(ph, n0, j):
                def one(b, s):
                    split_ahead(ph, b, s, j)
                    if s % 2 == 0:
                        return
                    first = isinstance(b, int) and b == 0 and s == 1
                    if not first:
                        rest(lin(s // 2 - 1, (b, 2)), (s // 2 + 1) % 2, n0, j)
                    filled(ph, b, s, j)
                    dve.wait_ge(drained_act, lin(ph.da0 + s // 2 + 1, (b, 2), (j, ph.da_e)))
                    dve.wait_ge(turned, lin(1 if first else s // 2, (b, 2), (j, 11)))
                    V.tensor_tensor(HF2[:, s // 2, :], SG[:, 0:256], ps[:, s, 0:256], ALU.mult).then_inc(hf_ready, 1)
                    dve.wait_ge(hf_ready, lin(n0 + s // 2 + 1, (b, 2), (j, 11)))
                    V.sem_inc(drained_dve, 1)
                return one

            def rest(i, parity, n0, j):
                dve.wait_ge(mh_ready, lin(n0 + i + 1, (j, 11)))
                V.tensor_tensor(pair(jml, i), ps[:, 4 + parity, 0:256], pair(jmh, i).bitcast(F32),
                                ALU.subtract).then_inc(hidden_ready, 1)

            dve.wait_ge(c_act, 2)
            V.tensor_tensor(CL, cf[:].unsqueeze(2).broadcast_to([P, KT, P]), CH.bitcast(F32),
                            ALU.subtract).then_inc(moving, 1)
            dve.wait_ge(consts_in, 16)
            split(PH["ada0"], 0, 0)
            split(PH["ada0"], 0, 1)
            for l in range(2):
                def ada_out(b, s, bank):
                    return V.tensor_tensor(DG[:, lin(s, (b, RAWS))], bank[:, 0:2 * P].rearrange("p (m c) -> p m c", m=2),
                                           ident.unsqueeze(1).broadcast_to([P, 2, P]), ALU.mult)
                columns(f"ada{l}", ada_out)
                dve.wait_ge(drained_dve, PH[f"ada{l}"].next.dd0)
                link(V.tensor_reduce(ada[:, l, :], DG.rearrange("p i m c -> p (i m) c"), AX.X, ALU.add))
            for l in range(2):
                link(V.tensor_tensor(ada[:, l, :], ada[:, l, :], pr[:, PCOL[f"bada_{l}"]:PCOL[f"bada_{l}"] + 48], ALU.add))
                for o in (8, 32):
                    link(V.tensor_scalar(ada[:, l, o:o + 8], ada[:, l, o:o + 8], 1.0, None, ALU.add))
            dve.wait_ge(pos_in, 16)
            link(V.tensor_copy(cosr[:], pos[:]))
            link(V.tensor_scalar(cosr[:], cosr[:], col("invf"), None, ALU.mult))
            two_pi = 2 * np.pi
            parts, left = [], two_pi
            for bits in (2 ** 5, 2 ** 13, 2 ** 21):
                v = float(np.floor(left * bits) / bits)
                parts.append(v)
                left -= v
            parts.append(float(left))
            magic = float(1.5 * 2 ** 23)
            for dst, shift in ((std, 0.25), (rstd, 0.0)):
                link(V.tensor_scalar(sinr[:], cosr[:], float(1 / two_pi), shift, ALU.mult, ALU.add))
                link(V.tensor_scalar(sinr[:], sinr[:], magic, None, ALU.add))
                link(V.tensor_scalar(sinr[:], sinr[:], -magic, None, ALU.add))
                link(V.scalar_tensor_tensor(dst[:], sinr[:], -parts[0], cosr[:], ALU.mult, ALU.add))
                for v in parts[1:]:
                    link(V.scalar_tensor_tensor(dst[:], sinr[:], -v, dst[:], ALU.mult, ALU.add))
                if shift:
                    link(V.tensor_scalar(dst[:], dst[:], float(np.pi / 2), None, ALU.add))
                link(V.tensor_scalar(dst[:], dst[:], 3.1415925, -3.1415925, ALU.min, ALU.max))
            V.sem_inc(trig_arg, 1)

            def rope(ntiles, k0):
                for i in range(ntiles // 2):
                    dve.wait_ge(swapped, k0 + i + 1)
                    if k0 + i:
                        dve.wait_ge(roped, k0 + i)
                    link(V.tensor_tensor(RT.rearrange("p (a t) -> p a t", a=2),
                                         ps[:, i % 8, :].rearrange("p (a t) -> p a t", a=2),
                                         SINA.unsqueeze(1).broadcast_to([P, 2, S]), ALU.mult))
                    dve.wait_ge(cos_done, k0 + i + 1)
                    V.tensor_tensor(QK[:, 2 * i:2 * i + 2, :].rearrange("p a t -> p (a t)"), RC[:, i % 2, :], RT,
                                    ALU.add).then_inc(roped, 1)

            def attention(groups, heads_of, masks, g0):
                G = len(masks)
                for i in range(groups):
                    dve.wait_ge(qk_done, g0 + i + 1)
                    if g0 + i:
                        dve.wait_ge(pt_done, g0 + i)
                    link(V.tensor_tensor(SS[:, 0:G, :], ps[:, 0:G, 0:TRI], MASK[:, masks[0]:masks[0] + G, :], ALU.add))
                    V.sem_inc(masked, 1)
                    V.tensor_reduce(st[:, 2:3], SS[:, 0:G, 0:128], AX.XY, ALU.max)
                    link(V.tensor_reduce(st[:, 3:4], SS[:, 0:G, 128:384], AX.XY, ALU.max))
                    V.tensor_scalar(st[:, 0:2], st[:, 2:4], -QSCALE, None, ALU.mult).then_inc(mx_ready, 1)
                    dve.wait_ge(exp_done, g0 + i + 1)
                    link(V.reciprocal(st[:, 6:8], st[:, 4:6]))
                    V.tensor_scalar(SS[:, 0:G, 0:128], SS[:, 0:G, 0:128], st[:, 6:7], None, ALU.mult)
                    V.tensor_scalar(SS[:, 0:G, 128:384], SS[:, 0:G, 128:384], st[:, 7:8], None,
                                    ALU.mult).then_inc(p_ready, 1)

            def add_residual(b, s, bank):
                xv = x[:].rearrange("p (i a) t -> p i (a t)", a=2)[:, lin(s, (b, RAWS))]
                return V.scalar_tensor_tensor(xv, xv, ALPHA, bank, ALU.mult, ALU.add)

            def first_half(m, bank):
                return V.scalar_tensor_tensor(x[:, m, :], x[:, m, :], ALPHA, bank, ALU.mult, ALU.add)

            def second_half(m, bank):
                return V.tensor_tensor(x[:, m, :], x[:, m, :], bank, ALU.add)

            dve.wait_ge(x_in, 16)
            V.sem_inc(src_ready, 4)
            rest_of(x)
            columns("aqk")
            columns("av")
            rope(16, 0)
            attention(16, lambda i: [i], [0], 0)
            rest_of(SRC)
            columns("ao", add_residual)
            layer_norm("lnA0g", "lnA0b")
            relu_phase("ain0")
            rows("aout0", first_half)
            relu_phase("ain1")
            dve.wait_ge(drained_dve, PH["ain1"].dd0)
            rows("aout1", second_half)
            layer_norm("lnA1g", "lnA1b")
            columns("bqk")
            columns("bv")
            rope(12, 8)
            attention(4, None, [1, 2, 3], 16)
            rest_of(SRC, 6)
            rows("bo", first_half)
            layer_norm("lnA2g", "lnA2b")
            relu_phase("bin0")
            rows("bout0", first_half)
            relu_phase("bin1")
            rows("bout1", second_half)
            layer_norm_modulated("lnA3g", "lnA3b", 0, 0)

            taps = [0]
            for l in range(2):
                V.memset(U[:, :, 0:TAPS - 1], 0.0)
                columns(f"pb{l}")

                def gated(b, s, bank):
                    i = lin(s, (b, RAWS))
                    cv = CV.rearrange("p (i a) t -> p i a t", a=2)[:, i]
                    uv = U.rearrange("p (i a) t -> p i a t", a=2)[:, i]
                    return V.tensor_tensor(uv[:, :, TAPS - 1:PADW], cv, bank.rearrange("p (a t) -> p a t", a=2),
                                           ALU.mult)
                columns(f"pa{l}", gated)
                wv = pr[:, PCOL[f"wdw_{l}"]:PCOL[f"wdw_{l}"] + KT * TAPS].rearrange("p (j k) -> p k j", k=TAPS)
                base = taps[0]

                def tap(i, wv=wv, base=base, l=l):
                    for j in range(KT):
                        if isinstance(i, int) and i == 0:
                            ins = V.tensor_scalar(CV[:, j, :], U[:, j, 0:S], wv[:, 0, j:j + 1], col(f"bdw_{l}", j),
                                                  ALU.mult, ALU.add)
                        else:
                            dve.wait_ge(tap_done, lin(base + j + 1 - KT, (i, KT)))
                            ins = V.scalar_tensor_tensor(CV[:, j, :], U[:, j, bass.ds(i, S)],
                                                         wv[:, i, j:j + 1], CV[:, j, :], ALU.mult, ALU.add)
                        ins.then_inc(tap_done, 1)
                dve.wait_ge(drained_dve, PH[f"pqk{l}"].dd0)
                tap(0)
                off = 1
                for nm in (f"pqk{l}", f"pv{l}", f"prg{l}", f"pgc{l}"):
                    columns(nm, extra=lambda i, off=off: tap(lin(off, (i, 1))))
                    off += PH[nm].n
                columns(f"pgr{l}")
                tap(29)
                tap(30)
                taps[0] += KT * TAPS
                normed(CV)
                for c in range(4):
                    v = CV[:, 2 * c:2 * c + 2, :]
                    V.tensor_tensor(v, v, rstd[:].unsqueeze(1).broadcast_to([P, 2, S]), ALU.mult).then_inc(u_ready, 1)
                rest_of(SRC)
                dve.wait_ge(decay_in, 16 * (l + 1))
                for h in range(RET_HEADS):
                    dve.wait_ge(st_done, 4 * l + h + 1)
                    if h >= 2:
                        dve.wait_ge(o_done, 8 * l + 2 * (h - 1))
                    V.tensor_tensor(RST[:, h % 2, :], ps[:, h % 2, 0:TRI], DEC[:, h, :], ALU.mult).then_inc(st_decayed, 1)
                sv = st[:, 16:64].rearrange("p (i c) -> p i c", c=6)
                mv = st[:, 64:80].rearrange("p (i c) -> p i c", c=2)
                for i in range(8):
                    dve.wait_ge(o_copied, 8 * l + i + 1)
                    link(V.bn_stats(sv[:, i], ON[:, i // 2, i % 2, :]))
                for i in range(8):
                    last = V.bn_aggr(mv[:, i], sv[:, i])
                last.then_inc(ovar, 1)
                dve.wait_ge(ostd, l + 1)
                link(V.reciprocal(st[:, 88:96], st[:, 80:88]))
                for i in range(8):
                    V.tensor_scalar(ON[:, i // 2, i % 2, :], ON[:, i // 2, i % 2, :], mv[:, i, 0:1],
                                    st[:, 88 + i:89 + i], ALU.subtract, ALU.mult).then_inc(o_normed, 1)
                for i in range(8):
                    dve.wait_ge(g_turned, 8 * l + i + 1)
                    rg = RG[:, 2 * i:2 * i + 2, :].rearrange("p a t -> p (a t)")
                    V.tensor_tensor(rg, rg, ps[:, i, :], ALU.mult).then_inc(hf_ready, 1)
                for i in range(8):
                    dve.wait_ge(mh_ready, nl[0] + i + 1)
                    V.tensor_tensor(ml[:, 2 * i:2 * i + 2, :], RG[:, 2 * i:2 * i + 2, :],
                                    mh[:, 2 * i:2 * i + 2, :].bitcast(F32), ALU.subtract).then_inc(hidden_ready, 1)
                nl[0] += 8

                def conv_gate(b, s, bank):
                    v = GC.rearrange("p (i a) t -> p i (a t)", a=2)[:, lin(s, (b, RAWS))]
                    return V.tensor_tensor(v, v, bank, ALU.mult)
                columns(f"co{l}", conv_gate)
                rows(f"ro{l}", lambda m, bank: V.tensor_tensor(GR[:, m, :], GR[:, m, :], bank, ALU.mult))
                dve.wait_ge(drained_dve, PH[f"wo{l}"].dd0)
                for c in range(5):
                    if c < 4:
                        v = slice(2 * c, 2 * c + 2)
                        V.tensor_tensor(SRC[:, v, :], GR[:, v, :], GC[:, v, :], ALU.add).then_inc(src_ready, 1)
                    if c > 0:
                        rest_chunk(SRC, c - 1)
                link(V.tensor_scalar(x[:], x[:], ALPHA, None, ALU.mult))

                def gated_add(which):
                    def go(m, bank):
                        g = ada[:, l, 24 * which + 16 + m:24 * which + 17 + m]
                        return V.scalar_tensor_tensor(x[:, m, :], bank, g, x[:, m, :], ALU.mult, ALU.add)
                    return go

                def mix_out(b, s, bank, l=l):
                    i = lin(s, (b, RAWS))
                    for a in range(2):
                        last = gated_add(0)(2 * i + a, bank[:, a * S:a * S + S])
                    return last
                columns(f"wo{l}", mix_out)
                x_done = layer_norm_modulated(f"ln1_{l}g", f"ln1_{l}b", l, 1)
                link(x_done)
                if l == 0:
                    run_units(dve, PH["gu0"], gate_unit(PH["gu0"], nl[0]))
                    nl[0] += 11
                    link(V.tensor_scalar(x[:], x[:], ALPHA, None, ALU.mult))
                    rows("dn0", gated_add(1))
                    layer_norm_modulated("ln2_0g", "ln2_0b", 1, 0)
                    continue
                dve.wait_ge(logits, 1)
                link(V.tensor_copy(LG, ps[:, 6, 0:16].rearrange("p (t e) -> p t e", t=2)))
                mx = st[:, 0:16].rearrange("p (t c) -> p t c", t=2)
                ixf = st[:, 16:32].rearrange("p (t c) -> p t c", t=2)
                for t in range(TT):
                    link(V.max(mx[:, t], LG[:, t]))
                    link(V.max_index(ix[:, 8 * t:8 * t + 8], mx[:, t], LG[:, t]))
                link(V.tensor_copy(st[:, 16:32], ix[:]))
                V.tensor_tensor(st[:, 32:34], mx[:, :, 1], mx[:, :, 0], ALU.subtract).then_inc(gap_ready, 1)
                dve.wait_ge(gap_exp, 1)
                link(V.tensor_scalar(st[:, 36:38], st[:, 34:36], 1.0, None, ALU.add))
                link(V.reciprocal(st[:, 38:40], st[:, 36:38]))
                link(V.tensor_tensor(st[:, 40:42], st[:, 38:40], st[:, 34:36], ALU.mult))
                i8, i16 = col("iota", 0, EXPERTS), col("iota", 0, JOBS)
                for t in range(TT):
                    V.tensor_scalar(SEL[:, t], i8, ixf[:, t, 0:1], None, ALU.is_equal)
                    V.tensor_scalar(SEL2[:, t], i8, ixf[:, t, 1:2], None, ALU.is_equal)
                    V.tensor_scalar(CMB[:, t], i8, ixf[:, t, 0:1], st[:, 38 + t:39 + t], ALU.is_equal, ALU.mult)
                    link(V.tensor_scalar(CMB2[:, t], i8, ixf[:, t, 1:2], st[:, 40 + t:41 + t], ALU.is_equal, ALU.mult))
                V.tensor_tensor(SEL, SEL, SEL2, ALU.add).then_inc(sel_ready, 1)
                V.tensor_tensor(CMB, CMB, CMB2, ALU.add)
                link(V.memset(CUM, 0.0))
                dve.wait_ge(ranked, 1)
                link(V.tensor_scalar(POS, ps[:, 5, 0:16].rearrange("p (t e) -> p t e", t=2), float(D), 1000.0,
                                     ALU.mult, ALU.add))
                link(V.tensor_tensor(POS, POS, SEL, ALU.mult))
                V.tensor_scalar(POS, POS, -1000.0, None, ALU.add)
                link(V.tensor_scalar(CNT, ps[:, 5, 16:24], float(BLK) / D, 1.0, ALU.is_gt, ALU.add))
                link(V.tensor_copy(CUM[:, 0, 4:12], CNT))
                for i, d in enumerate((1, 2, 4)):
                    link(V.tensor_tensor(CUM[:, i + 1, 4:12], CUM[:, i, 4:12], CUM[:, i, 4 - d:12 - d], ALU.add))
                cum = CUM[:, 3, 4:12]
                for e in range(EXPERTS):
                    V.tensor_scalar(MJ[:, 0, e], i16, cum[:, e:e + 1], None, ALU.is_ge)
                    last = V.tensor_scalar(MJ[:, 1, e], i16, cum[:, e:e + 1], CNT[:, e:e + 1], ALU.is_ge, ALU.mult)
                link(last)
                V.tensor_reduce(EXPJ, MJ[:, 0].rearrange("p e j -> p j e"), AX.X, ALU.add)
                link(V.tensor_reduce(STARTJ, MJ[:, 1].rearrange("p e j -> p j e"), AX.X, ALU.add))
                V.tensor_copy(ji[:, JOBS:JOBS + 1], cum[:, 7:8])
                V.tensor_copy(ji[:, 0:JOBS], EXPJ).then_inc(jobs_ready, 1)
                link(V.tensor_tensor(STARTJ, i16, STARTJ, ALU.subtract))
                for e in range(EXPERTS):
                    for t in range(TT):
                        V.tensor_scalar(MJ[:, t, e], EXPJ, float(e), POS[:, t, e:e + 1], ALU.is_equal, ALU.mult)
                        last = V.tensor_scalar(MJ[:, 2 + t, e], EXPJ, float(e), CMB[:, t, e:e + 1], ALU.is_equal, ALU.mult)
                link(last)
                V.tensor_reduce(PJ, MJ[:, 0:2].rearrange("p t e j -> p t j e"), AX.X, ALU.add)
                link(V.tensor_reduce(CJ, MJ[:, 2:4].rearrange("p t e j -> p t j e"), AX.X, ALU.add))
                for t in range(TT):
                    last = V.scalar_tensor_tensor(PJ[:, t], STARTJ, -float(BLK), PJ[:, t], ALU.mult, ALU.add)
                link(last)
                def gather_matrix(j):
                    for t in range(TT):
                        last = V.tensor_scalar(gx[:, t, :], col("iota", 0, BLK), PJ[:, t, bass.ds(j, 1)], None,
                                               ALU.is_equal)
                    last.then_inc(g_ready, 1)

                def gathered(j):
                    for q in range(2):
                        dve.wait_ge(xg_hi, lin(q + 1, (j, 2)))
                        V.tensor_tensor(xl[:, 4 * q:4 * q + 4, 0:BLK],
                                        ps[:, 6 + q, :].rearrange("p (k t) -> p k t", k=4),
                                        xh[:, 4 * q:4 * q + 4, 0:BLK].bitcast(F32), ALU.subtract).then_inc(xg_lo, 1)

                def add_scattered(j):
                    av = ACC.rearrange("p (q a) t -> p q (a t)", a=2)
                    for q in range(4):
                        dve.wait_ge(sc_filled, lin(q + 1, (j, 4)))
                        V.tensor_tensor(av[:, q], av[:, q], ps[:, 6 + q % 2, :], ALU.add).then_inc(sc_added, 1)
                gather_matrix(0)
                V.memset(ACC, 0.0)
                V.memset(gt[:].bitcast(F32), 0.0)
                V.memset(xh[:, :, BLK:2 * BLK].bitcast(F32), 0.0)
                V.memset(xl[:, :, BLK:2 * BLK].bitcast(F32), 0.0).then_inc(y_split, 1)
                gathered(0)
                n0 = nl[0]
                n_jobs = dve.value_load(ji[0:1, JOBS:JOBS + 1], min_val=EXPERTS, max_val=JOBS - 1)
                gu, dn = PH["gu1"], PH["dn1"]
                with dve.Fori(0, n_jobs) as j:
                    one = job_unit(gu, n0, j)

                    def middle():
                        add_scattered(j)
                        dve.wait_ge(gt_filled, j + 1)
                        gather_matrix(j + 1)
                    job_units(dve, gu, one, middle)
                    gathered(j + 1)
                    rest(FT // 2 - 1, 0, n0, j)
                    run_units(dve, dn, lambda b, s: split_ahead(dn, b, s, j))
                    dve.wait_ge(y_hi, j + 1)
                    V.tensor_tensor(xl[:, :, BLK:2 * BLK], YF.rearrange("p (m c) -> p m c", m=KT),
                                    xh[:, :, BLK:2 * BLK].bitcast(F32), ALU.subtract).then_inc(y_split, 1)
                add_scattered(n_jobs)
                dve.wait_ge(sc_added, n_jobs * 4 + 4)
                link(V.tensor_scalar(x[:], x[:], ALPHA, None, ALU.mult))
                for m in range(KT):
                    last = gated_add(1)(m, ACC[:, m, :])
                last.then_inc(ln_in, 1)
                normed(x[:])
                for j in range(KT):
                    last = V.scalar_tensor_tensor(x[:, j, :], x[:, j, :], col("ln2_1g", j), rstd[:], ALU.mult, ALU.mult)
                link(last)
                for j in range(KT):
                    last = V.tensor_scalar(x[:, j, :], x[:, j, :], col("ln2_1b", j), None, ALU.add)
                last.then_inc(final, 1)

        @block.tensor
        def _(pe):
            mm = nc.tensor.matmul

            def three(out, w, m, start, stop):
                (w_h, w_l), (m_h, m_l) = w, m
                mm(out, w_l, m_h, start=start, stop=False)
                mm(out, w_h, m_l, start=False, stop=False)
                return mm(out, w_h, m_h, start=False, stop=stop)

            def split_ready(ph, b, s, half, e):
                pe.wait_ge(lo_split, unit_no(ph, b, s, e, 2, half + 1))

            def columns(ph, kind, bank_free, e=0, moving_op=None, middle=None, after=None, tiles=TT):
                mhh, mll = moving_op or (xh, xl)

                def one(b, s):
                    bank_free(b, s)
                    if kind == "N":
                        w_h = wh[:, s % 2, :].rearrange("p (k c) -> p k c", k=KT)
                        w_l = wl[:, s % 2, :].rearrange("p (k c) -> p k c", k=KT)
                        for t in range(tiles):
                            for k in range(KT):
                                if t == 0 and k % 4 == 0:
                                    split_ready(ph, b, s, k // 4, e)
                                tok = slice(t * P, t * P + P)
                                o = ps[:, s, t * 256:t * 256 + 256]
                                mm(o, mll[:, k, tok], w_h[:, k, :], start=k == 0, stop=False)
                                mm(o, mhh[:, k, tok], w_l[:, k, :], start=False, stop=False)
                                last = mm(o, mhh[:, k, tok], w_h[:, k, :], start=False, stop=k == KT - 1)
                                if t == tiles - 1 and k % 4 == 3:
                                    last.then_inc(consumed, 1)
                        if after is not None:
                            after(b, s)
                        return
                    w_h = wh[:, s % 2, :].rearrange("p (m k c) -> p m k c", m=2, k=KT)
                    w_l = wl[:, s % 2, :].rearrange("p (m k c) -> p m k c", m=2, k=KT)
                    split_ready(ph, b, s, 0, e)
                    n = mhh.shape[2]
                    for m in range(2):
                        if m:
                            split_ready(ph, b, s, 1, e)
                        for k in range(KT):
                            last = three(ps[:, s, m * n:m * n + n], (w_h[:, m, k, :], w_l[:, m, k, :]),
                                         (mhh[:, k, 0:n], mll[:, k, 0:n]), k == 0, k == KT - 1)
                        last.then_inc(consumed, 1)
                if middle is not None:
                    job_units(pe, ph, one, middle)
                else:
                    run_units(pe, ph, one, 0)

            def rows(ph, need, e=0, hidden=True, bank_free=None):
                mhh, mll = (mh, ml) if hidden else (xh, xl)
                last_unit = ph.n - 1

                def one(b, s):
                    w_h = wh[:, s % 2, :].rearrange("p (k m c) -> p k m c", k=2, m=KT)
                    w_l = wl[:, s % 2, :].rearrange("p (k m c) -> p k m c", k=2, m=KT)
                    need(b, s)
                    for kk in range(2):
                        split_ready(ph, b, s, kk, e)
                        kt = lin(2 * s + kk, (b, 2 * RAWS))
                        st0 = isinstance(b, int) and b == 0 and s == 0 and kk == 0
                        sp0 = isinstance(b, int) and RAWS * b + s == last_unit and kk == 1
                        for m in range(KT):
                            bank = ROW_M.index(m)
                            if st0 and bank_free is not None and bank < 4:
                                bank_free(bank)
                            last = three(ps[:, bank, 0:S], (w_h[:, kk, m, :], w_l[:, kk, m, :]),
                                         (mhh[:, kt, :], mll[:, kt, :]), st0, sp0)
                        last.then_inc(consumed, 1)
                for i in range(ph.n):
                    one(i // RAWS, i % RAWS)

            def by_act(ph, before=None):
                def go(b, s):
                    if not isinstance(b, int) or b == 0:
                        if before == "dve":
                            pe.wait_ge(drained_dve, ph.dd0 + s - 3)
                    pe.wait_ge(drained_act, lin(ph.da0 + s - 3, (b, RAWS)))
                return go

            def by_dve(ph, before=None):
                def go(b, s):
                    if not isinstance(b, int) or b == 0:
                        if before == "act":
                            pe.wait_ge(drained_act, ph.da0 + s - 3)
                    pe.wait_ge(drained_dve, lin(ph.dd0 + s - 3, (b, RAWS)))
                return go

            def all_free(ph, e=0):
                pe.wait_ge(drained_act, lin(ph.da0, (e, ph.da_e)))
                pe.wait_ge(drained_dve, lin(ph.dd0, (e, ph.dd_e)))

            def proj(name, by, kind="T", before=None):
                ph = PH[name]
                if before is None:
                    all_free(ph)
                columns(ph, kind, by(ph, before))

            hid = [0]

            def relu_phase(name, after_rows=False):
                ph = PH[name]
                if not after_rows:
                    all_free(ph)
                h0 = hid[0]
                hid[0] += ph.n

                def bank(b, s):
                    if after_rows and (not isinstance(b, int) or b == 0):
                        pe.wait_ge(drained_dve, ph.dd0 - 8 + s + 1)
                    if not isinstance(b, int) or b > 0:
                        pe.wait_ge(nonlin, lin(nls[0] + s - 3, (b, RAWS)))
                columns(ph, "T", bank)
                nls[0] += ph.n
                return h0

            nls = [4]

            def out_phase(name, h0):
                ph = PH[name]
                pe.wait_ge(drained_dve, ph.dd0)
                rows(ph, lambda b, s: pe.wait_ge(hidden_ready, lin(h0 + s + 1, (b, RAWS))),
                     bank_free=lambda bank: pe.wait_ge(nonlin, nls[0] - 3 + bank))

            lns = [0]

            def layer_norm(src, ready, order=range(KT)):
                n = lns[0]
                lns[0] += 1
                for i, k in enumerate(order):
                    ready(i)
                    last = mm(ps[:, 4, 0:S], ones, src[:, k, :], start=i == 0, stop=i == KT - 1)
                last.then_inc(ln_mean, 1)
                for k in range(KT):
                    if k % 2 == 0:
                        pe.wait_ge(ln_sq, 4 * n + k // 2 + 1)
                    last = mm(ps[:, 5, 0:S], ones, SRC[:, k, :], start=k == 0, stop=k == KT - 1)
                last.then_inc(ln_var, 1)

            def after_columns(name):
                d = PH[name].dd0
                return lambda i: pe.wait_ge(drained_dve, d + i // 2 + 1) if i % 2 == 0 else None

            def after_rows(name):
                d = PH[name].dd0
                return lambda i: pe.wait_ge(drained_dve, d + max(i + 1, 6))

            def dve_after(name):
                return PH[name].dd0 + PH[name].dve_drains

            mv = [1]

            def moving_ready(tiles=KT):
                mv[0] += tiles // 2
                pe.wait_ge(moving, mv[0])

            def rope(ntiles, k0):
                pe.wait_ge(drained_act, PH["ao"].da0 if k0 == 0 else PH["bo"].da0)
                for i in range(ntiles // 2):
                    mm(ps[:, i % 8, :], swap, QK[:, 2 * i:2 * i + 2, :].rearrange("p a t -> p (a t)"),
                       start=True, stop=True).then_inc(swapped, 1)

            def attention(groups, heads_of, g0, h0, ktile0):
                G = len(heads_of(0))
                for i in range(groups):
                    if i:
                        pe.wait_ge(masked, g0 + i)
                    for k, h in enumerate(heads_of(i)):
                        r = slice(64 * (h % 2), 64 * (h % 2) + 64)
                        q, kk = QK[r, h // 2, :], QK[r, ktile0 + h // 2, :]
                        mm(ps[:, k, 0:128], q[:, 0:128], kk[:, 0:128], start=True, stop=True)
                        last = mm(ps[:, k, 128:384], q[:, 128:256], kk[:, 0:256], start=True, stop=True)
                    last.then_inc(qk_done, 1)
                    pe.wait_ge(p_ready, g0 + i + 1)
                    for k in range(G):
                        for c in range(3):
                            last = nc.tensor.transpose(ps[:, 3 + k, c * P:c * P + P], SS[:, k, c * P:c * P + P], ident)
                    last.then_inc(pt_done, 1)
                    pe.wait_ge(pt_copied, g0 + i + 1)
                    for k, h in enumerate(heads_of(i)):
                        n = h0 + i * G + k
                        if n >= 2:
                            pe.wait_ge(ao_copied, n - 1)
                        r = slice(64 * (h % 2), 64 * (h % 2) + 64)
                        v0, v1 = VN[:, 0, h * 64:h * 64 + 64], VN[:, 1, h * 64:h * 64 + 64]
                        mm(ps[r, 6 + n % 2, 0:128], v0, PT[:, k, 0:128], start=True, stop=True)
                        mm(ps[r, 6 + n % 2, 128:256], v0, PT[:, k, 128:256], start=True, stop=False)
                        mm(ps[r, 6 + n % 2, 128:256], v1, PT[:, k, 256:384], start=False,
                           stop=True).then_inc(pv_done, 1)

            pe.wait_ge(consts_in, 16)
            pe.wait_ge(moving, 1)
            for l in range(2):
                ph = PH[f"ada{l}"]
                all_free(ph)
                columns(ph, "N", by_dve(ph), moving_op=(CH, CL), tiles=1)

            moving_ready()
            proj("aqk", by_act)
            proj("av", by_act, "N", before="act")
            rope(16, 0)
            pe.wait_ge(roped, 8)
            attention(16, lambda i: [i], 0, 0, 8)
            moving_ready()
            proj("ao", by_dve)
            layer_norm(x, after_columns("ao"))
            moving_ready()
            h0 = relu_phase("ain0")
            out_phase("aout0", h0)
            h0 = relu_phase("ain1", True)
            out_phase("aout1", h0)
            layer_norm(x, after_rows("aout1"), ROW_M)
            moving_ready()
            proj("bqk", by_act)
            proj("bv", by_act, "N")
            rope(12, 8)
            pe.wait_ge(roped, 14)
            attention(4, lambda j: [j, 4 + j, 8 + j], 16, 16, 6)
            moving_ready(6)
            ph = PH["bo"]
            all_free(ph)
            rows(ph, lambda b, s: None, hidden=False)
            layer_norm(x, after_rows("bo"), ROW_M)
            moving_ready()
            h0 = relu_phase("bin0")
            out_phase("bout0", h0)
            h0 = relu_phase("bin1", True)
            out_phase("bout1", h0)
            layer_norm(x, after_rows("bout1"), ROW_M)

            for l in range(2):
                moving_ready()
                proj(f"pb{l}", by_act)
                proj(f"pa{l}", by_dve, before="act")
                proj(f"pqk{l}", by_act, before="dve")
                proj(f"pv{l}", by_act, "N", before="act")
                proj(f"prg{l}", by_act, before="act")
                proj(f"pgc{l}", by_act, before="act")
                proj(f"pgr{l}", by_act, before="act")
                pe.wait_ge(drained_act, PH[f"co{l}"].da0)
                layer_norm(CV, lambda i, l=l: pe.wait_ge(tap_done, KT * TAPS * (l + 1) - KT + i + 1))
                pe.wait_ge(ret_roped, l + 1)
                for h in range(RET_HEADS + 1):
                    if h < RET_HEADS:
                        if h >= 2:
                            pe.wait_ge(st_decayed, 4 * l + h - 1)
                        for a in range(2):
                            mm(ps[:, h % 2, 0:256], RK[:, 2 * h + a, 0:128], RQ[:, 2 * h + a, :], start=a == 0, stop=a == 1)
                        for a in range(2):
                            last = mm(ps[:, h % 2, 256:384], RK[:, 2 * h + a, 128:256], RQ[:, 2 * h + a, 128:256],
                                      start=a == 0, stop=a == 1)
                        last.then_inc(st_done, 1)
                    if h >= 1:
                        g = h - 1
                        pe.wait_ge(st_decayed, 4 * l + g + 1)
                        va, vb = (RV[:, t, g * RET_DV:(g + 1) * RET_DV] for t in range(TT))
                        s_ = RST[:, g % 2, :]
                        i = 2 * g
                        if i >= 4:
                            pe.wait_ge(o_copied, 8 * l + i - 3)
                        elif g == 1:
                            pe.wait_ge(ln_std, lns[0])
                        mm(ps[:, 2 + i % 4, :], s_[:, 0:128], va, start=True, stop=True).then_inc(o_done, 1)
                        i += 1
                        if i >= 4:
                            pe.wait_ge(o_copied, 8 * l + i - 3)
                        mm(ps[:, 2 + i % 4, :], s_[:, 128:256], va, start=True, stop=False)
                        mm(ps[:, 2 + i % 4, :], s_[:, 256:384], vb, start=False, stop=True).then_inc(o_done, 1)
                pe.wait_ge(o_copied, 8 * l + 8)
                for i in range(8):
                    h, dd = i // 2, i % 2
                    pe.wait_ge(o_normed, 8 * l + 2 * h + 2)
                    for a in range(2):
                        for t in range(TT):
                            last = nc.tensor.transpose(
                                ps[:, i, a * S + t * P:a * S + t * P + P],
                                ON[:, h, t, (2 * dd + a) * P:(2 * dd + a) * P + P], ident)
                    last.then_inc(g_turned, 1)
                pe.wait_ge(hidden_ready, hid[0] + 8)
                moving_ready()
                proj(f"co{l}", by_dve)
                hid[0] += 8
                rows(PH[f"ro{l}"], lambda b, s: None,
                     bank_free=lambda bank, d=PH[f"ro{l}"].dd0: pe.wait_ge(drained_dve, d - 3 + bank))
                moving_ready()
                proj(f"wo{l}", by_dve)
                layer_norm(x, after_columns(f"wo{l}"))
                moving_ready()

                def gate_banks(ph, e=0):
                    def bank(b, s):
                        if isinstance(b, int) and b == 0:
                            return
                        if s % 2 == 0:
                            pe.wait_ge(drained_act, lin(ph.da0 + s // 2 - 1, (b, 2), (e, ph.da_e)))
                        else:
                            pe.wait_ge(drained_dve, lin(ph.dd0 + s // 2 - 1, (b, 2), (e, ph.dd_e)))
                    return bank

                if l == 0:
                    all_free(PH["gu0"])
                    columns(PH["gu0"], "T", gate_banks(PH["gu0"]))
                    h0 = hid[0]
                    rows(PH["dn0"], lambda b, s: pe.wait_ge(hidden_ready, h0 + RAWS * b + s + 1),
                         bank_free=lambda bank: all_free(PH["dn0"]) if bank == 0 else None)
                    hid[0] += 11
                    layer_norm(x, after_rows("dn0"), ROW_M)
                else:
                    for t in range(TT):
                        for k in range(KT):
                            last = mm(ps[:, 6, 8 * t:8 * t + 8], SRC[:, k, t * P:t * P + P],
                                      pr[:, PCOL["wr"] + 8 * k:PCOL["wr"] + 8 * k + 8], start=k == 0, stop=k == KT - 1)
                    last.then_inc(logits, 1)
                    all_free(PH["gu1"])
                    for i in range(4):
                        for c in range(4):
                            last = nc.tensor.transpose(ps[:, i, c * P:c * P + P],
                                                       SRC[:, i % 2 * 4 + c, i // 2 * P:i // 2 * P + P], ident)
                        last.then_inc(h_turned, 1)
                    tri = cs[:, 3, :]
                    pe.wait_ge(sel_ready, 1)
                    mm(ps[:, 5, 0:8], tri, SEL[:, 0], start=True, stop=True)
                    mm(ps[:, 5, 8:16], ones, SEL[:, 0], start=True, stop=False)
                    mm(ps[:, 5, 8:16], tri, SEL[:, 1], start=False, stop=True)
                    mm(ps[:, 5, 16:24], ones, SEL[:, 0], start=True, stop=False)
                    mm(ps[:, 5, 16:24], ones, SEL[:, 1], start=False, stop=True).then_inc(ranked, 1)

                    def gather(j):
                        pe.wait_ge(g_ready, j + 1)
                        for q in range(2):
                            for a in range(4):
                                f = slice((4 * q + a) * P, (4 * q + a) * P + P)
                                o = ps[:, 6 + q, a * P:a * P + P]
                                mm(o, hn[:, 0, f], gx[:, 0, :], start=True, stop=False)
                                last = mm(o, hn[:, 1, f], gx[:, 1, :], start=False, stop=True)
                            last.then_inc(xg_filled, 1)

                    def turn(i, parity, j):
                        pe.wait_ge(hf_ready, lin(h0 + i + 1, (j, 11)))
                        if isinstance(i, int) and i == 0:
                            pe.wait_ge(yf_done, j + 1)
                        elif not (isinstance(i, int) and i == 1):
                            pe.wait_ge(hidden_ready, lin(h0 + i - 1, (j, 11)))
                        for a in range(2):
                            last = nc.tensor.transpose(ps[:, 4 + parity, a * P:a * P + P],
                                                       HF2[:, parity, a * P:a * P + P], ident)
                        last.then_inc(turned, 1)

                    def scatter(j):
                        pe.wait_ge(y_split, j + 1)
                        for q in range(4):
                            if q >= 2:
                                pe.wait_ge(sc_added, lin(q - 1, (j, 4)))
                            for a in range(2):
                                o = ps[:, 6 + q % 2, a * S:a * S + S]
                                mm(o, xh[:, 2 * q + a, BLK:2 * BLK], gt[:], start=True, stop=False)
                                last = mm(o, xl[:, 2 * q + a, BLK:2 * BLK], gt[:], start=False, stop=True)
                            last.then_inc(sc_filled, 1)

                    h0 = hid[0]
                    pe.wait_ge(h_copied, 4)
                    gather(0)
                    pe.wait_ge(jobs_ready, 1)
                    n_jobs = pe.value_load(ji[0:1, JOBS:JOBS + 1], min_val=EXPERTS, max_val=JOBS - 1)
                    gu, dn = PH["gu1"], PH["dn1"]
                    h0 = hid[0]
                    with pe.Fori(0, n_jobs) as j:
                        pe.wait_ge(xg_hi, lin(2, (j, 2)))
                        pe.wait_ge(xg_lo, lin(2, (j, 2)))

                        def middle():
                            scatter(j)
                            pe.wait_ge(sc_added, lin(3, (j, 4)))
                            for t in range(TT):
                                nc.tensor.transpose(ps[:, 6, t * P:t * P + P], gx[:, t, :], ident)
                            for t in range(TT):
                                last = mm(ps[:, 6, S:S + 1], gx[:, t, :], CJ[:, t, bass.ds(j, 1)],
                                          start=t == 0, stop=t == TT - 1)
                            last.then_inc(gt_filled, 1)

                        def turn_before(b, s):
                            if s % 2 == 0 and not (isinstance(b, int) and b == 0 and s == 0):
                                turn(lin(s // 2 - 1, (b, 2)), (s // 2 + 1) % 2, j)
                        columns(gu, "N", gate_banks(gu, j), j, middle=middle, after=turn_before, tiles=1)
                        pe.wait_ge(gt_copied, j + 1)
                        pe.wait_ge(sc_added, lin(4, (j, 4)))
                        gather(j + 1)
                        turn(FT // 2 - 1, 0, j)
                        pe.wait_ge(hidden_ready, lin(h0 + 11, (j, 11)))
                        for i in range(dn.n):
                            b, s = i // RAWS, i % RAWS
                            w_h = wh[:, s % 2, :].rearrange("p (k h c) -> p k h c", k=2, h=2)
                            w_l = wl[:, s % 2, :].rearrange("p (k h c) -> p k h c", k=2, h=2)
                            for kk in range(2):
                                split_ready(dn, b, s, kk, j)
                                kt = 2 * i + kk
                                first, final_k = kt == 0, kt == FT - 1
                                for h in range(2):
                                    o = ps[:, 4 + h, :]
                                    mm(o, jml[:, kt, :], w_h[:, kk, h, :], start=first, stop=False)
                                    mm(o, jmh[:, kt, :], w_l[:, kk, h, :], start=False, stop=False)
                                    last = mm(o, jmh[:, kt, :], w_h[:, kk, h, :], start=False, stop=final_k)
                                last.then_inc(consumed, 1)
                    pe.wait_ge(xg_hi, n_jobs * 2 + 2)
                    pe.wait_ge(xg_lo, n_jobs * 2 + 2)
                    scatter(n_jobs)
                    layer_norm(x, lambda i: pe.wait_ge(ln_in, 1))


def col_units(w):
    n = w.shape[1] // 256
    return w.reshape(KT, P, n, 2, P).transpose(2, 1, 3, 0, 4).reshape(n, P, UNIT)


def col_units_n(w):
    n = w.shape[1] // 256
    return w.reshape(KT, P, n, 256).transpose(2, 1, 0, 3).reshape(n, P, UNIT)


def row_units(w):
    n = w.shape[0] // 256
    return w.reshape(n, 2, P, D).transpose(0, 2, 1, 3).reshape(n, P, UNIT)


def feat(v):
    return v.reshape(-1, P).T


def shape_constants():
    cs = np.zeros((P, 4, P), np.float32)
    cs[:, 0] = np.eye(P)
    cs[:, 1] = 1.0 / D
    cs[:, 3] = np.triu(np.ones((P, P)), 1) / D
    for h in range(2):
        for i in range(32):
            cs[64 * h + 32 + i, 2, 64 * h + i] = -1.0
            cs[64 * h + i, 2, 64 * h + 32 + i] = 1.0
    inv = (1.0 / (np.float32(10000.0) ** (np.arange(0, HEAD, 2, dtype=np.float32) / np.float32(HEAD)))).astype(np.float32)
    ang = (np.arange(S, dtype=np.float32)[:, None] * inv[None]).astype(np.float32)
    rows = np.arange(P) % 32
    cosa, sina = np.cos(ang).T[rows], np.sin(ang).T[rows]
    q, k = np.arange(S)[:, None], np.arange(S)[None]
    causal = k <= q
    seen = [causal, causal & (q - k <= 128), causal & ((q - k) % 4 == 0), causal & ((q - k) % 16 == 0)]
    masks = []
    for m in seen:
        a = np.where(m, 0.0, NEG).astype(np.float32)
        masks.append(np.concatenate([a[:P, :P], a[P:, :]], axis=1))
    block_a = np.concatenate(masks + [cosa, sina], axis=1).astype(np.float32)
    log_g = np.log1p(-np.exp2(-5.0 - np.arange(RET_HEADS)))
    dec = []
    for h in range(RET_HEADS):
        n, m = np.arange(S)[None], np.arange(S)[:, None]
        a = np.where(n >= m, np.exp(log_g[h] * np.maximum(n - m, 0)), 0.0) * RET_DK ** -0.5
        dec.append(np.concatenate([a[:P, :], a[P:, P:]], axis=1))
    decay = np.concatenate(dec, axis=1).astype(np.float32)
    invf = (np.float32(10000.0) ** (-np.arange(P, dtype=np.float32) / np.float32(P))).astype(np.float32)
    return cs, block_a, decay, invf


def kernel(**inputs):
    import concourse.bacc as _bacc
    from concourse.bass_utils import run_bass_kernel_spmd as _run

    a = {k: np.asarray(v) for k, v in inputs.items()}
    cs, block_a, decay, invf = shape_constants()

    ws = np.empty((TOTAL + LOOKAHEAD, P, UNIT), np.float32)

    def put(name, units, off=0):
        g = PH[name].g0 + off
        ws[g:g + len(units)] = units

    for l in range(2):
        put(f"ada{l}", col_units_n(a["w_ada_2"][l]))
    qkv, wo = a["moba_w_qkv"][0], a["moba_w_o"][0]
    put("aqk", col_units(qkv[:, :2 * D]))
    put("av", col_units_n(qkv[:, 2 * D:]))
    put("ao", col_units(wo))
    dq = a["dil_w_qkv"][0]
    put("bqk", col_units(dq[:, :1536]))
    put("bv", col_units_n(dq[:, 1536:]))
    put("bo", row_units(a["dil_w_o"][0]))
    for l, c in enumerate("ab"):
        for h in range(2):
            hs = slice(h * HALF_HIDDEN, (h + 1) * HALF_HIDDEN)
            put(f"{c}in{h}", col_units(a["mlp_w_in"][l][:, hs]))
            put(f"{c}out{h}", row_units(a["mlp_w_out"][l][hs]))
    for l in range(2):
        w = a["w_in_2"][l]
        put(f"pa{l}", col_units(w[:, 0:D]))
        put(f"pb{l}", col_units(w[:, D:2 * D]))
        put(f"pqk{l}", col_units(w[:, 2 * D:4 * D]))
        put(f"pv{l}", col_units_n(w[:, 4 * D:6 * D]))
        put(f"prg{l}", col_units(w[:, 6 * D:8 * D]))
        put(f"pgc{l}", col_units(w[:, 8 * D:9 * D]))
        put(f"pgr{l}", col_units(w[:, 9 * D:10 * D]))
        put(f"co{l}", col_units(a["w_conv_o_2"][l]))
        put(f"ro{l}", row_units(a["w_ret_o_2"][l]))
        put(f"wo{l}", col_units(a["w_out_2"][l]))

    def gated(g, u, units=col_units):
        return np.stack([units(g), units(u)], axis=1).reshape(-1, P, UNIT)

    put("gu0", gated(a["ffn_w_gate_2"][0], a["ffn_w_up_2"][0]))
    put("dn0", row_units(a["ffn_w_down_2"][0]))
    for e in range(EXPERTS):
        put("gu1", gated(a["moe_w_gate_2"][0, e], a["moe_w_up_2"][0, e], col_units_n), 33 * e)
        put("dn1", row_units(a["moe_w_down_2"][0, e]), 33 * e)
    ws[TOTAL:] = ws[:LOOKAHEAD]

    par = np.zeros((P, NPAR), np.float32)

    def pcol(name, v):
        par[:, PCOL[name]:PCOL[name] + v.shape[1]] = v

    for i, (g, b) in enumerate([("ln_mix", 0), ("ln_mlp", 0), ("ln_mix", 1), ("ln_mlp", 1)]):
        pcol(f"lnA{i}g", feat(a[f"{g}_g"][b]))
        pcol(f"lnA{i}b", feat(a[f"{g}_b"][b]))
    for l in range(2):
        for k, nm in (("c", "ln_conv"), ("1", "ln1"), ("2", "ln2")):
            pcol(f"ln{k}_{l}g", feat(a[f"{nm}_g_2"][l]))
            pcol(f"ln{k}_{l}b", feat(a[f"{nm}_b_2"][l]))
        pcol(f"bdw_{l}", feat(a["b_dw_2"][l]))
        pcol(f"bada_{l}", feat(a["b_ada_2"][l]))
        pcol(f"wdw_{l}", a["w_dw_2"][l].reshape(TAPS, KT, P).transpose(2, 1, 0).reshape(P, KT * TAPS))
    pcol("c", feat(a["c_2"][0]))
    pcol("invf", invf[:, None])
    pcol("iota", np.tile(np.arange(P, dtype=np.float32), (P, 1)))
    pcol("eps", np.full((P, 1), EPS, np.float32))
    pcol("wr", a["moe_w_router_2"][0].reshape(KT, P, EXPERTS).transpose(1, 0, 2).reshape(P, KT * EXPERTS))

    arrays = {
        "wstream": ws,
        "xT": np.ascontiguousarray(a["x"][0].reshape(S, KT, P).transpose(2, 1, 0)),
        "par": par,
        "posb": np.ascontiguousarray(np.broadcast_to(a["positions_2"].astype(np.int32).reshape(1, S), (P, S))),
        "consts": cs, "blocka": block_a, "decay": decay,
    }
    nc = _bacc.Bacc("TRN2", target_bir_lowering=False, num_devices=1)
    args = [nc.dram_tensor(n, v.shape, mybir.dt.from_np(v.dtype), kind="ExternalInput").ap() for n, v in arrays.items()]
    out = nc.dram_tensor("outT", (P, KT, S), F32, kind="ExternalOutput").ap()
    build(nc, *args, out)
    r = _run(nc, [arrays], core_ids=[0])
    got = r.results[0]["outT"]
    return np.ascontiguousarray(got.transpose(2, 1, 0).reshape(1, S, D))
```

```python
from contextlib import ExitStack

import numpy as np

import concourse.bass as bass
from concourse import mybir

P = 128
S = 256
D = 1024
KT = D // P
TT = S // P
UNIT = 2048
RAWS = 4
HEAD = 64
HALF_HIDDEN = 2048
FF = 2816
FT = FF // P
EXPERTS = 8
BLK = 128
JOBS = 16
RET_HEADS = 4
RET_DK = 256
RET_DV = 512
TAPS = 31
ALPHA = float(4.0 ** 0.25)
EPS = 1e-5
NEG = -1e30
QSCALE = HEAD ** -0.5
TRI = 384

F32 = mybir.dt.float32
F32R = mybir.dt.float32r
I32 = mybir.dt.int32
U32 = mybir.dt.uint32
ALU = mybir.AluOpType
ACT = mybir.ActivationFunctionType
AX = mybir.AxisListType

PCOL = {}
_n = 0
for _name, _w in ([(f"lnA{i}{c}", KT) for i in range(4) for c in "gb"]
                  + [(f"ln{k}_{l}{c}", KT) for l in range(2) for k in ("c", "1", "2") for c in "gb"]
                  + [(f"bdw_{l}", KT) for l in range(2)] + [(f"bada_{l}", 48) for l in range(2)]
                  + [("c", KT), ("invf", 1), ("iota", P), ("eps", 1), ("wr", 8 * EXPERTS)]
                  + [(f"wdw_{l}", KT * TAPS) for l in range(2)]):
    PCOL[_name] = _n
    _n += _w
NPAR = _n

ORDER = [("ada0", 24, "ada"), ("ada1", 24, "ada"),
         ("aqk", 8, "T"), ("av", 4, "N"), ("ao", 4, "T"),
         ("ain0", 8, "relu"), ("aout0", 8, "R"), ("ain1", 8, "relu"), ("aout1", 8, "R"),
         ("bqk", 6, "T"), ("bv", 3, "N"), ("bo", 3, "R"),
         ("bin0", 8, "relu"), ("bout0", 8, "R"), ("bin1", 8, "relu"), ("bout1", 8, "R")]
for _l in range(2):
    ORDER += [(f"pb{_l}", 4, "T"), (f"pa{_l}", 4, "T"), (f"pqk{_l}", 8, "T"), (f"pv{_l}", 8, "N"),
              (f"prg{_l}", 8, "T"), (f"pgc{_l}", 4, "T"), (f"pgr{_l}", 4, "T"),
              (f"co{_l}", 4, "T"), (f"ro{_l}", 8, "R"), (f"wo{_l}", 4, "T"),
              (f"gu{_l}", 22, "T"), (f"dn{_l}", 11, "R")]


class Phase:
    pass


def slot_uses(n):
    return [len(range(s, n, RAWS)) for s in range(RAWS)]


def plan():
    phases = {}
    g, uses, da, dd = 0, [0] * RAWS, 4, 4
    prev_n = None
    eu = [a + b for a, b in zip(slot_uses(22), slot_uses(11))]
    for name, n, kind in ORDER:
        p = Phase()
        p.name, p.n, p.kind, p.g0, p.uses0 = name, n, kind, g, list(uses)
        p.moe = name in ("gu1", "dn1")
        p.g_e, p.uses_e = (33, eu) if p.moe else (0, [0] * RAWS)
        p.raw_back = None if prev_n is None else [
            min(prev_n - i for i in range(prev_n) if i % RAWS == s) if prev_n > s else RAWS for s in range(RAWS)]
        p.pair_back = None if prev_n is None else [
            min([prev_n - i for i in range(prev_n) if i % 2 == s]) for s in range(2)]
        if name == "gu1":
            p.raw_back, p.pair_back = [3, 2, 1, 1], [1, 1]
        if prev_n == 3:
            p.raw_back = [3, 2, 1, 1]
        p.da0, p.dd0 = da, dd
        ga = {"gu": n // 2, "pb": n, "pq": n, "pv": n, "pr": n, "pg": n}.get(name[:2], 0)
        ga = n if name in ("aqk", "av", "bqk", "bv") else ga
        p.act_drains = ga
        p.dve_drains = {"R": 8, "relu": 0}.get(kind, n - ga)
        p.da_e, p.dd_e = (11, 11) if p.moe else (0, 0)
        da, dd = da + p.act_drains, dd + p.dve_drains
        g += n
        uses = [a + b for a, b in zip(uses, slot_uses(n))]
        prev_n = n
        phases[name] = p
    names = [n for n, _, _ in ORDER]
    for a, b in zip(names, names[1:]):
        phases[a].next = phases[b]
    phases["dn1"].next = phases["gu1"]
    return phases, g


PH, STREAM = plan()
TOTAL = PH["gu1"].g0 + 33 * EXPERTS
LOOKAHEAD = 2


ROW_M = [4, 5, 6, 7, 0, 1, 2, 3]


def lin(const, *terms):
    for reg, k in terms:
        if k and not (isinstance(reg, int) and reg == 0):
            const = reg * k + const
    return const


def build(nc, wstream, xT, par, posb, consts, blockA, decay, outT):
    with ExitStack() as ctx:
        def sb(name, shape, dt=F32):
            return ctx.enter_context(nc.sbuf_tensor(name, shape, dt))

        def sem(name):
            return ctx.enter_context(nc.semaphore(name))

        raw = sb("raw", [P, RAWS, UNIT])
        wh = sb("wh", [P, 2, UNIT], F32R)
        wl = sb("wl", [P, 2, UNIT], F32R)
        x = sb("x", [P, KT, S])
        xh = sb("xh", [P, KT, S], F32R)
        xl = sb("xl", [P, KT, S], F32R)
        cs = sb("cs", [P, 4, P])
        ji = sb("ji", [P, JOBS + 1], I32)
        pr = sb("pr", [P, NPAR])
        cosr = sb("cosr", [P, S])
        sinr = sb("sinr", [P, S])
        std = sb("std", [P, S])
        rstd = sb("rstd", [P, S])
        ada = sb("ada", [P, 2, 48])
        cf = sb("cf", [P, KT])
        bs = sb("bs", [P, KT])
        st = sb("st", [P, 128])
        ix = sb("ix", [P, 16], U32)
        pos = sb("pos", [P, S], I32)
        work = sb("work", [P, 14592])
        with ExitStack() as hidden:
            mh = hidden.enter_context(nc.sbuf_tensor("mh", [P, FT, S], F32R))
            ml = hidden.enter_context(nc.sbuf_tensor("ml", [P, FT, S], F32R))
        CH = mh[:, 0:4, :].rearrange("p a (b c) -> p (a b) c", c=P)
        CL = mh[:, 4:8, :].rearrange("p a (b c) -> p (a b) c", c=P)
        with ExitStack() as mixer:
            ret = mixer.enter_context(nc.sbuf_tensor("ret", [P, 11264], F32))
        hn = sb("hn", [P, TT, D])
        jmh = sb("jmh", [P, FT, BLK], F32R)
        jml = sb("jml", [P, FT, BLK], F32R)
        gx = sb("gx", [P, TT, BLK])
        gt = sb("gt", [P, S], F32R)

        def view(buf, off, width, pat, **kw):
            return buf[:, off:off + width].rearrange(pat, **kw)

        ident, ones, swap = cs[:, 0, :], cs[:, 1, :], cs[:, 2, :]
        RG = view(work, 0, 4096, "p (j t) -> p j t", t=S)
        GC = view(work, 4096, 2048, "p (j t) -> p j t", t=S)
        GR = view(work, 6144, 2048, "p (j t) -> p j t", t=S)
        PADW = TAPS - 1 + S
        U = view(work, 8192, KT * PADW, "p (j t) -> p j t", t=PADW)
        CV = view(work, 10480, 2048, "p (j t) -> p j t", t=S)
        SRC = view(work, 12528, 2048, "p (j t) -> p j t", t=S)
        RQ = view(ret, 0, 2048, "p (j t) -> p j t", t=S)
        RK = view(ret, 2048, 2048, "p (j t) -> p j t", t=S)
        RV = view(ret, 4096, 4096, "p (t c) -> p t c", t=TT)
        DEC = view(ret, 8192, RET_HEADS * TRI, "p (h c) -> p h c", h=RET_HEADS)
        RST = view(ret, 8192 + 1536, RET_HEADS * TRI, "p (h c) -> p h c", h=RET_HEADS)
        ON = view(ret, 0, 4096, "p (h n d) -> p h n d", h=RET_HEADS, n=TT)
        QK = view(work, 0, 4096, "p (j t) -> p j t", t=S)
        VN = view(work, 4096, 2048, "p (t c) -> p t c", t=TT)
        RC = view(work, 6144, 1024, "p (b c) -> p b c", b=2)
        SS = [view(buf, off, 3 * TRI, "p (g c) -> p g c", g=3) for buf, off in ((work, 7168), (ret, 0), (ret, 3 * TRI))]
        PT = [view(buf, off, 3 * TRI, "p (g c) -> p g c", g=3) for buf, off in ((work, 8320), (ret, 6 * TRI))]
        MASK = view(work, 9472, 4 * TRI, "p (g c) -> p g c", g=4)
        COSA = work[:, 11008:11264]
        SINA = work[:, 11264:11520]
        RT = work[:, 11520:12032]
        SG = work[:, 0:512]
        HF = work[:, 512:1024]
        HF2 = view(work, 512, 512, "p (b c) -> p b c", b=2)
        YF = work[:, 1024:2048]
        DG = [view(buf, off, 48 * P, "p (i m c) -> p i m c", i=24, m=2) for buf, off in ((work, 0), (ret, 2048))]
        LG = view(work, 2048, 16, "p (t e) -> p t e", t=TT)
        CMB = view(work, 2064, 16, "p (t e) -> p t e", t=TT)
        CMB2 = view(work, 2080, 16, "p (t e) -> p t e", t=TT)
        SEL = view(work, 2096, 16, "p (t e) -> p t e", t=TT)
        SEL2 = view(work, 2112, 16, "p (t e) -> p t e", t=TT)
        POS = view(work, 2128, 16, "p (t e) -> p t e", t=TT)
        CNT = work[:, 2144:2152]
        CUM = view(work, 2152, 4 * 12, "p (i c) -> p i c", i=4)
        EXPJ = work[:, 2200:2216]
        STARTJ = work[:, 2216:2232]
        PJ = view(work, 2232, 2 * JOBS, "p (t j) -> p t j", t=TT)
        CJ = view(work, 2264, 2 * JOBS, "p (t j) -> p t j", t=TT)
        WS = work[:, 2296:2297]
        MJ = view(work, 2304, 4 * 8 * JOBS, "p (t e j) -> p t e j", t=4, e=EXPERTS)
        ISJ = view(work, 2816, 8 * JOBS, "p (e j) -> p e j", e=EXPERTS)
        ACC = view(work, 4096, 2048, "p (j t) -> p j t", t=S)

        ps = ctx.enter_context(nc.psum_tensor("ps", [P, 8, 512], F32))

        def col(name, j=0, w=1):
            return pr[:, PCOL[name] + j:PCOL[name] + j + w]

        landed = [sem(f"raw_landed{s}") for s in range(RAWS)]
        hi_split = sem("hi_split")
        lo_split = sem("lo_split")
        consumed = sem("consumed")
        drained_act = sem("drained_act")
        drained_dve = sem("drained_dve")
        consts_in = sem("consts_in")
        x_in = sem("x_in")
        par_in = sem("par_in")
        pos_in = sem("pos_in")
        blocka_in = sem("blocka_in")
        decay_in = sem("decay_in")
        out_done = sem("out_done")
        src_ready = sem("src_ready")
        xh_ready = sem("xh_ready")
        moving = sem("moving")
        nonlin = sem("nonlin")
        hf_ready = sem("hf_ready")
        mh_ready = sem("mh_ready")
        hidden_ready = sem("hidden_ready")
        ln_mean = sem("ln_mean")
        ln_cen = sem("ln_cen")
        ln_sq = sem("ln_sq")
        ln_var = sem("ln_var")
        ln_std = sem("ln_std")
        swapped = sem("swapped")
        cos_done = sem("cos_done")
        roped = sem("roped")
        qk_done = sem("qk_done")
        masked = sem("masked")
        mx_ready = sem("mx_ready")
        exp_done = sem("exp_done")
        p_ready = sem("p_ready")
        pt_done = sem("pt_done")
        pt_copied = sem("pt_copied")
        pv_done = sem("pv_done")
        ao_copied = sem("ao_copied")
        vstep = sem("vstep")
        pstep = sem("pstep")
        tap_done = sem("tap_done")
        trig_arg = sem("trig_arg")
        trig_done = sem("trig_done")
        ret_roped = sem("ret_roped")
        st_done = sem("st_done")
        st_decayed = sem("st_decayed")
        o_done = sem("o_done")
        o_copied = sem("o_copied")
        ovar = sem("ovar")
        ostd = sem("ostd")
        o_normed = sem("o_normed")
        g_turned = sem("g_turned")
        logits = sem("logits")
        gap_ready = sem("gap_ready")
        gap_exp = sem("gap_exp")
        sel_ready = sem("sel_ready")
        ranked = sem("ranked")
        jobs_ready = sem("jobs_ready")
        h_turned = sem("h_turned")
        h_copied = sem("h_copied")
        turned = sem("turned")
        g_ready = sem("g_ready")
        xg_filled = sem("xg_filled")
        xg_hi = sem("xg_hi")
        xg_lo = sem("xg_lo")
        gt_filled = sem("gt_filled")
        gt_copied = sem("gt_copied")
        yf_done = sem("yf_done")
        y_hi = sem("y_hi")
        y_split = sem("y_split")
        sc_filled = sem("sc_filled")
        sc_added = sem("sc_added")
        ln_in = sem("ln_in")
        final = sem("final")
        u_ready = sem("u_ready")
        c_act = sem("c_act")

        block = ctx.enter_context(nc.Block())

        def run_units(eng, ph, emit, ahead=LOOKAHEAD):
            nb = max((ph.n - ahead) // RAWS, 0)
            if nb > 1:
                with eng.Fori(0, nb) as b:
                    for s in range(RAWS):
                        emit(b, s)
            else:
                nb = 0
            for i in range(nb * RAWS, ph.n):
                emit(i // RAWS, i % RAWS)

        def job_units(eng, ph, emit, between):
            for s in range(RAWS):
                emit(0, s)
                if s in between:
                    between[s]()
            with eng.Fori(1, (ph.n - LOOKAHEAD) // RAWS) as b:
                for s in range(RAWS):
                    emit(b, s)
            for i in range((ph.n - LOOKAHEAD) // RAWS * RAWS, ph.n):
                emit(i // RAWS, i % RAWS)

        def ahead_of(ph, b, s, e):
            s2 = s + LOOKAHEAD
            if isinstance(b, int) and RAWS * b + s2 >= ph.n:
                i = RAWS * b + s2 - ph.n
                return ph.next, i // RAWS, i % RAWS, (e + 1 if ph.name == "dn1" else e)
            return ph, b + s2 // RAWS, s2 % RAWS, e

        def unit_no(ph, b, s, e, k=1, add=0):
            return lin(k * (ph.g0 + s) + add, (b, k * RAWS), (e, k * ph.g_e))

        def turned_bank(G, i):
            return i % 2 if G == 1 else 0

        @block.sync
        def _(sp):
            sp.dma_start(cs[:], consts).then_inc(consts_in, 16)
            sp.dma_start(pr[:], par).then_inc(par_in, 16)
            sp.dma_start(pos[:], posb).then_inc(pos_in, 16)

            def stream(ph, e=0):
                def load(b, s, peeled):
                    if peeled and ph.raw_back is not None:
                        sp.wait_ge(lo_split, lin(2 * (ph.g0 - ph.raw_back[s] + 1), (e, 2 * ph.g_e)))
                    elif not peeled:
                        sp.wait_ge(lo_split, unit_no(ph, b, s, e, 2, -2 * RAWS + 2))
                    sp.dma_start(raw[:, s, :], wstream[unit_no(ph, b, s, e)]).then_inc(landed[s], 16)
                for s in range(min(RAWS, ph.n)):
                    load(0, s, True)
                nb = ph.n // RAWS
                if nb > 1:
                    with sp.Fori(1, nb) as b:
                        for s in range(RAWS):
                            load(b, s, False)
                for i in range(max(nb, 1) * RAWS, ph.n):
                    load(i // RAWS, i % RAWS, False)

            def jobs(sp):
                gu, dn = PH["gu1"], PH["dn1"]

                def load(ph, b, s, j, expert):
                    if isinstance(b, int) and b == 0:
                        sp.wait_ge(lo_split, lin(2 * (ph.g0 - ph.raw_back[s] + 1), (j, 2 * ph.g_e)))
                    else:
                        sp.wait_ge(lo_split, unit_no(ph, b, s, j, 2, -2 * RAWS + 2))
                    sp.dma_start(raw[:, s, :], wstream[unit_no(ph, b, s, expert)]).then_inc(landed[s], 16)
                for s in range(LOOKAHEAD):
                    load(gu, 0, s, 0, 0)
                sp.wait_ge(jobs_ready, 1)
                n_jobs = sp.value_load(ji[0:1, JOBS:JOBS + 1], min_val=EXPERTS, max_val=JOBS - 1)
                with sp.Fori(0, n_jobs) as j:
                    expert = sp.value_load(ji[0:1, bass.ds(j, 1)], min_val=0, max_val=EXPERTS - 1)
                    for s in range(LOOKAHEAD, RAWS):
                        load(gu, 0, s, j, expert)
                    with sp.Fori(1, gu.n // RAWS) as b:
                        for s in range(RAWS):
                            load(gu, b, s, j, expert)
                    for i in range(gu.n // RAWS * RAWS, gu.n):
                        load(gu, i // RAWS, i % RAWS, j, expert)
                    for i in range(dn.n):
                        load(dn, i // RAWS, i % RAWS, j, expert)
                    after = sp.value_load(ji[0:1, bass.ds(j + 1, 1)], min_val=0, max_val=EXPERTS)
                    for s in range(LOOKAHEAD):
                        load(gu, 0, s, j + 1, after)

            for name, _, _ in ORDER:
                ph = PH[name]
                if name == "dn1":
                    continue
                if name == "gu1":
                    jobs(sp)
                    continue
                stream(ph)
                if name == "ada0":
                    sp.dma_start(x[:], xT).then_inc(x_in, 16)
                    sp.dma_start(work[:, 9472:11520], blockA).then_inc(blocka_in, 16)
                if name[:2] == "pb":
                    sp.wait_ge(consumed, 2 * ph.g0)
                    sp.dma_start(ret[:, 8192:8192 + 1536], decay).then_inc(decay_in, 16)
            sp.wait_ge(final, 1)
            sp.dma_start(outT, x[:]).then_inc(out_done, 16)
            sp.wait_ge(out_done, 16)

        @block.scalar
        def _(act):
            A = nc.scalar.activation

            def split(ph, b, s, e=0):
                r = raw[:, s, :].rearrange("p (h c) -> p h c", h=2)
                o = wh[:, s % 2, :].rearrange("p (h c) -> p h c", h=2)
                act.wait_ge(landed[s], lin(16 * (ph.uses0[s] + 1), (b, 16), (e, 16 * ph.uses_e[s])))
                for half in range(2):
                    if isinstance(b, int) and b == 0 and s < 2:
                        if ph.pair_back is not None:
                            act.wait_ge(consumed, lin(2 * (ph.g0 - ph.pair_back[s]) + half + 1, (e, 2 * ph.g_e)))
                    else:
                        act.wait_ge(consumed, unit_no(ph, b, s, e, 2, half + 1 - 4))
                    A(o[:, half], r[:, half], ACT.Copy).then_inc(hi_split, 1)

            def split_ahead(ph, b, s, e=0):
                split(*ahead_of(ph, b, s, e))

            def filled(ph, b, s, e=0):
                act.wait_ge(consumed, unit_no(ph, b, s, e, 2, 2))

            def columns(name, drain=None, extra=None):
                ph = PH[name]
                if drain is not None and ph.dd0 > 4:
                    act.wait_ge(drained_dve, ph.dd0)

                def one(b, s):
                    split_ahead(ph, b, s)
                    if drain is not None:
                        filled(ph, b, s)
                        drain(lin(s, (b, RAWS)), ps[:, s, :]).then_inc(drained_act, 1)
                    if extra is not None:
                        extra(lin(s, (b, RAWS)))
                run_units(act, ph, one)

            copies = [0, 0, 0]

            def xh_chunk(src, c):
                copies[0] += 1
                act.wait_ge(src_ready, copies[0])
                A(xh[:, 2 * c:2 * c + 2, :], src[:, 2 * c:2 * c + 2, :], ACT.Copy).then_inc(xh_ready, 1)

            def xh_from(src, tiles=KT):
                for c in range(tiles // 2):
                    xh_chunk(src, c)

            lns = [0]

            def layer_norm(src):
                n = lns[0]
                lns[0] += 1
                for c in range(4):
                    act.wait_ge(ln_cen, 4 * n + c + 1)
                    A(SRC[:, 2 * c:2 * c + 2, :], src[:, 2 * c:2 * c + 2, :], ACT.Square).then_inc(ln_sq, 1)
                act.wait_ge(ln_var, n + 1)
                A(std[:], ps[:, 5, 0:S], ACT.Sqrt, bias=col("eps")).then_inc(ln_std, 1)

            nl = [0]

            def relu_phase(name):
                ph, n0 = PH[name], nl[0]
                nl[0] += ph.n

                def one(b, s):
                    split_ahead(ph, b, s)
                    filled(ph, b, s)
                    A(SG, ps[:, s, :], ACT.Relu).then_inc(nonlin, 1)
                    act.wait_ge(hf_ready, lin(n0 + s + 1, (b, RAWS)))
                    A(mh[:, :, :].rearrange("p (i a) t -> p i (a t)", a=2)[:, lin(s, (b, RAWS))], HF,
                      ACT.Copy).then_inc(mh_ready, 1)
                run_units(act, ph, one)

            def gate_unit(ph, n0):
                def one(b, s):
                    split_ahead(ph, b, s)
                    if s % 2 == 0:
                        filled(ph, b, s)
                        A(SG, ps[:, s, :], ACT.Silu).then_inc(drained_act, 1)
                    else:
                        act.wait_ge(hf_ready, lin(n0 + s // 2 + 1, (b, 2)))
                        A(mh[:, :, :].rearrange("p (i a) t -> p i (a t)", a=2)[:, lin(s // 2, (b, 2))], HF,
                          ACT.Copy).then_inc(mh_ready, 1)
                return one

            def job_unit(ph, n0, j):
                def one(b, s):
                    last_pair = isinstance(b, int) and RAWS * b + s >= ph.n - 2
                    if not last_pair:
                        split_ahead(ph, b, s, j)
                    if s % 2 == 0:
                        act.wait_ge(hf_ready, lin(n0 + s // 2, (b, 2), (j, 11)))
                        filled(ph, b, s, j)
                        A(SG[:, 0:256], ps[:, s, 0:256], ACT.Silu).then_inc(drained_act, 1)
                        if last_pair:
                            split_ahead(ph, b, s, j)
                        return
                    if last_pair:
                        split_ahead(ph, b, s, j)
                    if not (isinstance(b, int) and b == 0 and s == 1):
                        upper(lin(s // 2 - 1, (b, 2)), 4 + (s // 2 + 1) % 2, j)
                return one

            def upper(i, bank, j):
                act.wait_ge(turned, lin(i + 2, (j, 11)))
                A(jmh[:].rearrange("p (i a) t -> p i (a t)", a=2)[:, i], ps[:, bank, 0:256],
                  ACT.Copy).then_inc(mh_ready, 1)

            act.sem_inc(drained_act, 4)
            act.sem_inc(drained_dve, 4)
            act.sem_inc(nonlin, 4)
            act.wait_ge(par_in, 16)
            A(cf[:], col("c", 0, KT), ACT.Silu).then_inc(c_act, 1)
            act.wait_ge(c_act, 1)
            A(CH, cf[:].unsqueeze(2).broadcast_to([P, KT, P]), ACT.Copy).then_inc(c_act, 1)
            act.wait_ge(trig_arg, 1)
            A(cosr[:], std[:], ACT.Sin)
            A(sinr[:], rstd[:], ACT.Sin).then_inc(trig_done, 1)
            split(PH["ada0"], 0, 0)
            split(PH["ada0"], 0, 1)
            columns("ada0")
            xh_from(x[:])
            columns("ada1")

            def attention(groups, heads_of, g0, h0):
                G = len(heads_of(0))

                def exponentials(i):
                    sc, q = SS[i % 3], st[:, 8 * (i % 3):8 * (i % 3) + 8]
                    act.wait_ge(mx_ready, g0 + i + 1)
                    A(sc[:, 0:G, 0:128], sc[:, 0:G, 0:128], ACT.Exp, bias=q[:, 0:1], scale=QSCALE, accum_out=q[:, 4:5])
                    A(sc[:, 0:G, 128:384], sc[:, 0:G, 128:384], ACT.Exp, bias=q[:, 1:2], scale=QSCALE,
                      accum_out=q[:, 5:6]).then_inc(exp_done, 1)

                def outputs(i):
                    for k, h in enumerate(heads_of(i)):
                        n = h0 + i * G + k
                        r = slice(64 * (h % 2), 64 * (h % 2) + 64)
                        act.wait_ge(pv_done, n + 1)
                        A(SRC[r, h // 2, :], ps[r, 6 + n % 2, 0:S], ACT.Copy).then_inc(ao_copied, 1)
                exponentials(0)
                for i in range(groups):
                    if i + 1 < groups:
                        exponentials(i + 1)
                    if G == 1 and i:
                        outputs(i - 1)
                    act.wait_ge(pt_done, g0 + i + 1)
                    b = 3 + turned_bank(G, i)
                    A(PT[i % 2][:, 0:G, :], ps[:, b:b + G, 0:TRI], ACT.Copy).then_inc(pt_copied, 1)
                    if G > 1:
                        outputs(i)
                if G == 1:
                    outputs(groups - 1)

            def pairs_out(dst):
                v = dst.rearrange("p (i a) t -> p i (a t)", a=2)
                return lambda i, bank: A(v[:, i], bank, ACT.Copy)

            def tokens_out(dst):
                v = dst.rearrange("p t (i c) -> p i t c", c=256)
                return lambda i, bank: A(v[:, i], bank.rearrange("p (t c) -> p t c", t=2), ACT.Copy)

            def pairs_act(dst, func):
                v = dst.rearrange("p (i a) t -> p i (a t)", a=2)
                return lambda i, bank: A(v[:, i], bank, func)

            columns("aqk", pairs_out(QK[:, 0:16, :]))
            columns("av", tokens_out(VN))
            attention(16, lambda i: [i], 0, 0)
            act.wait_ge(ao_copied, 16)
            act.sem_inc(src_ready, 4)
            xh_from(SRC)
            columns("ao")
            layer_norm(x[:])
            xh_from(x[:])
            relu_phase("ain0")
            columns("aout0")
            relu_phase("ain1")
            columns("aout1")
            layer_norm(x[:])
            xh_from(x[:])
            columns("bqk", pairs_out(QK[:, 0:12, :]))
            columns("bv", tokens_out(VN[:, :, 0:768]))
            attention(4, lambda j: [j, 4 + j, 8 + j], 16, 16)
            act.wait_ge(ao_copied, 28)
            act.sem_inc(src_ready, 3)
            xh_from(SRC, 6)
            columns("bo")
            layer_norm(x[:])
            xh_from(x[:])
            relu_phase("bin0")
            columns("bout0")
            relu_phase("bin1")
            columns("bout1")
            layer_norm(x[:])

            for l in range(2):
                xh_from(SRC)
                columns(f"pb{l}", pairs_act(CV, ACT.Sigmoid))
                columns(f"pa{l}")
                columns(f"pqk{l}", pairs_out(ret[:, 0:4096].rearrange("p (j t) -> p j t", t=S)))
                columns(f"pv{l}", tokens_out(RV))
                columns(f"prg{l}", pairs_act(RG, ACT.Silu))
                columns(f"pgc{l}", pairs_act(GC, ACT.Sigmoid))
                for i in range(8):
                    act.wait_ge(o_done, 8 * l + i + 1)
                    A(ON[:, i // 2, i % 2, :], ps[:, 4 + i % 4, :], ACT.Copy).then_inc(o_copied, 1)
                columns(f"pgr{l}", pairs_act(GR, ACT.Sigmoid))
                act.wait_ge(ovar, l + 1)
                A(st[:, 80:88], st[:, 64:80].rearrange("p (i c) -> p i c", c=2)[:, :, 1], ACT.Sqrt,
                  bias=col("eps")).then_inc(ostd, 1)
                act.wait_ge(ret_roped, l + 1)
                layer_norm(CV)
                for j in range(KT):
                    act.wait_ge(u_ready, 4 * l + j // 2 + 1)
                    last = A(SRC[:, j, :], CV[:, j, :], ACT.Silu, bias=col(f"lnc_{l}b", j), scale=col(f"lnc_{l}g", j))
                    if j % 2:
                        last.then_inc(src_ready, 1)
                        xh_chunk(SRC, j // 2)

                def gated_upper(u, l=l):
                    act.wait_ge(g_turned, 8 * l + 2 * u + 2)
                    for i in (2 * u, 2 * u + 1):
                        act.wait_ge(hf_ready, nl[0] + i + 1)
                        A(mh[:, 2 * i:2 * i + 2, :], RG[:, 2 * i:2 * i + 2, :], ACT.Copy).then_inc(mh_ready, 1)
                columns(f"co{l}", extra=gated_upper)
                nl[0] += 8
                columns(f"ro{l}")
                xh_from(SRC)
                columns(f"wo{l}")
                layer_norm(x[:])
                xh_from(SRC)
                if l == 0:
                    run_units(act, PH["gu0"], gate_unit(PH["gu0"], nl[0]))
                    nl[0] += 11
                    columns("dn0")
                    layer_norm(x[:])
                else:
                    act.wait_ge(gap_ready, 1)
                    A(st[:, 34:36], st[:, 32:34], ACT.Exp).then_inc(gap_exp, 1)
                    for i in range(4):
                        act.wait_ge(h_turned, i + 1)
                        A(hn[:, i // 2, i % 2 * 512:i % 2 * 512 + 512], ps[:, i, :], ACT.Copy).then_inc(h_copied, 1)
                    act.sem_inc(yf_done, 1)
                    act.sem_inc(turned, 1)

                    def gathered(j):
                        for q in range(2):
                            act.wait_ge(xg_filled, lin(q + 1, (j, 2)))
                            A(xh[:, 4 * q:4 * q + 4, 0:BLK], ps[:, 6 + q, :].rearrange("p (k t) -> p k t", k=4),
                              ACT.Copy).then_inc(xg_hi, 1)

                    def output_upper(j):
                        act.wait_ge(yf_done, j + 1)
                        A(xh[:, :, BLK:2 * BLK], YF.rearrange("p (m c) -> p m c", m=KT), ACT.Copy).then_inc(y_hi, 1)
                    gathered(0)
                    act.wait_ge(jobs_ready, 1)
                    n_jobs = act.value_load(ji[0:1, JOBS:JOBS + 1], min_val=EXPERTS, max_val=JOBS - 1)
                    gu, dn = PH["gu1"], PH["dn1"]
                    with act.Fori(0, n_jobs) as j:
                        one = job_unit(gu, nl[0], j)

                        def middle():
                            act.wait_ge(gt_filled, j + 1)
                            A(gt[:], ps[:, 6, 0:S], ACT.Copy)
                            A(WS, ps[:, 6, S:S + 1], ACT.Copy).then_inc(gt_copied, 1)
                        job_units(act, gu, one, {0: lambda: output_upper(j), 3: middle})
                        gathered(j + 1)
                        upper(FT // 2 - 1, 2, j)
                        run_units(act, dn, lambda b, s: split_ahead(dn, b, s, j))
                        act.wait_ge(consumed, unit_no(dn, 0, dn.n, j, 2))
                        act.wait_ge(gt_copied, j + 1)
                        A(YF.rearrange("p (h c) -> p h c", h=2), ps[:, 4:6, :], ACT.Copy, scale=WS).then_inc(yf_done, 1)
                    output_upper(n_jobs)
                    layer_norm(x[:])

        @block.gpsimd
        def _(pool):
            steps = [0]

            def link(ins):
                steps[0] += 1
                ins.then_inc(pstep, 1)
                pool.wait_ge(pstep, steps[0])

            T2 = nc.gpsimd.tensor_tensor

            def rope_cos(ntiles, k0, act_total):
                pool.wait_ge(drained_act, act_total)
                for i in range(ntiles // 2):
                    if i >= 2:
                        pool.wait_ge(roped, k0 + i - 1)
                    T2(RC[:, i % 2, :].rearrange("p (a t) -> p a t", a=2), QK[:, 2 * i:2 * i + 2, :],
                       COSA.unsqueeze(1).broadcast_to([P, 2, S]), ALU.mult).then_inc(cos_done, 1)

            pool.wait_ge(blocka_in, 16)
            rope_cos(16, 0, PH["av"].da0)
            rope_cos(12, 8, PH["bv"].da0)
            pool.wait_ge(trig_done, 1)
            for l in range(2):
                pool.wait_ge(drained_act, PH[f"pv{l}"].da0)
                pool.wait_ge(moving, 1 + 4 * (7 + 4 * l) - 1)
                cosb = cosr[:].unsqueeze(1).broadcast_to([P, 4, S])
                sinb = sinr[:].unsqueeze(1).broadcast_to([P, 4, S])
                t1, t2 = SRC[:, 0:4, :], SRC[:, 4:8, :]
                for q in (RQ, RK):
                    v = q.rearrange("p (h a) t -> p a h t", a=2)
                    x1, x2 = v[:, 0], v[:, 1]
                    T2(t1, x1, sinb, ALU.mult)
                    link(T2(t2, x2, sinb, ALU.mult))
                    T2(x1, x1, cosb, ALU.mult)
                    link(T2(x2, x2, cosb, ALU.mult))
                    T2(x1, x1, t2, ALU.subtract)
                    ins = T2(x2, x2, t1, ALU.add)
                    if q is RQ:
                        link(ins)
                    else:
                        ins.then_inc(ret_roped, 1)

            def output_rest(j):
                pool.wait_ge(y_hi, j + 1)
                T2(xl[:, :, BLK:2 * BLK], YF.rearrange("p (m c) -> p m c", m=KT), xh[:, :, BLK:2 * BLK].bitcast(F32),
                   ALU.subtract).then_inc(y_split, 1)
            pool.wait_ge(jobs_ready, 1)
            n_jobs = pool.value_load(ji[0:1, JOBS:JOBS + 1], min_val=EXPERTS, max_val=JOBS - 1)
            with pool.Fori(0, n_jobs) as j:
                output_rest(j)
            output_rest(n_jobs)

        @block.vector
        def _(dve):
            V = nc.vector
            steps = [0]

            def link(ins):
                steps[0] += 1
                ins.then_inc(vstep, 1)
                dve.wait_ge(vstep, steps[0])

            def split(ph, b, s, e=0, between=None):
                r = raw[:, s, :].rearrange("p (h c) -> p h c", h=2)
                hi = wh[:, s % 2, :].rearrange("p (h c) -> p h c", h=2)
                o = wl[:, s % 2, :].rearrange("p (h c) -> p h c", h=2)
                for half in range(2):
                    dve.wait_ge(hi_split, unit_no(ph, b, s, e, 2, half + 1))
                    V.tensor_tensor(o[:, half], r[:, half], hi[:, half].bitcast(F32),
                                    ALU.subtract).then_inc(lo_split, 1)
                    if half == 0 and between is not None:
                        between()

            def split_ahead(ph, b, s, e=0, between=None):
                split(*ahead_of(ph, b, s, e), between=between)

            def filled(ph, b, s, e=0):
                dve.wait_ge(consumed, unit_no(ph, b, s, e, 2, 2))

            def columns(name, drain=None, extra=None):
                ph = PH[name]
                if drain is not None and ph.da0 > 4:
                    dve.wait_ge(drained_act, ph.da0)

                def one(b, s):
                    def empty():
                        filled(ph, b, s)
                        drain(b, s, ps[:, s, :]).then_inc(drained_dve, 1)
                    split_ahead(ph, b, s, between=None if drain is None else empty)
                    if extra is not None:
                        extra(lin(s, (b, RAWS)))
                run_units(dve, ph, one)

            def rows(name, drain):
                ph = PH[name]

                def empty():
                    dve.wait_ge(consumed, 2 * (ph.g0 + ph.n))
                    for bank in range(8):
                        drain(ROW_M[bank], ps[:, bank, 0:S]).then_inc(drained_dve, 1)

                def one(b, s):
                    last = isinstance(b, int) and RAWS * b + s == ph.n - 1
                    split_ahead(ph, b, s, between=empty if last else None)
                run_units(dve, ph, one)

            splits = [0]

            def rest_chunk(src, c):
                splits[0] += 1
                dve.wait_ge(xh_ready, splits[0])
                v = slice(2 * c, 2 * c + 2)
                V.tensor_tensor(xl[:, v, :], src[:, v, :], xh[:, v, :].bitcast(F32), ALU.subtract).then_inc(moving, 1)

            def rest_of(src, tiles=KT):
                for c in range(tiles // 2):
                    rest_chunk(src, c)

            lns = [0]

            def normed(src, between=None):
                n = lns[0]
                lns[0] += 1
                dve.wait_ge(ln_mean, n + 1)
                for c in range(4):
                    v = src[:, 2 * c:2 * c + 2, :]
                    V.tensor_tensor(v, v, ps[:, 4, 0:S].unsqueeze(1).broadcast_to([P, 2, S]),
                                    ALU.subtract).then_inc(ln_cen, 1)
                if between is not None:
                    between()
                dve.wait_ge(ln_std, n + 1)
                link(V.reciprocal(rstd[:], std[:]))

            def layer_norm(g, b):
                normed(x[:])
                for c in range(5):
                    if c < 4:
                        for j in (2 * c, 2 * c + 1):
                            last = V.scalar_tensor_tensor(x[:, j, :], x[:, j, :], col(g, j), rstd[:], ALU.mult, ALU.mult)
                        link(last)
                        for j in (2 * c, 2 * c + 1):
                            last = V.tensor_scalar(x[:, j, :], x[:, j, :], col(b, j), None, ALU.add)
                        last.then_inc(src_ready, 1)
                    if c > 0:
                        rest_chunk(x, c - 1)

            def layer_norm_modulated(g, b, l, which):
                o = 24 * which
                link(V.tensor_tensor(bs[:], col(b, 0, KT), ada[:, l, o + 8:o + 16], ALU.mult))
                link(V.tensor_tensor(bs[:], bs[:], ada[:, l, o:o + 8], ALU.add))
                normed(x[:])
                for c in range(5):
                    if c < 4:
                        for j in (2 * c, 2 * c + 1):
                            last = V.scalar_tensor_tensor(x[:, j, :], x[:, j, :], col(g, j), rstd[:], ALU.mult, ALU.mult)
                        link(last)
                        for j in (2 * c, 2 * c + 1):
                            last = V.tensor_scalar(SRC[:, j, :], x[:, j, :], ada[:, l, o + 8 + j:o + 9 + j],
                                                   bs[:, j:j + 1], ALU.mult, ALU.add)
                        last.then_inc(src_ready, 1)
                    if c > 0:
                        rest_chunk(SRC, c - 1)
                for j in range(KT):
                    last = V.tensor_scalar(x[:, j, :], x[:, j, :], col(b, j), None, ALU.add)
                return last

            nl = [0, 4]

            def relu_phase(name):
                ph, n0, h0 = PH[name], nl[0], nl[1]
                nl[0] += ph.n
                nl[1] += ph.n

                def one(b, s):
                    split_ahead(ph, b, s)
                    i = lin(s, (b, RAWS))
                    dve.wait_ge(nonlin, lin(h0 + s + 1, (b, RAWS)))
                    if n0 or s or b:
                        dve.wait_ge(hidden_ready, lin(n0 + s, (b, RAWS)))
                    V.tensor_tensor(HF, SG, SG, ALU.mult).then_inc(hf_ready, 1)
                    dve.wait_ge(mh_ready, lin(n0 + s + 1, (b, RAWS)))
                    V.tensor_tensor(pair(ml, i), HF, pair(mh, i).bitcast(F32), ALU.subtract).then_inc(hidden_ready, 1)
                run_units(dve, ph, one)

            def pair(t, i):
                return t[:, :, :].rearrange("p (i a) t -> p i (a t)", a=2)[:, i]

            def gate_unit(ph, n0):
                def one(b, s):
                    split_ahead(ph, b, s)
                    if s % 2 == 1:
                        filled(ph, b, s)
                        dve.wait_ge(drained_act, lin(ph.da0 + s // 2 + 1, (b, 2)))
                        dve.wait_ge(hidden_ready, lin(n0 + s // 2, (b, 2)))
                        V.tensor_tensor(HF, SG, ps[:, s, :], ALU.mult).then_inc(hf_ready, 1)
                        dve.wait_ge(mh_ready, lin(n0 + s // 2 + 1, (b, 2)))
                        i = lin(s // 2, (b, 2))
                        V.tensor_tensor(pair(ml, i), HF, pair(mh, i).bitcast(F32),
                                        ALU.subtract).then_inc(hidden_ready, 1)
                        V.sem_inc(drained_dve, 1)
                return one

            def job_unit(ph, n0, j):
                def one(b, s):
                    if s % 2 == 0:
                        split_ahead(ph, b, s, j)
                        return
                    first = isinstance(b, int) and b == 0 and s == 1

                    def times():
                        filled(ph, b, s, j)
                        dve.wait_ge(drained_act, lin(ph.da0 + s // 2 + 1, (b, 2), (j, ph.da_e)))
                        dve.wait_ge(turned, lin(1 if first else s // 2, (b, 2), (j, 11)))
                        V.tensor_tensor(HF2[:, s // 2, :], SG[:, 0:256], ps[:, s, 0:256], ALU.mult).then_inc(hf_ready, 1)
                        dve.wait_ge(hf_ready, lin(n0 + s // 2 + 1, (b, 2), (j, 11)))
                        V.sem_inc(drained_dve, 1)
                    if isinstance(b, int) and RAWS * b + s == ph.n - 1:
                        times()
                        split_ahead(ph, b, s, j)
                    else:
                        split_ahead(ph, b, s, j, between=times)
                    if not first:
                        rest(lin(s // 2 - 1, (b, 2)), 4 + (s // 2 + 1) % 2, n0, j)
                return one

            def rest(i, bank, n0, j):
                dve.wait_ge(mh_ready, lin(n0 + i + 1, (j, 11)))
                V.tensor_tensor(pair(jml, i), ps[:, bank, 0:256], pair(jmh, i).bitcast(F32),
                                ALU.subtract).then_inc(hidden_ready, 1)

            dve.wait_ge(pos_in, 16)
            dve.wait_ge(par_in, 16)
            link(V.tensor_copy(cosr[:], pos[:]))
            link(V.tensor_scalar(cosr[:], cosr[:], col("invf"), None, ALU.mult))
            two_pi = 2 * np.pi
            parts, left = [], two_pi
            for bits in (2 ** 5, 2 ** 13, 2 ** 21):
                v = float(np.floor(left * bits) / bits)
                parts.append(v)
                left -= v
            parts.append(float(left))
            magic = float(1.5 * 2 ** 23)
            for dst, shift in ((std, 0.25), (rstd, 0.0)):
                link(V.tensor_scalar(sinr[:], cosr[:], float(1 / two_pi), shift, ALU.mult, ALU.add))
                link(V.tensor_scalar(sinr[:], sinr[:], magic, None, ALU.add))
                link(V.tensor_scalar(sinr[:], sinr[:], -magic, None, ALU.add))
                link(V.scalar_tensor_tensor(dst[:], sinr[:], -parts[0], cosr[:], ALU.mult, ALU.add))
                for v in parts[1:]:
                    link(V.scalar_tensor_tensor(dst[:], sinr[:], -v, dst[:], ALU.mult, ALU.add))
                if shift:
                    link(V.tensor_scalar(dst[:], dst[:], float(np.pi / 2), None, ALU.add))
                link(V.tensor_scalar(dst[:], dst[:], 3.1415925, -3.1415925, ALU.min, ALU.max))
            V.sem_inc(trig_arg, 1)
            dve.wait_ge(c_act, 2)
            V.tensor_tensor(CL, cf[:].unsqueeze(2).broadcast_to([P, KT, P]), CH.bitcast(F32),
                            ALU.subtract).then_inc(moving, 1)
            dve.wait_ge(consts_in, 16)
            split(PH["ada0"], 0, 0)
            split(PH["ada0"], 0, 1)
            for l in range(2):
                def ada_out(b, s, bank, l=l):
                    return V.tensor_tensor(DG[l][:, lin(s, (b, RAWS))],
                                           bank[:, 0:2 * P].rearrange("p (m c) -> p m c", m=2),
                                           ident.unsqueeze(1).broadcast_to([P, 2, P]), ALU.mult)
                columns(f"ada{l}", ada_out)
                if l == 0:
                    dve.wait_ge(x_in, 16)
                    V.sem_inc(src_ready, 4)
                    rest_of(x)
                    dve.wait_ge(drained_dve, PH["ada1"].dd0)
                    link(V.tensor_reduce(ada[:, 0, :], DG[0].rearrange("p i m c -> p (i m) c"), AX.X, ALU.add))

            def modulation(i):
                if i == 0:
                    dve.wait_ge(drained_dve, PH["aqk"].dd0)
                link(V.tensor_reduce(ada[:, 1, 6 * i:6 * i + 6],
                                     DG[1][:, 3 * i:3 * i + 3].rearrange("p i m c -> p (i m) c"), AX.X, ALU.add))
                if i == 7:
                    for l in range(2):
                        link(V.tensor_tensor(ada[:, l, :], ada[:, l, :],
                                             pr[:, PCOL[f"bada_{l}"]:PCOL[f"bada_{l}"] + 48], ALU.add))
                        for o in (8, 32):
                            link(V.tensor_scalar(ada[:, l, o:o + 8], ada[:, l, o:o + 8], 1.0, None, ALU.add))

            def rope(ntiles, k0):
                for i in range(ntiles // 2):
                    dve.wait_ge(swapped, k0 + i + 1)
                    if k0 + i:
                        dve.wait_ge(roped, k0 + i)
                    link(V.tensor_tensor(RT.rearrange("p (a t) -> p a t", a=2),
                                         ps[:, i % 8, :].rearrange("p (a t) -> p a t", a=2),
                                         SINA.unsqueeze(1).broadcast_to([P, 2, S]), ALU.mult))
                    dve.wait_ge(cos_done, k0 + i + 1)
                    V.tensor_tensor(QK[:, 2 * i:2 * i + 2, :].rearrange("p a t -> p (a t)"), RC[:, i % 2, :], RT,
                                    ALU.add).then_inc(roped, 1)

            def attention(groups, masks, g0):
                G = len(masks)

                def maxima(i):
                    sc, q, b = SS[i % 3], st[:, 8 * (i % 3):8 * (i % 3) + 8], turned_bank(G, i)
                    dve.wait_ge(qk_done, g0 + i + 1)
                    if i >= 3:
                        dve.wait_ge(pt_done, g0 + i - 2)
                    V.tensor_tensor(sc[:, 0:G, :], ps[:, b:b + G, 0:TRI], MASK[:, masks[0]:masks[0] + G, :],
                                    ALU.add).then_inc(masked, 1)
                    dve.wait_ge(masked, g0 + i + 1)
                    V.tensor_reduce(q[:, 2:3], sc[:, 0:G, 0:128], AX.XY, ALU.max)
                    link(V.tensor_reduce(q[:, 3:4], sc[:, 0:G, 128:384], AX.XY, ALU.max))
                    V.tensor_scalar(q[:, 0:2], q[:, 2:4], -QSCALE, None, ALU.mult).then_inc(mx_ready, 1)

                def probabilities(i):
                    sc, q = SS[i % 3], st[:, 8 * (i % 3):8 * (i % 3) + 8]
                    dve.wait_ge(exp_done, g0 + i + 1)
                    link(V.reciprocal(q[:, 6:8], q[:, 4:6]))
                    V.tensor_scalar(sc[:, 0:G, 0:128], sc[:, 0:G, 0:128], q[:, 6:7], None, ALU.mult)
                    V.tensor_scalar(sc[:, 0:G, 128:384], sc[:, 0:G, 128:384], q[:, 7:8], None,
                                    ALU.mult).then_inc(p_ready, 1)
                maxima(0)
                for i in range(groups):
                    if i + 1 < groups:
                        maxima(i + 1)
                    probabilities(i)

            def add_residual(b, s, bank):
                xv = x[:].rearrange("p (i a) t -> p i (a t)", a=2)[:, lin(s, (b, RAWS))]
                return V.scalar_tensor_tensor(xv, xv, ALPHA, bank, ALU.mult, ALU.add)

            def first_half(m, bank):
                return V.scalar_tensor_tensor(x[:, m, :], x[:, m, :], ALPHA, bank, ALU.mult, ALU.add)

            def second_half(m, bank):
                return V.tensor_tensor(x[:, m, :], x[:, m, :], bank, ALU.add)

            columns("aqk", extra=modulation)
            columns("av")
            rope(16, 0)
            attention(16, [0], 0)
            rest_of(SRC)
            columns("ao", add_residual)
            layer_norm("lnA0g", "lnA0b")
            relu_phase("ain0")
            rows("aout0", first_half)
            relu_phase("ain1")
            dve.wait_ge(drained_dve, PH["ain1"].dd0)
            rows("aout1", second_half)
            layer_norm("lnA1g", "lnA1b")
            columns("bqk")
            columns("bv")
            rope(12, 8)
            attention(4, [1, 2, 3], 16)
            rest_of(SRC, 6)
            rows("bo", first_half)
            layer_norm("lnA2g", "lnA2b")
            relu_phase("bin0")
            rows("bout0", first_half)
            relu_phase("bin1")
            rows("bout1", second_half)
            layer_norm_modulated("lnA3g", "lnA3b", 0, 0)

            taps = [0]
            for l in range(2):
                V.memset(U[:, :, 0:TAPS - 1], 0.0)
                columns(f"pb{l}")

                def gated(b, s, bank):
                    i = lin(s, (b, RAWS))
                    cv = CV.rearrange("p (i a) t -> p i a t", a=2)[:, i]
                    uv = U.rearrange("p (i a) t -> p i a t", a=2)[:, i]
                    return V.tensor_tensor(uv[:, :, TAPS - 1:PADW], cv, bank.rearrange("p (a t) -> p a t", a=2),
                                           ALU.mult)
                columns(f"pa{l}", gated)
                wv = pr[:, PCOL[f"wdw_{l}"]:PCOL[f"wdw_{l}"] + KT * TAPS].rearrange("p (j k) -> p k j", k=TAPS)
                base = taps[0]

                def tap(i, tiles=range(KT), wv=wv, base=base, l=l):
                    for j in tiles:
                        if isinstance(i, int) and i == 0:
                            ins = V.tensor_scalar(CV[:, j, :], U[:, j, 0:S], wv[:, 0, j:j + 1], col(f"bdw_{l}", j),
                                                  ALU.mult, ALU.add)
                        else:
                            dve.wait_ge(tap_done, lin(base + j + 1 - KT, (i, KT)))
                            ins = V.scalar_tensor_tensor(CV[:, j, :], U[:, j, bass.ds(i, S)],
                                                         wv[:, i, j:j + 1], CV[:, j, :], ALU.mult, ALU.add)
                        ins.then_inc(tap_done, 1)
                dve.wait_ge(drained_dve, PH[f"pqk{l}"].dd0)
                tap(0)
                off = 1
                for nm in (f"pqk{l}", f"pv{l}", f"prg{l}"):
                    columns(nm, extra=lambda i, off=off: tap(lin(off, (i, 1))))
                    off += PH[nm].n
                columns(f"pgc{l}", extra=lambda i, off=off: tap(off + i) if i < 3 else None)
                dve.wait_ge(decay_in, 16 * (l + 1))
                for h in range(RET_HEADS):
                    dve.wait_ge(st_done, 4 * l + h + 1)
                    V.tensor_tensor(RST[:, h, :], ps[:, 4 + h, 0:TRI], DEC[:, h, :], ALU.mult).then_inc(st_decayed, 1)
                tap(TAPS - 3)
                tap(TAPS - 2)
                sv = st[:, 16:64].rearrange("p (i c) -> p i c", c=6)
                mv = st[:, 64:80].rearrange("p (i c) -> p i c", c=2)

                def statistics(u, l=l):
                    for i in (2 * u, 2 * u + 1):
                        dve.wait_ge(o_copied, 8 * l + i + 1)
                        last = V.bn_stats(sv[:, i], ON[:, i // 2, i % 2, :])
                    link(last)
                    tap(TAPS - 1, (2 * u, 2 * u + 1))
                columns(f"pgr{l}", extra=statistics)
                taps[0] += KT * TAPS
                for i in range(8):
                    last = V.bn_aggr(mv[:, i], sv[:, i])
                last.then_inc(ovar, 1)
                dve.wait_ge(ostd, l + 1)
                link(V.reciprocal(st[:, 88:96], st[:, 80:88]))

                def norm_o(l=l):
                    for i in range(8):
                        V.tensor_scalar(ON[:, i // 2, i % 2, :], ON[:, i // 2, i % 2, :], mv[:, i, 0:1],
                                        st[:, 88 + i:89 + i], ALU.subtract, ALU.mult).then_inc(o_normed, 1)

                def gate(pairs, l=l):
                    for i in pairs:
                        dve.wait_ge(g_turned, 8 * l + i + 1)
                        rg = RG[:, 2 * i:2 * i + 2, :].rearrange("p a t -> p (a t)")
                        V.tensor_tensor(rg, rg, ps[:, 4 + i % 4, :], ALU.mult).then_inc(hf_ready, 1)
                normed(CV, between=norm_o)
                for c in range(4):
                    v = CV[:, 2 * c:2 * c + 2, :]
                    V.tensor_tensor(v, v, rstd[:].unsqueeze(1).broadcast_to([P, 2, S]), ALU.mult).then_inc(u_ready, 1)
                gate(range(4))
                rest_of(SRC)

                def gated_rest(u):
                    gate((4 + u,))
                    for i in (2 * u, 2 * u + 1):
                        dve.wait_ge(mh_ready, nl[0] + i + 1)
                        V.tensor_tensor(ml[:, 2 * i:2 * i + 2, :], RG[:, 2 * i:2 * i + 2, :],
                                        mh[:, 2 * i:2 * i + 2, :].bitcast(F32), ALU.subtract).then_inc(hidden_ready, 1)

                def conv_gate(b, s, bank):
                    v = GC.rearrange("p (i a) t -> p i (a t)", a=2)[:, lin(s, (b, RAWS))]
                    return V.tensor_tensor(v, v, bank, ALU.mult)
                columns(f"co{l}", conv_gate, gated_rest)
                nl[0] += 8
                rows(f"ro{l}", lambda m, bank: V.tensor_tensor(GR[:, m, :], GR[:, m, :], bank, ALU.mult))
                dve.wait_ge(drained_dve, PH[f"wo{l}"].dd0)
                for c in range(5):
                    if c < 4:
                        v = slice(2 * c, 2 * c + 2)
                        V.tensor_tensor(SRC[:, v, :], GR[:, v, :], GC[:, v, :], ALU.add).then_inc(src_ready, 1)
                    if c > 0:
                        rest_chunk(SRC, c - 1)
                link(V.tensor_scalar(x[:], x[:], ALPHA, None, ALU.mult))

                def gated_add(which):
                    def go(m, bank):
                        g = ada[:, l, 24 * which + 16 + m:24 * which + 17 + m]
                        return V.scalar_tensor_tensor(x[:, m, :], bank, g, x[:, m, :], ALU.mult, ALU.add)
                    return go

                def mix_out(b, s, bank, l=l):
                    i = lin(s, (b, RAWS))
                    for a in range(2):
                        last = gated_add(0)(2 * i + a, bank[:, a * S:a * S + S])
                    return last
                columns(f"wo{l}", mix_out)
                x_done = layer_norm_modulated(f"ln1_{l}g", f"ln1_{l}b", l, 1)
                link(x_done)
                if l == 0:
                    run_units(dve, PH["gu0"], gate_unit(PH["gu0"], nl[0]))
                    nl[0] += 11
                    link(V.tensor_scalar(x[:], x[:], ALPHA, None, ALU.mult))
                    rows("dn0", gated_add(1))
                    layer_norm_modulated("ln2_0g", "ln2_0b", 1, 0)
                    continue
                V.memset(CUM, 0.0)
                V.memset(gt[:].bitcast(F32), 0.0)
                V.memset(YF, 0.0)
                V.memset(ACC, 0.0)
                dve.wait_ge(logits, 1)
                link(V.tensor_copy(LG, ps[:, 6, 0:16].rearrange("p (t e) -> p t e", t=2)))
                mx = st[:, 0:16].rearrange("p (t c) -> p t c", t=2)
                ixf = st[:, 16:32].rearrange("p (t c) -> p t c", t=2)
                for t in range(TT):
                    link(V.max(mx[:, t], LG[:, t]))
                    link(V.max_index(ix[:, 8 * t:8 * t + 8], mx[:, t], LG[:, t]))
                link(V.tensor_copy(st[:, 16:32], ix[:]))
                V.tensor_tensor(st[:, 32:34], mx[:, :, 1], mx[:, :, 0], ALU.subtract).then_inc(gap_ready, 1)
                dve.wait_ge(gap_exp, 1)
                link(V.tensor_scalar(st[:, 36:38], st[:, 34:36], 1.0, None, ALU.add))
                link(V.reciprocal(st[:, 38:40], st[:, 36:38]))
                link(V.tensor_tensor(st[:, 40:42], st[:, 38:40], st[:, 34:36], ALU.mult))
                i8, i16 = col("iota", 0, EXPERTS), col("iota", 0, JOBS)
                for t in range(TT):
                    V.tensor_scalar(SEL[:, t], i8, ixf[:, t, 0:1], None, ALU.is_equal)
                    V.tensor_scalar(SEL2[:, t], i8, ixf[:, t, 1:2], None, ALU.is_equal)
                    V.tensor_scalar(CMB[:, t], i8, ixf[:, t, 0:1], st[:, 38 + t:39 + t], ALU.is_equal, ALU.mult)
                    link(V.tensor_scalar(CMB2[:, t], i8, ixf[:, t, 1:2], st[:, 40 + t:41 + t], ALU.is_equal, ALU.mult))
                V.tensor_tensor(SEL, SEL, SEL2, ALU.add).then_inc(sel_ready, 1)
                V.tensor_tensor(CMB, CMB, CMB2, ALU.add)
                dve.wait_ge(ranked, 1)
                link(V.tensor_scalar(POS, ps[:, 5, 0:16].rearrange("p (t e) -> p t e", t=2), float(D), 1000.0,
                                     ALU.mult, ALU.add))
                link(V.tensor_tensor(POS, POS, SEL, ALU.mult))
                link(V.tensor_scalar(POS, POS, -1000.0, None, ALU.add))

                def gather_matrix(slots):
                    for t in range(TT):
                        last = V.tensor_scalar(gx[:, t, :], col("iota", 0, BLK), slots(t), None, ALU.is_equal)
                    last.then_inc(g_ready, 1)

                def gathered(j):
                    for q in range(2):
                        dve.wait_ge(xg_hi, lin(q + 1, (j, 2)))
                        V.tensor_tensor(xl[:, 4 * q:4 * q + 4, 0:BLK],
                                        ps[:, 6 + q, :].rearrange("p (k t) -> p k t", k=4),
                                        xh[:, 4 * q:4 * q + 4, 0:BLK].bitcast(F32), ALU.subtract).then_inc(xg_lo, 1)

                gather_matrix(lambda t: POS[:, t, 0:1])
                link(V.tensor_scalar(CNT, ps[:, 5, 16:24], float(BLK) / D, 1.0, ALU.is_gt, ALU.add))
                link(V.tensor_copy(CUM[:, 0, 4:12], CNT))
                for i, d in enumerate((1, 2, 4)):
                    link(V.tensor_tensor(CUM[:, i + 1, 4:12], CUM[:, i, 4:12], CUM[:, i, 4 - d:12 - d], ALU.add))
                cum = CUM[:, 3, 4:12]

                def each_job(v):
                    return v.unsqueeze(2).broadcast_to([P, EXPERTS, JOBS])

                def each_expert(v):
                    return v.unsqueeze(1).broadcast_to([P, EXPERTS, JOBS])
                link(V.tensor_tensor(MJ[:, 0], each_expert(i16), each_job(cum), ALU.is_ge))
                link(V.tensor_tensor(MJ[:, 1], MJ[:, 0], each_job(CNT), ALU.mult))
                V.tensor_reduce(EXPJ, MJ[:, 0].rearrange("p e j -> p j e"), AX.X, ALU.add)
                link(V.tensor_reduce(STARTJ, MJ[:, 1].rearrange("p e j -> p j e"), AX.X, ALU.add))
                V.tensor_copy(ji[:, JOBS:JOBS + 1], cum[:, 7:8])
                V.tensor_copy(ji[:, 0:JOBS], EXPJ).then_inc(jobs_ready, 1)
                gathered(0)
                link(V.tensor_tensor(STARTJ, i16, STARTJ, ALU.subtract))
                link(V.tensor_tensor(ISJ, each_expert(EXPJ), each_job(i8), ALU.is_equal))
                for t in range(TT):
                    V.tensor_tensor(MJ[:, t], ISJ, each_job(POS[:, t]), ALU.mult)
                    last = V.tensor_tensor(MJ[:, 2 + t], ISJ, each_job(CMB[:, t]), ALU.mult)
                link(last)
                V.tensor_reduce(PJ, MJ[:, 0:2].rearrange("p t e j -> p t j e"), AX.X, ALU.add)
                link(V.tensor_reduce(CJ, MJ[:, 2:4].rearrange("p t e j -> p t j e"), AX.X, ALU.add))
                for t in range(TT):
                    last = V.scalar_tensor_tensor(PJ[:, t], STARTJ, -float(BLK), PJ[:, t], ALU.mult, ALU.add)
                link(last)
                def add_scattered(j, quarters=range(4)):
                    av = ACC.rearrange("p (q a) t -> p q (a t)", a=2)
                    for q in quarters:
                        dve.wait_ge(sc_filled, lin(q + 1, (j, 4)))
                        V.tensor_tensor(av[:, q], av[:, q], ps[:, 6 + q % 2, :], ALU.add).then_inc(sc_added, 1)
                n0 = nl[0]
                n_jobs = dve.value_load(ji[0:1, JOBS:JOBS + 1], min_val=EXPERTS, max_val=JOBS - 1)
                gu, dn = PH["gu1"], PH["dn1"]
                with dve.Fori(0, n_jobs) as j:
                    one = job_unit(gu, n0, j)

                    def middle():
                        add_scattered(j, (2, 3))
                        dve.wait_ge(gt_filled, j + 1)
                        gather_matrix(lambda t: PJ[:, t, bass.ds(j + 1, 1)])
                    job_units(dve, gu, one, {2: lambda: add_scattered(j, (0, 1)), 3: middle})
                    gathered(j + 1)
                    rest(FT // 2 - 1, 2, n0, j)
                    run_units(dve, dn, lambda b, s: split_ahead(dn, b, s, j))
                add_scattered(n_jobs)
                dve.wait_ge(sc_added, n_jobs * 4 + 4)
                link(V.tensor_scalar(x[:], x[:], ALPHA, None, ALU.mult))
                for m in range(KT):
                    last = gated_add(1)(m, ACC[:, m, :])
                last.then_inc(ln_in, 1)
                normed(x[:])
                for j in range(KT):
                    last = V.scalar_tensor_tensor(x[:, j, :], x[:, j, :], col("ln2_1g", j), rstd[:], ALU.mult, ALU.mult)
                link(last)
                for j in range(KT):
                    last = V.tensor_scalar(x[:, j, :], x[:, j, :], col("ln2_1b", j), None, ALU.add)
                last.then_inc(final, 1)

        @block.tensor
        def _(pe):
            mm = nc.tensor.matmul

            def three(out, w, m, start, stop):
                (w_h, w_l), (m_h, m_l) = w, m
                mm(out, w_l, m_h, start=start, stop=False)
                mm(out, w_h, m_l, start=False, stop=False)
                return mm(out, w_h, m_h, start=False, stop=stop)

            def split_ready(ph, b, s, half, e):
                pe.wait_ge(lo_split, unit_no(ph, b, s, e, 2, half + 1))

            def columns(ph, kind, bank_free, e=0, moving_op=None, between=None, after=None, tiles=TT):
                mhh, mll = moving_op or (xh, xl)
                base, soon[0] = soon[0], None

                def one(b, s):
                    bank_free(b, s)
                    if kind == "N":
                        w_h = wh[:, s % 2, :].rearrange("p (k c) -> p k c", k=KT)
                        w_l = wl[:, s % 2, :].rearrange("p (k c) -> p k c", k=KT)
                        for t in range(tiles):
                            for k in range(KT):
                                if t == 0 and k % 4 == 0:
                                    split_ready(ph, b, s, k // 4, e)
                                tok = slice(t * P, t * P + P)
                                o = ps[:, s, t * 256:t * 256 + 256]
                                mm(o, mll[:, k, tok], w_h[:, k, :], start=k == 0, stop=False)
                                mm(o, mhh[:, k, tok], w_l[:, k, :], start=False, stop=False)
                                last = mm(o, mhh[:, k, tok], w_h[:, k, :], start=False, stop=k == KT - 1)
                                if t == tiles - 1 and k % 4 == 3:
                                    last.then_inc(consumed, 1)
                        if after is not None:
                            after(b, s)
                        return
                    w_h = wh[:, s % 2, :].rearrange("p (m k c) -> p m k c", m=2, k=KT)
                    w_l = wl[:, s % 2, :].rearrange("p (m k c) -> p m k c", m=2, k=KT)
                    split_ready(ph, b, s, 0, e)
                    n = mhh.shape[2]
                    for m in range(2):
                        if m:
                            split_ready(ph, b, s, 1, e)
                        for k in range(KT):
                            if base is not None and isinstance(b, int) and b == s == m == 0 and k % 2 == 0:
                                pe.wait_ge(moving, base + k // 2 + 1)
                            last = three(ps[:, s, m * n:m * n + n], (w_h[:, m, k, :], w_l[:, m, k, :]),
                                         (mhh[:, k, 0:n], mll[:, k, 0:n]), k == 0, k == KT - 1)
                        last.then_inc(consumed, 1)
                    if after is not None:
                        after(b, s)
                if between is not None:
                    job_units(pe, ph, one, between)
                elif base is not None:
                    for i in range(ph.n):
                        one(i // RAWS, i % RAWS)
                else:
                    run_units(pe, ph, one, 0)

            def rows(ph, need, e=0, hidden=True, bank_free=None):
                mhh, mll = (mh, ml) if hidden else (xh, xl)
                last_unit = ph.n - 1

                def one(b, s):
                    w_h = wh[:, s % 2, :].rearrange("p (k m c) -> p k m c", k=2, m=KT)
                    w_l = wl[:, s % 2, :].rearrange("p (k m c) -> p k m c", k=2, m=KT)
                    need(b, s)
                    for kk in range(2):
                        split_ready(ph, b, s, kk, e)
                        kt = lin(2 * s + kk, (b, 2 * RAWS))
                        st0 = isinstance(b, int) and b == 0 and s == 0 and kk == 0
                        sp0 = isinstance(b, int) and RAWS * b + s == last_unit and kk == 1
                        for m in range(KT):
                            bank = ROW_M.index(m)
                            if st0 and bank_free is not None and bank < 4:
                                bank_free(bank)
                            last = three(ps[:, bank, 0:S], (w_h[:, kk, m, :], w_l[:, kk, m, :]),
                                         (mhh[:, kt, :], mll[:, kt, :]), st0, sp0)
                        last.then_inc(consumed, 1)
                for i in range(ph.n):
                    one(i // RAWS, i % RAWS)

            def by_act(ph, before=None):
                def go(b, s):
                    if not isinstance(b, int) or b == 0:
                        if before == "dve":
                            pe.wait_ge(drained_dve, ph.dd0 + s - 3)
                    pe.wait_ge(drained_act, lin(ph.da0 + s - 3, (b, RAWS)))
                return go

            def by_dve(ph, before=None):
                def go(b, s):
                    if not isinstance(b, int) or b == 0:
                        if before == "act":
                            pe.wait_ge(drained_act, ph.da0 + s - 3)
                    pe.wait_ge(drained_dve, lin(ph.dd0 + s - 3, (b, RAWS)))
                return go

            def all_free(ph, e=0):
                pe.wait_ge(drained_act, lin(ph.da0, (e, ph.da_e)))
                pe.wait_ge(drained_dve, lin(ph.dd0, (e, ph.dd_e)))

            def proj(name, by, kind="T", before=None, after=None):
                ph = PH[name]
                if before is None:
                    all_free(ph)
                columns(ph, kind, by(ph, before), after=after)

            hid = [0]

            def relu_phase(name, after_rows=False):
                ph = PH[name]
                if not after_rows:
                    all_free(ph)
                h0 = hid[0]
                hid[0] += ph.n

                def bank(b, s):
                    if after_rows and (not isinstance(b, int) or b == 0):
                        pe.wait_ge(drained_dve, ph.dd0 - 8 + s + 1)
                    if not isinstance(b, int) or b > 0:
                        pe.wait_ge(nonlin, lin(nls[0] + s - 3, (b, RAWS)))
                columns(ph, "T", bank)
                nls[0] += ph.n
                return h0

            nls = [4]

            def out_phase(name, h0):
                ph = PH[name]
                pe.wait_ge(drained_dve, ph.dd0)
                rows(ph, lambda b, s: pe.wait_ge(hidden_ready, lin(h0 + s + 1, (b, RAWS))),
                     bank_free=lambda bank: pe.wait_ge(nonlin, nls[0] - 3 + bank))

            lns = [0]

            def layer_norm(src, ready, order=range(KT)):
                n = lns[0]
                lns[0] += 1
                for i, k in enumerate(order):
                    ready(i)
                    last = mm(ps[:, 4, 0:S], ones, src[:, k, :], start=i == 0, stop=i == KT - 1)
                last.then_inc(ln_mean, 1)
                for k in range(KT):
                    if k % 2 == 0:
                        pe.wait_ge(ln_sq, 4 * n + k // 2 + 1)
                    last = mm(ps[:, 5, 0:S], ones, SRC[:, k, :], start=k == 0, stop=k == KT - 1)
                last.then_inc(ln_var, 1)

            def after_columns(name):
                d = PH[name].dd0
                return lambda i: pe.wait_ge(drained_dve, d + i // 2 + 1) if i % 2 == 0 else None

            def after_rows(name):
                d = PH[name].dd0
                return lambda i: pe.wait_ge(drained_dve, d + max(i + 1, 6))

            mv = [1]
            soon = [None]

            def moving_ready(tiles=KT):
                mv[0] += tiles // 2
                pe.wait_ge(moving, mv[0])

            def moving_soon():
                soon[0] = mv[0]
                mv[0] += KT // 2

            def rope(ntiles, k0):
                pe.wait_ge(drained_act, PH["ao"].da0 if k0 == 0 else PH["bo"].da0)
                for i in range(ntiles // 2):
                    mm(ps[:, i % 8, :], swap, QK[:, 2 * i:2 * i + 2, :].rearrange("p a t -> p (a t)"),
                       start=True, stop=True).then_inc(swapped, 1)

            def attention(groups, heads_of, g0, h0, ktile0):
                G = len(heads_of(0))

                def scores(i):
                    b = turned_bank(G, i)
                    back = 2 if G == 1 else 1
                    if i >= back:
                        pe.wait_ge(masked, g0 + i - back + 1)
                    for k, h in enumerate(heads_of(i)):
                        r = slice(64 * (h % 2), 64 * (h % 2) + 64)
                        q, kk = QK[r, h // 2, :], QK[r, ktile0 + h // 2, :]
                        mm(ps[:, b + k, 0:128], q[:, 0:128], kk[:, 0:128], start=True, stop=True)
                        last = mm(ps[:, b + k, 128:384], q[:, 128:256], kk[:, 0:256], start=True, stop=True)
                    last.then_inc(qk_done, 1)

                scores(0)
                scores(1)
                for i in range(groups):
                    if i + 2 < groups:
                        scores(i + 2)
                    pe.wait_ge(p_ready, g0 + i + 1)
                    b = 3 + turned_bank(G, i)
                    for k in range(G):
                        for c in range(3):
                            last = nc.tensor.transpose(ps[:, b + k, c * P:c * P + P],
                                                       SS[i % 3][:, k, c * P:c * P + P], ident)
                    last.then_inc(pt_done, 1)
                    pe.wait_ge(pt_copied, g0 + i + 1)
                    pt = PT[i % 2]
                    for k, h in enumerate(heads_of(i)):
                        n = h0 + i * G + k
                        if n >= 2:
                            pe.wait_ge(ao_copied, n - 1)
                        r = slice(64 * (h % 2), 64 * (h % 2) + 64)
                        v0, v1 = VN[:, 0, h * 64:h * 64 + 64], VN[:, 1, h * 64:h * 64 + 64]
                        mm(ps[r, 6 + n % 2, 0:128], v0, pt[:, k, 0:128], start=True, stop=True)
                        mm(ps[r, 6 + n % 2, 128:256], v0, pt[:, k, 128:256], start=True, stop=False)
                        mm(ps[r, 6 + n % 2, 128:256], v1, pt[:, k, 256:384], start=False,
                           stop=True).then_inc(pv_done, 1)

            pe.wait_ge(consts_in, 16)
            pe.wait_ge(moving, 1)
            for l in range(2):
                ph = PH[f"ada{l}"]
                all_free(ph)
                columns(ph, "N", by_dve(ph), moving_op=(CH, CL), tiles=1)

            moving_ready()
            proj("aqk", by_act)
            proj("av", by_act, "N", before="act")
            rope(16, 0)
            pe.wait_ge(roped, 8)
            attention(16, lambda i: [i], 0, 0, 8)
            moving_soon()
            proj("ao", by_dve)
            layer_norm(x, after_columns("ao"))
            moving_soon()
            h0 = relu_phase("ain0")
            out_phase("aout0", h0)
            h0 = relu_phase("ain1", True)
            out_phase("aout1", h0)
            layer_norm(x, after_rows("aout1"), ROW_M)
            moving_soon()
            proj("bqk", by_act)
            proj("bv", by_act, "N")
            rope(12, 8)
            pe.wait_ge(roped, 14)
            attention(4, lambda j: [j, 4 + j, 8 + j], 16, 16, 6)
            moving_ready(6)
            ph = PH["bo"]
            all_free(ph)
            rows(ph, lambda b, s: None, hidden=False)
            layer_norm(x, after_rows("bo"), ROW_M)
            moving_soon()
            h0 = relu_phase("bin0")
            out_phase("bout0", h0)
            h0 = relu_phase("bin1", True)
            out_phase("bout1", h0)
            layer_norm(x, after_rows("bout1"), ROW_M)

            for l in range(2):
                moving_soon()
                proj(f"pb{l}", by_act)
                proj(f"pa{l}", by_dve, before="act")
                proj(f"pqk{l}", by_act, before="dve")
                proj(f"pv{l}", by_act, "N", before="act")
                proj(f"prg{l}", by_act, before="act")
                proj(f"pgc{l}", by_act, before="act")
                pe.wait_ge(ret_roped, l + 1)
                pe.wait_ge(drained_act, PH[f"prg{l}"].da0)
                for h in range(RET_HEADS):
                    for a in range(2):
                        mm(ps[:, 4 + h, 0:256], RK[:, 2 * h + a, 0:128], RQ[:, 2 * h + a, :], start=a == 0, stop=a == 1)
                    for a in range(2):
                        last = mm(ps[:, 4 + h, 256:384], RK[:, 2 * h + a, 128:256], RQ[:, 2 * h + a, 128:256],
                                  start=a == 0, stop=a == 1)
                    last.then_inc(st_done, 1)
                for i in range(8):
                    g = i // 2
                    if i < 4:
                        pe.wait_ge(st_decayed, 4 * l + i + 1)
                    else:
                        pe.wait_ge(o_copied, 8 * l + i - 3)
                    va, vb = (RV[:, t, g * RET_DV:(g + 1) * RET_DV] for t in range(TT))
                    s_ = RST[:, g, :]
                    if i % 2 == 0:
                        mm(ps[:, 4 + i % 4, :], s_[:, 0:128], va, start=True, stop=True).then_inc(o_done, 1)
                    else:
                        mm(ps[:, 4 + i % 4, :], s_[:, 128:256], va, start=True, stop=False)
                        mm(ps[:, 4 + i % 4, :], s_[:, 256:384], vb, start=False, stop=True).then_inc(o_done, 1)
                proj(f"pgr{l}", by_act, before="act")

                def turn_o(pairs, l=l):
                    for i in pairs:
                        h, dd = i // 2, i % 2
                        pe.wait_ge(o_normed, 8 * l + 2 * h + 2)
                        if i >= 4:
                            pe.wait_ge(hf_ready, ro0 + i - 3)
                        for a in range(2):
                            for t in range(TT):
                                last = nc.tensor.transpose(
                                    ps[:, 4 + i % 4, a * S + t * P:a * S + t * P + P],
                                    ON[:, h, t, (2 * dd + a) * P:(2 * dd + a) * P + P], ident)
                        last.then_inc(g_turned, 1)
                pe.wait_ge(o_copied, 8 * l + 8)
                ro0 = hid[0]
                hid[0] += 8
                layer_norm(CV, lambda i, l=l: pe.wait_ge(tap_done, KT * TAPS * (l + 1) - KT + i + 1))
                pe.wait_ge(ln_std, lns[0])
                turn_o(range(4))
                moving_soon()
                proj(f"co{l}", by_dve, after=lambda b, s: turn_o((4 + s,)))
                pe.wait_ge(hf_ready, ro0 + 8)
                rows(PH[f"ro{l}"], lambda b, s: pe.wait_ge(hidden_ready, ro0 + RAWS * b + s + 1),
                     bank_free=lambda bank, d=PH[f"ro{l}"].dd0: pe.wait_ge(drained_dve, d - 3 + bank))
                moving_soon()
                proj(f"wo{l}", by_dve)
                layer_norm(x, after_columns(f"wo{l}"))
                moving_ready()

                def gate_banks(ph, e=0):
                    def bank(b, s):
                        if isinstance(b, int) and b == 0:
                            return
                        if s % 2 == 0:
                            pe.wait_ge(drained_act, lin(ph.da0 + s // 2 - 1, (b, 2), (e, ph.da_e)))
                        else:
                            pe.wait_ge(drained_dve, lin(ph.dd0 + s // 2 - 1, (b, 2), (e, ph.dd_e)))
                    return bank

                if l == 0:
                    all_free(PH["gu0"])
                    columns(PH["gu0"], "T", gate_banks(PH["gu0"]))
                    h0 = hid[0]
                    rows(PH["dn0"], lambda b, s: pe.wait_ge(hidden_ready, h0 + RAWS * b + s + 1),
                         bank_free=lambda bank: all_free(PH["dn0"]) if bank == 0 else None)
                    hid[0] += 11
                    layer_norm(x, after_rows("dn0"), ROW_M)
                else:
                    for t in range(TT):
                        for k in range(KT):
                            last = mm(ps[:, 6, 8 * t:8 * t + 8], SRC[:, k, t * P:t * P + P],
                                      pr[:, PCOL["wr"] + 8 * k:PCOL["wr"] + 8 * k + 8], start=k == 0, stop=k == KT - 1)
                    last.then_inc(logits, 1)
                    all_free(PH["gu1"])
                    for i in range(4):
                        for c in range(4):
                            last = nc.tensor.transpose(ps[:, i, c * P:c * P + P],
                                                       SRC[:, i % 2 * 4 + c, i // 2 * P:i // 2 * P + P], ident)
                        last.then_inc(h_turned, 1)
                    tri = cs[:, 3, :]
                    pe.wait_ge(sel_ready, 1)
                    mm(ps[:, 5, 0:8], tri, SEL[:, 0], start=True, stop=True)
                    mm(ps[:, 5, 8:16], ones, SEL[:, 0], start=True, stop=False)
                    mm(ps[:, 5, 8:16], tri, SEL[:, 1], start=False, stop=True)
                    mm(ps[:, 5, 16:24], ones, SEL[:, 0], start=True, stop=False)
                    mm(ps[:, 5, 16:24], ones, SEL[:, 1], start=False, stop=True).then_inc(ranked, 1)

                    def gather(j):
                        pe.wait_ge(g_ready, j + 1)
                        for q in range(2):
                            for a in range(4):
                                f = slice((4 * q + a) * P, (4 * q + a) * P + P)
                                o = ps[:, 6 + q, a * P:a * P + P]
                                mm(o, hn[:, 0, f], gx[:, 0, :], start=True, stop=False)
                                last = mm(o, hn[:, 1, f], gx[:, 1, :], start=False, stop=True)
                            last.then_inc(xg_filled, 1)

                    def turn(i, bank, j):
                        pe.wait_ge(hf_ready, lin(h0 + i + 1, (j, 11)))
                        if isinstance(i, int) and i == 0:
                            pe.wait_ge(yf_done, j + 1)
                        elif not (isinstance(i, int) and i == 1):
                            pe.wait_ge(hidden_ready, lin(h0 + i - 1, (j, 11)))
                        for a in range(2):
                            last = nc.tensor.transpose(ps[:, bank, a * P:a * P + P],
                                                       HF2[:, bank % 2, a * P:a * P + P], ident)
                        last.then_inc(turned, 1)

                    def scatter(j, quarters=range(4)):
                        pe.wait_ge(y_split, j + 1)
                        for q in quarters:
                            if q >= 2:
                                pe.wait_ge(sc_added, lin(q - 1, (j, 4)))
                            for a in range(2):
                                o = ps[:, 6 + q % 2, a * S:a * S + S]
                                mm(o, xh[:, 2 * q + a, BLK:2 * BLK], gt[:], start=True, stop=False)
                                last = mm(o, xl[:, 2 * q + a, BLK:2 * BLK], gt[:], start=False, stop=True)
                            last.then_inc(sc_filled, 1)

                    h0 = hid[0]
                    pe.wait_ge(h_copied, 4)
                    gather(0)
                    pe.wait_ge(jobs_ready, 1)
                    n_jobs = pe.value_load(ji[0:1, JOBS:JOBS + 1], min_val=EXPERTS, max_val=JOBS - 1)
                    gu, dn = PH["gu1"], PH["dn1"]
                    h0 = hid[0]
                    with pe.Fori(0, n_jobs) as j:
                        pe.wait_ge(xg_hi, lin(2, (j, 2)))
                        pe.wait_ge(xg_lo, lin(2, (j, 2)))

                        def middle():
                            scatter(j, (2, 3))
                            pe.wait_ge(sc_added, lin(3, (j, 4)))
                            for t in range(TT):
                                nc.tensor.transpose(ps[:, 6, t * P:t * P + P], gx[:, t, :], ident)
                            for t in range(TT):
                                last = mm(ps[:, 6, S:S + 1], gx[:, t, :], CJ[:, t, bass.ds(j, 1)],
                                          start=t == 0, stop=t == TT - 1)
                            last.then_inc(gt_filled, 1)

                        def turn_before(b, s):
                            if s % 2 == 0 and not (isinstance(b, int) and b == 0 and s == 0):
                                turn(lin(s // 2 - 1, (b, 2)), 4 + (s // 2 + 1) % 2, j)
                        columns(gu, "N", gate_banks(gu, j), j, after=turn_before, tiles=1,
                                between={2: lambda: scatter(j, (0, 1)), 3: middle})
                        pe.wait_ge(gt_copied, j + 1)
                        pe.wait_ge(sc_added, lin(4, (j, 4)))
                        gather(j + 1)
                        turn(FT // 2 - 1, 2, j)
                        pe.wait_ge(hidden_ready, lin(h0 + 10, (j, 11)))
                        for i in range(dn.n):
                            b, s = i // RAWS, i % RAWS
                            w_h = wh[:, s % 2, :].rearrange("p (k h c) -> p k h c", k=2, h=2)
                            w_l = wl[:, s % 2, :].rearrange("p (k h c) -> p k h c", k=2, h=2)
                            if i == dn.n - 1:
                                pe.wait_ge(hidden_ready, lin(h0 + 11, (j, 11)))
                            for kk in range(2):
                                split_ready(dn, b, s, kk, j)
                                kt = 2 * i + kk
                                first, final_k = kt == 0, kt == FT - 1
                                for h in range(2):
                                    o = ps[:, 4 + h, :]
                                    mm(o, jml[:, kt, :], w_h[:, kk, h, :], start=first, stop=False)
                                    mm(o, jmh[:, kt, :], w_l[:, kk, h, :], start=False, stop=False)
                                    last = mm(o, jmh[:, kt, :], w_h[:, kk, h, :], start=False, stop=final_k)
                                last.then_inc(consumed, 1)
                    pe.wait_ge(xg_hi, n_jobs * 2 + 2)
                    pe.wait_ge(xg_lo, n_jobs * 2 + 2)
                    scatter(n_jobs)
                    layer_norm(x, lambda i: pe.wait_ge(ln_in, 1))


def col_units(w):
    n = w.shape[1] // 256
    return w.reshape(KT, P, n, 2, P).transpose(2, 1, 3, 0, 4).reshape(n, P, UNIT)


def col_units_n(w):
    n = w.shape[1] // 256
    return w.reshape(KT, P, n, 256).transpose(2, 1, 0, 3).reshape(n, P, UNIT)


def row_units(w):
    n = w.shape[0] // 256
    return w.reshape(n, 2, P, D).transpose(0, 2, 1, 3).reshape(n, P, UNIT)


def feat(v):
    return v.reshape(-1, P).T


def shape_constants():
    cs = np.zeros((P, 4, P), np.float32)
    cs[:, 0] = np.eye(P)
    cs[:, 1] = 1.0 / D
    cs[:, 3] = np.triu(np.ones((P, P)), 1) / D
    for h in range(2):
        for i in range(32):
            cs[64 * h + 32 + i, 2, 64 * h + i] = -1.0
            cs[64 * h + i, 2, 64 * h + 32 + i] = 1.0
    inv = (1.0 / (np.float32(10000.0) ** (np.arange(0, HEAD, 2, dtype=np.float32) / np.float32(HEAD)))).astype(np.float32)
    ang = (np.arange(S, dtype=np.float32)[:, None] * inv[None]).astype(np.float32)
    rows = np.arange(P) % 32
    cosa, sina = np.cos(ang).T[rows], np.sin(ang).T[rows]
    q, k = np.arange(S)[:, None], np.arange(S)[None]
    causal = k <= q
    seen = [causal, causal & (q - k <= 128), causal & ((q - k) % 4 == 0), causal & ((q - k) % 16 == 0)]
    masks = []
    for m in seen:
        a = np.where(m, 0.0, NEG).astype(np.float32)
        masks.append(np.concatenate([a[:P, :P], a[P:, :]], axis=1))
    block_a = np.concatenate(masks + [cosa, sina], axis=1).astype(np.float32)
    log_g = np.log1p(-np.exp2(-5.0 - np.arange(RET_HEADS)))
    dec = []
    for h in range(RET_HEADS):
        n, m = np.arange(S)[None], np.arange(S)[:, None]
        a = np.where(n >= m, np.exp(log_g[h] * np.maximum(n - m, 0)), 0.0) * RET_DK ** -0.5
        dec.append(np.concatenate([a[:P, :], a[P:, P:]], axis=1))
    decay = np.concatenate(dec, axis=1).astype(np.float32)
    invf = (np.float32(10000.0) ** (-np.arange(P, dtype=np.float32) / np.float32(P))).astype(np.float32)
    return cs, block_a, decay, invf


def kernel(**inputs):
    import concourse.bacc as _bacc
    from concourse.bass_utils import run_bass_kernel_spmd as _run

    a = {k: np.asarray(v) for k, v in inputs.items()}
    cs, block_a, decay, invf = shape_constants()

    ws = np.empty((TOTAL + LOOKAHEAD, P, UNIT), np.float32)

    def put(name, units, off=0):
        g = PH[name].g0 + off
        ws[g:g + len(units)] = units

    for l in range(2):
        put(f"ada{l}", col_units_n(a["w_ada_2"][l]))
    qkv, wo = a["moba_w_qkv"][0], a["moba_w_o"][0]
    put("aqk", col_units(qkv[:, :2 * D]))
    put("av", col_units_n(qkv[:, 2 * D:]))
    put("ao", col_units(wo))
    dq = a["dil_w_qkv"][0]
    put("bqk", col_units(dq[:, :1536]))
    put("bv", col_units_n(dq[:, 1536:]))
    put("bo", row_units(a["dil_w_o"][0]))
    for l, c in enumerate("ab"):
        for h in range(2):
            hs = slice(h * HALF_HIDDEN, (h + 1) * HALF_HIDDEN)
            put(f"{c}in{h}", col_units(a["mlp_w_in"][l][:, hs]))
            put(f"{c}out{h}", row_units(a["mlp_w_out"][l][hs]))
    for l in range(2):
        w = a["w_in_2"][l]
        put(f"pa{l}", col_units(w[:, 0:D]))
        put(f"pb{l}", col_units(w[:, D:2 * D]))
        put(f"pqk{l}", col_units(w[:, 2 * D:4 * D]))
        put(f"pv{l}", col_units_n(w[:, 4 * D:6 * D]))
        put(f"prg{l}", col_units(w[:, 6 * D:8 * D]))
        put(f"pgc{l}", col_units(w[:, 8 * D:9 * D]))
        put(f"pgr{l}", col_units(w[:, 9 * D:10 * D]))
        put(f"co{l}", col_units(a["w_conv_o_2"][l]))
        put(f"ro{l}", row_units(a["w_ret_o_2"][l]))
        put(f"wo{l}", col_units(a["w_out_2"][l]))

    def gated(g, u, units=col_units):
        return np.stack([units(g), units(u)], axis=1).reshape(-1, P, UNIT)

    put("gu0", gated(a["ffn_w_gate_2"][0], a["ffn_w_up_2"][0]))
    put("dn0", row_units(a["ffn_w_down_2"][0]))
    for e in range(EXPERTS):
        put("gu1", gated(a["moe_w_gate_2"][0, e], a["moe_w_up_2"][0, e], col_units_n), 33 * e)
        put("dn1", row_units(a["moe_w_down_2"][0, e]), 33 * e)
    ws[TOTAL:] = ws[:LOOKAHEAD]

    par = np.zeros((P, NPAR), np.float32)

    def pcol(name, v):
        par[:, PCOL[name]:PCOL[name] + v.shape[1]] = v

    for i, (g, b) in enumerate([("ln_mix", 0), ("ln_mlp", 0), ("ln_mix", 1), ("ln_mlp", 1)]):
        pcol(f"lnA{i}g", feat(a[f"{g}_g"][b]))
        pcol(f"lnA{i}b", feat(a[f"{g}_b"][b]))
    for l in range(2):
        for k, nm in (("c", "ln_conv"), ("1", "ln1"), ("2", "ln2")):
            pcol(f"ln{k}_{l}g", feat(a[f"{nm}_g_2"][l]))
            pcol(f"ln{k}_{l}b", feat(a[f"{nm}_b_2"][l]))
        pcol(f"bdw_{l}", feat(a["b_dw_2"][l]))
        pcol(f"bada_{l}", feat(a["b_ada_2"][l]))
        pcol(f"wdw_{l}", a["w_dw_2"][l].reshape(TAPS, KT, P).transpose(2, 1, 0).reshape(P, KT * TAPS))
    pcol("c", feat(a["c_2"][0]))
    pcol("invf", invf[:, None])
    pcol("iota", np.tile(np.arange(P, dtype=np.float32), (P, 1)))
    pcol("eps", np.full((P, 1), EPS, np.float32))
    pcol("wr", a["moe_w_router_2"][0].reshape(KT, P, EXPERTS).transpose(1, 0, 2).reshape(P, KT * EXPERTS))

    arrays = {
        "wstream": ws,
        "xT": np.ascontiguousarray(a["x"][0].reshape(S, KT, P).transpose(2, 1, 0)),
        "par": par,
        "posb": np.ascontiguousarray(np.broadcast_to(a["positions_2"].astype(np.int32).reshape(1, S), (P, S))),
        "consts": cs, "blocka": block_a, "decay": decay,
    }
    nc = _bacc.Bacc("TRN2", target_bir_lowering=False, num_devices=1)
    args = [nc.dram_tensor(n, v.shape, mybir.dt.from_np(v.dtype), kind="ExternalInput").ap() for n, v in arrays.items()]
    out = nc.dram_tensor("outT", (P, KT, S), F32, kind="ExternalOutput").ap()
    build(nc, *args, out)
    r = _run(nc, [arrays], core_ids=[0])
    got = r.results[0]["outT"]
    return np.ascontiguousarray(got.transpose(2, 1, 0).reshape(1, S, D))
```
